# Optimizing a Trainium2 kernel written in Bass

```python
import jax, jax.numpy as jnp
from jax import lax
import numpy as np

D_MODEL = 1024
BATCH = 1
SEQ = 256
DEPTH = 2

MLA_HEADS = 8
MLA_NOPE = 64
MLA_ROPE = 32
MLA_V = 64
Q_LORA = 384
KV_LORA = 256
DSA_HEADS = 8
DSA_HEAD_DIM = 64
IDX_HEADS = 8
IDX_DIM = 32
TOPK_MAX = 256
D_FF = 2816
N_EXPERTS = 8
TOP_K = 2
D_FF_EXPERT = 3584
ROPE_THETA = 10000.0
Q_BLOCK = 128
NORM_EPS = 1e-5
MAX_POS_OFFSET = 1024
ALPHA = (2 * DEPTH) ** 0.25
BETA = (8 * DEPTH) ** -0.25
N_DENSE = (DEPTH + 1) // 2
N_MOE = DEPTH // 2

IN_SIZES = (
    Q_LORA,
    KV_LORA,
    MLA_ROPE,
    DSA_HEADS * DSA_HEAD_DIM,
    DSA_HEADS * DSA_HEAD_DIM,
    DSA_HEADS * DSA_HEAD_DIM,
    IDX_HEADS * IDX_DIM,
    IDX_DIM,
    IDX_HEADS,
    2 * D_MODEL,
)
D_IN = sum(IN_SIZES)

kernel_name = "hybrid_mla_dsa_deepnorm_moe"

def layer_norm(x, g, b):
    xf = x.astype(jnp.float32)
    mu = jnp.mean(xf, axis=-1, keepdims=True)
    var = jnp.mean(jnp.square(xf - mu), axis=-1, keepdims=True)
    return ((xf - mu) * lax.rsqrt(var + NORM_EPS) * g.astype(jnp.float32) + b.astype(jnp.float32)).astype(x.dtype)

def rms_norm(x, g):
    xf = x.astype(jnp.float32)
    ms = jnp.mean(jnp.square(xf), axis=-1, keepdims=True)
    return (xf * lax.rsqrt(ms + NORM_EPS) * g.astype(jnp.float32)).astype(x.dtype)

def rope(x, pos):
    d = x.shape[-1]
    inv = jnp.power(ROPE_THETA, -jnp.arange(0, d, 2, dtype=jnp.float32) / d)
    ang = pos.astype(jnp.float32)[:, :, None, None] * inv
    c, s = jnp.cos(ang), jnp.sin(ang)
    xf = x.astype(jnp.float32)
    x1, x2 = xf[..., : d // 2], xf[..., d // 2:]
    return jnp.concatenate([x1 * c - x2 * s, x1 * s + x2 * c], axis=-1).astype(x.dtype)

def to_blocks(a):
    B, S = a.shape[:2]
    return jnp.moveaxis(a.reshape((B, S // Q_BLOCK, Q_BLOCK) + a.shape[2:]), 1, 0)

def from_blocks(a):
    nb, B, Q = a.shape[:3]
    return jnp.moveaxis(a, 0, 1).reshape((B, nb * Q) + a.shape[3:])

def split_cols(a):
    idx = np.cumsum(IN_SIZES)[:-1].tolist()
    return jnp.split(a, idx, axis=-1)

def dense_causal_attention(q, k, v):
    S = q.shape[1]
    scale = q.shape[-1] ** -0.5
    key_pos = jnp.arange(S)

    def block(args):
        qb, start = args
        q_pos = start + jnp.arange(Q_BLOCK)
        logits = jnp.einsum('bqhd,bkhd->bhqk', qb, k).astype(jnp.float32) * scale
        logits = jnp.where(key_pos[None, :] <= q_pos[:, None], logits, -jnp.inf)
        p = jax.nn.softmax(logits, axis=-1).astype(v.dtype)
        return jnp.einsum('bhqk,bkhd->bqhd', p, v)

    starts = jnp.arange(0, S, Q_BLOCK)
    return from_blocks(lax.map(block, (to_blocks(q), starts)))

def mla_branch(c_q, c_kv, k_r, pos, g_q, w_uq, g_kv, w_ukv):
    B, S, _ = c_q.shape
    q = (rms_norm(c_q, g_q) @ w_uq).reshape(B, S, MLA_HEADS, MLA_NOPE + MLA_ROPE)
    q = jnp.concatenate([q[..., :MLA_NOPE], rope(q[..., MLA_NOPE:], pos)], axis=-1)
    kv = (rms_norm(c_kv, g_kv) @ w_ukv).reshape(B, S, MLA_HEADS, MLA_NOPE + MLA_V)
    k_nope, v = kv[..., :MLA_NOPE], kv[..., MLA_NOPE:]
    k_rope = rope(k_r[:, :, None, :], pos)
    k = jnp.concatenate([k_nope, jnp.broadcast_to(k_rope, (B, S, MLA_HEADS, MLA_ROPE))], axis=-1)
    o = dense_causal_attention(q, k, v)
    return o.reshape(B, S, MLA_HEADS * MLA_V)

def dsa_branch(q, k, v, q_i, k_i, w_i, pos):
    B, S, _ = q.shape
    n_sel = min(TOPK_MAX, S // 4)
    scale = DSA_HEAD_DIM ** -0.5
    q = rope(q.reshape(B, S, DSA_HEADS, DSA_HEAD_DIM), pos)
    k = rope(k.reshape(B, S, DSA_HEADS, DSA_HEAD_DIM), pos)
    v = v.reshape(B, S, DSA_HEADS, DSA_HEAD_DIM)
    q_i = rope(q_i.reshape(B, S, IDX_HEADS, IDX_DIM), pos)
    k_i = rope(k_i[:, :, None, :], pos)[:, :, 0, :]
    w_i = w_i * ((IDX_HEADS * IDX_DIM) ** -0.5)
    key_pos = jnp.arange(S)
    gather = jax.vmap(lambda a, ix: a[ix])

    def block(args):
        qb, qib, wib, start = args
        q_pos = start + jnp.arange(Q_BLOCK)
        dots = jnp.einsum('bqhd,bsd->bqhs', qib, k_i).astype(jnp.float32)
        score = jnp.einsum('bqh,bqhs->bqs', wib.astype(jnp.float32), jax.nn.relu(dots))
        score = jnp.where(key_pos[None, :] <= q_pos[:, None], score, -jnp.inf)
        _, idx = lax.top_k(score, n_sel)
        valid = idx <= q_pos[None, :, None]
        k_sel = gather(k, idx)
        v_sel = gather(v, idx)
        logits = jnp.einsum('bqhd,bqnhd->bqhn', qb, k_sel).astype(jnp.float32) * scale
        logits = jnp.where(valid[:, :, None, :], logits, -jnp.inf)
        p = jax.nn.softmax(logits, axis=-1).astype(v.dtype)
        return jnp.einsum('bqhn,bqnhd->bqhd', p, v_sel)

    starts = jnp.arange(0, S, Q_BLOCK)
    o = from_blocks(lax.map(block, (to_blocks(q), to_blocks(q_i), to_blocks(w_i), starts)))
    return o.reshape(B, S, DSA_HEADS * DSA_HEAD_DIM)

def mixer_sublayer(x, pos, w_in, g_q, w_uq, g_kv, w_ukv, w_o_mla, w_o_dsa, w_out):
    c_q, c_kv, k_r, dq, dk, dv, iq, ik, iw, gates = split_cols(x @ w_in)
    y_a = mla_branch(c_q, c_kv, k_r, pos, g_q, w_uq, g_kv, w_ukv) @ w_o_mla
    y_b = dsa_branch(dq, dk, dv, iq, ik, iw, pos) @ w_o_dsa
    g = jax.nn.sigmoid(gates.astype(jnp.float32)).astype(x.dtype)
    merged = g[..., :D_MODEL] * y_a + g[..., D_MODEL:] * y_b
    return merged @ w_out

def swiglu(x, w1, w3, w2):
    return (jax.nn.silu(x @ w1) * (x @ w3)) @ w2

def moe_ffn(x, w_router, w1, w3, w2):
    B, S, D = x.shape
    t = x.reshape(B * S, D)
    logits = (t @ w_router).astype(jnp.float32)
    top_val, top_idx = lax.top_k(logits, TOP_K)
    top_w = jax.nn.softmax(top_val, axis=-1)
    comb = jnp.sum(jax.nn.one_hot(top_idx, N_EXPERTS, dtype=jnp.float32) * top_w[..., None], axis=1)
    comb = comb.astype(t.dtype)
    y = jnp.zeros_like(t)
    for e in range(N_EXPERTS):
        y = y + comb[:, e:e + 1] * swiglu(t, w1[e], w3[e], w2[e])
    return y.reshape(B, S, D)

def setup_inputs(seed: int = 0) -> dict:
    key = jax.random.key(seed)
    ks = jax.random.split(key, 24)

    def nrm(k, shape, fan_in, s=1.0):
        return jax.random.normal(k, shape, jnp.float32) * (s * fan_in ** -0.5)

    def gain(k, shape):
        return 1.0 + 0.01 * jax.random.normal(k, shape, jnp.float32)

    x = jax.random.normal(ks[0], (BATCH, SEQ, D_MODEL), jnp.float32)
    offset = jax.random.randint(ks[1], (BATCH, 1), 0, MAX_POS_OFFSET, dtype=jnp.int32)
    positions = offset + jnp.arange(SEQ, dtype=jnp.int32)[None, :]
    return {
        "x": x,
        "positions": positions,
        "w_in": nrm(ks[2], (DEPTH, D_MODEL, D_IN), D_MODEL),
        "mla_q_norm": gain(ks[3], (DEPTH, Q_LORA)),
        "w_uq": nrm(ks[4], (DEPTH, Q_LORA, MLA_HEADS * (MLA_NOPE + MLA_ROPE)), Q_LORA),
        "mla_kv_norm": gain(ks[5], (DEPTH, KV_LORA)),
        "w_ukv": nrm(ks[6], (DEPTH, KV_LORA, MLA_HEADS * (MLA_NOPE + MLA_V)), KV_LORA),
        "w_o_mla": nrm(ks[7], (DEPTH, MLA_HEADS * MLA_V, D_MODEL), MLA_HEADS * MLA_V, BETA),
        "w_o_dsa": nrm(ks[8], (DEPTH, DSA_HEADS * DSA_HEAD_DIM, D_MODEL), DSA_HEADS * DSA_HEAD_DIM, BETA),
        "w_out": nrm(ks[9], (DEPTH, D_MODEL, D_MODEL), D_MODEL, BETA),
        "ln1_g": gain(ks[10], (DEPTH, D_MODEL)),
        "ln1_b": 0.01 * jax.random.normal(ks[11], (DEPTH, D_MODEL), jnp.float32),
        "ln2_g": gain(ks[12], (DEPTH, D_MODEL)),
        "ln2_b": 0.01 * jax.random.normal(ks[13], (DEPTH, D_MODEL), jnp.float32),
        "dense_w1": nrm(ks[14], (N_DENSE, D_MODEL, D_FF), D_MODEL),
        "dense_w3": nrm(ks[15], (N_DENSE, D_MODEL, D_FF), D_MODEL),
        "dense_w2": nrm(ks[16], (N_DENSE, D_FF, D_MODEL), D_FF, BETA),
        "moe_router": nrm(ks[17], (N_MOE, D_MODEL, N_EXPERTS), D_MODEL),
        "moe_w1": nrm(ks[18], (N_MOE, N_EXPERTS, D_MODEL, D_FF_EXPERT), D_MODEL),
        "moe_w3": nrm(ks[19], (N_MOE, N_EXPERTS, D_MODEL, D_FF_EXPERT), D_MODEL),
        "moe_w2": nrm(ks[20], (N_MOE, N_EXPERTS, D_FF_EXPERT, D_MODEL), D_FF_EXPERT, BETA),
    }

def reference(x, positions, w_in, mla_q_norm, w_uq, mla_kv_norm, w_ukv, w_o_mla, w_o_dsa, w_out,
              ln1_g, ln1_b, ln2_g, ln2_b, dense_w1, dense_w3, dense_w2,
              moe_router, moe_w1, moe_w3, moe_w2):
    for l in range(DEPTH):
        h = mixer_sublayer(x, positions, w_in[l], mla_q_norm[l], w_uq[l], mla_kv_norm[l], w_ukv[l],
                           w_o_mla[l], w_o_dsa[l], w_out[l])
        x = layer_norm(ALPHA * x + h, ln1_g[l], ln1_b[l])
        if l % 2 == 0:
            f = swiglu(x, dense_w1[l // 2], dense_w3[l // 2], dense_w2[l // 2])
        else:
            f = moe_ffn(x, moe_router[l // 2], moe_w1[l // 2], moe_w3[l // 2], moe_w2[l // 2])
        x = layer_norm(ALPHA * x + f, ln2_g[l], ln2_b[l])
    return x


_drawn_inputs = setup_inputs


def setup_inputs(seed=0):
    import zlib

    import numpy as np

    out = dict(_drawn_inputs(seed))
    spreads = {}
    factors = {'mla_q_norm': 8.0, 'mla_kv_norm': 8.0, 'ln1_g': 2.971, 'ln2_g': 2.952, 'ln2_b': 3.467}
    for name, (base, spread) in spreads.items():
        noise = np.random.default_rng([zlib.crc32(name.encode()), seed]).standard_normal(out[name].shape)
        drawn = base * np.exp(spread * noise) if base else spread * noise
        out[name] = __import__('jax').numpy.asarray(drawn.astype(out[name].dtype))
    for name, factor in factors.items():
        out[name] = (out[name] * factor).astype(out[name].dtype)
    return out
```

```python
from contextlib import ExitStack

import concourse.bass as bass
from concourse import mybir

ALU = mybir.AluOpType
ACT = mybir.ActivationFunctionType
F32 = mybir.dt.float32
I32 = mybir.dt.int32
AX_X = mybir.AxisListType.X

P = 128
D = 1024
SEQ = 256
T = SEQ // P
DEPTH = 2
KD = D // P
HEADS = 8
NOPE, ROPE, VDIM = 64, 32, 64
QK = NOPE + ROPE
Q_LORA, KV_LORA = 384, 256
DH = 64
IDX_HEADS, IDX_DIM = 8, 32
N_SEL = min(256, SEQ // 4)
D_FF = 2816
EXPERTS = 8
D_FFE = 3584
EPS = 1e-5
ALPHA = (2 * DEPTH) ** 0.25
THETA = 10000.0

C_Q = 0
C_KV = C_Q + Q_LORA
C_KR = C_KV + KV_LORA
C_DQ = C_KR + ROPE
C_DK = C_DQ + HEADS * DH
C_DV = C_DK + HEADS * DH
C_IQ = C_DV + HEADS * DH
C_IK = C_IQ + IDX_HEADS * IDX_DIM
C_IW = C_IK + IDX_DIM
C_GA = C_IW + IDX_HEADS
C_GB = C_GA + D
D_IN = C_GB + D

W = 512
CHUNKS = [(c, min(W, D_IN - c)) for c in range(0, D_IN, W)]
NCH = len(CHUNKS)
DENSE = [(c, min(W, D_FF - c)) for c in range(0, D_FF, W)]
NG = D_FFE // W
CAP = P
MASKED = -1e30
TAKEN = -3e38
FLOOR = -3.2e38
CREDIT = 1
UNUSED = 3e38
ROUND = 1.5 * 2 ** 23
TWO_PI = 6.283185307179586
HALF_PI = TWO_PI / 4
PI_F = 3.1415925
RQ = ROPE // 2
RD = DH // 2
NF = RQ + RD

RING = 7
SLOT = KD * W


def mixer_slots(l):
    return [("in", l, c) for c in range(NCH)] + [("uq", l), ("ukv", l), ("oa", l), ("ob", l), ("out", l, 0), ("out", l, 1)]


STREAM = mixer_slots(0) + [(w, g) for g in range(len(DENSE)) for w in ("w1", "w3", "w2")] + mixer_slots(1)
FIRST_MOE = len(STREAM)
PER_JOB = 3 * NG
assert PER_JOB % RING == 0


def split_2pi():
    import numpy as np

    def short(v):
        return float((np.float32(v).view(np.uint32) & np.uint32(0xFFFFC000)).view(np.float32))

    hi = short(TWO_PI)
    mid = short(TWO_PI - hi)
    return hi, mid, TWO_PI - hi - mid


def build(nc, a, out):
    ctx = ExitStack()
    with ctx:
        def sb(name, shape, dt=F32):
            return ctx.enter_context(nc.sbuf_tensor(name, shape, dt))

        def sem(name):
            return ctx.enter_context(nc.semaphore(name))

        ring = sb("ring", [P, RING, SLOT])
        x = sb("x", [P, T, D])
        xT = sb("xT", [P, KD, SEQ])
        proj = sb("proj", [P, T, D_IN])
        att = sb("att", [P, 2688])
        km = sb("km", [P, T, HEADS * QK])
        vm = sb("vm", [P, T, HEADS * VDIM])
        qTm_ = sb("qTm", [P, HEADS, SEQ])
        kTm_ = sb("kTm", [P, HEADS, SEQ])
        dT = sb("dT", [P, 2, 4, SEQ])
        causal = sb("causal", [P, T, SEQ])
        select = sb("select", [P, T, SEQ])
        score = sb("score", [P, T, SEQ])
        ident = sb("ident", [P, P])
        ones = sb("ones", [P, P])
        before = sb("before", [P, P])
        trig = sb("trig", [P, T, 2 * NF])
        turns = sb("turns", [P, T, 2 * NF])
        invf = sb("invf", [P, NF])
        posi = sb("posi", [P, T], I32)
        posf = sb("posf", [P, T])
        rope32 = sb("rope32", [P, T, 2, ROPE])
        rope64 = sb("rope64", [P, T, 2, DH])
        gcol = sb("gcol", [P, DEPTH, 5])
        small = sb("small", [P, 256])
        wr = sb("wr", [P, KD, EXPERTS])
        jobs = sb("jobs", [1, 32], I32)

        qm = xT[:, 0:6, :].rearrange("p a b -> p (a b)").rearrange("p (t n) -> p t n", t=T)
        cT = att[:, 0:5 * SEQ].rearrange("p (k s) -> p k s", k=5)
        ropeA = att[:, 1280:1792]
        ropeB = att[:, 1792:2304]
        NSM, NPT = 4, 3
        sm = att[:, 0:NSM * 384].rearrange("p (n s) -> p n s", n=NSM)
        pT = att[:, NSM * 384:NSM * 384 + NPT * 384].rearrange("p (n s) -> p n s", n=NPT)
        qTm, kTm = qTm_[0:QK], kTm_[0:QK]
        oT = qTm_[:, :, :].rearrange("p a s -> p (a s)").rearrange("p (m k s) -> p m k s", m=2, k=4)
        relu = kTm_[:, 0:6, :].rearrange("p a s -> p (a s)").rearrange("p (n s) -> p n s", n=4)
        lnp = kTm_[:, :, :].rearrange("p a s -> p (a s)").rearrange("p (w n) -> p w n", w=2)
        iT = dT[:, 0, 0:3, :]
        qTd, kTd = dT[:, 0], dT[:, 1]
        o_tok = [[proj[:, t, C_DQ + m * W:C_DQ + (m + 1) * W] for t in range(T)] for m in range(2)]

        ffn = proj[:, :, :].rearrange("p t n -> p (t n)")
        used = [0]

        def scratch(n):
            used[0] += n
            assert used[0] <= T * D_IN
            return ffn[:, used[0] - n:used[0]]

        silu = scratch(T * W).rearrange("p (t n) -> p t n", t=T)
        hid = scratch(T * W).rearrange("p (t n) -> p t n", t=T)
        hT = scratch(4 * SEQ).rearrange("p (c s) -> p c s", c=4)
        xeT = scratch(KD * CAP).rearrange("p (k s) -> p k s", k=KD)
        oe = scratch(D)
        y = scratch(T * D).rearrange("p (t n) -> p t n", t=T)
        pick = scratch(T * CAP).rearrange("p (t s) -> p t s", t=T)
        comb_at = scratch(T * CAP).rearrange("p (t s) -> p t s", t=T)
        combT = scratch(SEQ)
        slot_no = scratch(2 * CAP)

        rt = small[:, 0:160].rearrange("p (t n) -> p t n", t=T)
        r_list, r_top, r_keys = rt[:, :, 0:16], rt[:, :, 16:24], rt[:, :, 24:32]
        r_sel, r_exp, r_comb, r_pos, r_cnt = (rt[:, :, 32 + 8 * i:40 + 8 * i] for i in range(5))
        r_one = rt[:, :, 72:76]
        cur = small[:, 160:164]
        iws = small[:, 168:184].rearrange("p (t n) -> p t n", t=T)
        expo = small[:, 184:185]

        stat = sb("stat", [P, T, 2, 6])
        mv = sb("mv", [P, T, 2])
        rstd = sb("rstd", [P, T, 2])
        rms = sb("rms", [P, T, 4])
        top8 = sb("top8", [P, T, 8])
        mx = sb("mx", [P, 16, T])
        den = sb("den", [P, 16, T])
        rden = sb("rden", [P, T, HEADS])
        junk = sb("junk", [P, Q_LORA])
        flags = sb("flags", [1, 64])

        bank = [ctx.enter_context(nc.psum_tensor(f"bank{i}", [P, W], F32)) for i in range(8)]

        landed = [sem(f"landed{i}") for i in range(RING)]
        x_in, small_in, lnp_in, out_done = sem("x_in"), sem("small_in"), sem("lnp_in"), sem("out_done")
        consts = sem("consts_ready")
        sin_in, trig_done, tables = sem("sin_in_ready"), sem("trig_done"), sem("rope_tables_ready")
        proj_mm, proj_ev = sem("proj_mm"), sem("proj_evacuated")
        idx_roped, dsa_roped, kr_roped, qm_roped = (sem(n) for n in ("idx_roped", "dsa_roped", "kr_roped", "qm_roped"))
        idx_tr, idx_ev, dots_mm, relu_ev, scored, selected = (
            sem(n) for n in ("idx_turned", "idx_evacuated", "dots_mm", "relu_ready", "head_scored", "keys_selected"))
        sq_done, ms_ready, rms_ready, lat_norm, c_tr, c_ev = (
            sem(n) for n in ("squares_summed", "mean_square_ready", "rms_ready", "latents_normed", "latents_turned", "latents_evacuated"))
        uq_mm, uq_ev, ukv_mm, ukv_ev, kr_put = (sem(n) for n in ("uq_mm", "uq_evacuated", "ukv_mm", "ukv_evacuated", "key_rope_placed"))
        dsa_tr, dsa_ev, mq_tr, mq_ev, mk_tr, mk_ev = (
            sem(n) for n in ("dsa_turned", "dsa_evacuated", "mla_q_turned", "mla_q_evacuated", "mla_k_turned", "mla_k_evacuated"))
        qk_mm, row_max, probs, p_tr, p_ev, pv_mm, o_ev = (
            sem(n) for n in ("qk_mm", "row_max_ready", "probs_ready", "probs_turned", "probs_evacuated", "pv_mm", "heads_normed"))
        o_tr, oT_ev, y_mm, merged, m_tr, m_ev, out_mm = (
            sem(n) for n in ("heads_turned", "heads_evacuated", "branches_mm", "merged", "merged_turned", "merged_evacuated", "out_mm"))
        ln_var, ln_rstd, ln_done, x_tr, x_ev = (sem(n) for n in ("ln_variance", "ln_rstd", "ln_done", "x_turned", "x_evacuated"))
        w1_mm, w3_mm, silu_ev, hid_ev, h_tr, h_ev, w2_mm = (
            sem(n) for n in ("w1_mm", "w3_mm", "silu_ready", "hidden_ready", "hidden_turned", "hidden_evacuated", "w2_mm"))
        route_mm, chosen, exp_done, pos_mm, routed = (
            sem(n) for n in ("router_mm", "experts_chosen", "router_exp_done", "positions_mm", "routed"))
        slot_ids, cur_put, pick_put, comb_put = (sem(n) for n in ("slot_ids_ready", "expert_column_ready", "pick_ready", "combine_ready"))
        gat_mm, gat_ev, comb_tr, comb_ev, oe_ev, sc_mm, y_add = (
            sem(n) for n in ("gather_mm", "gather_evacuated", "combine_turned", "combine_evacuated", "expert_out_ready", "scatter_mm", "y_added"))
        pool_passed = sem("pool_passed_wait")
        dve_step, act_step, pool_step = sem("dve_step"), sem("act_step"), sem("pool_step")

        def arrived(eng, item):
            i = STREAM.index(item)
            eng.wait_ge(landed[i % RING], 16 * (i // RING + 1))

        def slot(item):
            return ring[:, STREAM.index(item) % RING, :]

        def last_reader(item):
            kind = item[0]
            if kind == "in":
                return proj_mm, item[1] * T * NCH + T * (item[2] + 1)
            if kind == "uq":
                return uq_mm, 4 * (item[1] + 1)
            if kind == "ukv":
                return ukv_mm, 4 * (item[1] + 1)
            if kind in ("oa", "ob"):
                return y_mm, 4 * (item[1] + 1)
            if kind == "out":
                return out_mm, 4 * item[1] + T * (item[2] + 1)
            return (w2_mm, item[1] + 1) if kind == "w2" else ({"w1": w1_mm, "w3": w3_mm}[kind], T * (item[1] + 1))

        def moe_slot(m):
            return ring[:, (FIRST_MOE + m) % RING, :]

        def moe_arrived(eng, j, m):
            i = FIRST_MOE + m
            eng.wait_ge(landed[i % RING], j * (16 * PER_JOB // RING) + 16 * (i // RING + 1))

        DG = len(DENSE)

        def weights_by_chunk(w, c, n):
            return w.rearrange("(k p) n -> p k n", p=P)[:, :, c:c + n]

        def source(item):
            kind = item[0]
            if kind == "in":
                c, n = CHUNKS[item[2]]
                return weights_by_chunk(a["w_in"][item[1]], c, n), KD, n
            if kind == "out":
                return weights_by_chunk(a["w_out"][item[1]], item[2] * W, W), KD, W
            if kind in ("uq", "ukv", "oa", "ob"):
                w = a[{"uq": "w_uq", "ukv": "w_ukv", "oa": "w_o_mla", "ob": "w_o_dsa"}[kind]][item[1]]
                return w.rearrange("(k p) n -> p k n", p=P), w.shape[0] // P, w.shape[1]
            c, n = DENSE[item[1]]
            if kind == "w2":
                return a["dense_w2"][0][c:c + n, :].rearrange("(k p) n -> p k n", p=P), n // P, D
            return weights_by_chunk(a["dense_" + kind][0], c, n), KD, n

        def as_weights(view, k, n):
            return view[:, 0:k * n].rearrange("p (k n) -> p k n", k=k)

        block = ctx.enter_context(nc.Block())

        def crowded_experts(eng, body):
            many = eng.value_load(jobs[0:1, 2 * EXPERTS:2 * EXPERTS + 1], min_val=0, max_val=4)
            with eng.If(many > 0):
                with eng.Fori(0, EXPERTS) as e:
                    crowded = eng.value_load(jobs[0:1, bass.ds(e, 1)], min_val=0, max_val=1)
                    with eng.If(crowded > 0):
                        rank = eng.value_load(jobs[0:1, bass.ds(e + EXPERTS, 1)], min_val=0, max_val=4)
                        body(rank + EXPERTS, e)


        @block.sync
        def _(sp):
            sp.dma_start(x[:, :, :], a["x"][0].rearrange("(t p) d -> p t d", p=P)).then_inc(x_in, 16)
            for i, item in enumerate(STREAM):
                if i >= RING:
                    sp.wait_ge(*last_reader(STREAM[i - RING]))
                src, k, n = source(item)
                sp.dma_start(as_weights(slot(item), k, n), src).then_inc(landed[i % RING], 16)

            def expert_load(e, m):
                g, w = m // 3, m % 3
                if w == 2:
                    src = a["moe_w2"][0][e].rearrange("(g k p) n -> g p k n", p=P, k=4)[g]
                    dst = as_weights(moe_slot(m), 4, D)
                else:
                    src = weights_by_chunk(a[("moe_w1", "moe_w3")[w]][0][e], g * W, W)
                    dst = as_weights(moe_slot(m), KD, W)
                return dst, src

            def expert_stream(j, e):
                for m in range(PER_JOB):
                    back = m - RING
                    if back < 0:
                        sp.wait_ge(*last_reader(STREAM[FIRST_MOE + back]))
                        back += PER_JOB
                        base = -NG
                    else:
                        base = 0
                    reader, dense = ((w1_mm, T * DG), (w3_mm, T * DG), (w2_mm, DG))[back % 3]
                    sp.wait_ge(reader, NG * j + (dense + base + back // 3 + 1))
                    dst, src = expert_load(e, m)
                    sp.dma_start(dst, src).then_inc(landed[(FIRST_MOE + m) % RING], 16)

            with sp.Fori(0, EXPERTS) as e:
                expert_stream(e, e)

            sp.wait_ge(routed, 1)
            crowded_experts(sp, expert_stream)
            sp.wait_ge(ln_done, 2 * DEPTH)
            sp.dma_start(out[0].rearrange("(t p) d -> p t d", p=P), x[:, :, :]).then_inc(out_done, 16)
            sp.wait_ge(out_done, 16)


        def pool_experts(pool):
            pool.wait_ge(merged, 4 * DEPTH)
            pool.wait_ge(x_ev, 4 * (2 * DEPTH))
            pool.iota(slot_no, pattern=[[1, 2 * CAP]], base=0, channel_multiplier=0,
                      allow_small_or_imprecise_dtypes=True).then_inc(slot_ids, 1)
            pool.wait_ge(slot_ids, 1)
            pool.wait_ge(routed, 1)

            def one_hots(j, e, half):
                ids = slot_no[:, half * CAP:(half + 1) * CAP]
                pool.wait_ge(comb_put, j + CREDIT)
                pool.tensor_copy(cur[:, 0:2], r_pos[:, :, bass.ds(e, 1)].rearrange("p t n -> p (t n)"))
                pool.tensor_copy(cur[:, 2:4], r_comb[:, :, bass.ds(e, 1)].rearrange("p t n -> p (t n)")).then_inc(cur_put, 1)
                pool.wait_ge(cur_put, j + 1)
                pool.wait_ge(gat_mm, 2 * j + CREDIT)
                pool.sem_inc(pool_passed, 1)
                for t in range(T):
                    ins = pool.tensor_scalar(pick[:, t, :], ids, cur[:, t:t + 1], None, ALU.is_equal)
                ins.then_inc(pick_put, 1)
                pool.wait_ge(pick_put, j + 1)
                pool.wait_ge(comb_tr, j + CREDIT)
                for t in range(T):
                    ins = pool.tensor_tensor(comb_at[:, t, :], pick[:, t, :], cur[:, 2 + t:3 + t].to_broadcast([P, CAP]), ALU.mult)
                ins.then_inc(comb_put, 1)

            pool.sem_inc(comb_put, CREDIT)
            with pool.Fori(0, EXPERTS) as e:
                one_hots(e, e, 0)
            crowded_experts(pool, lambda j, e: one_hots(j, e, 1))

        @block.gpsimd
        def _(pool):
            n = [0]

            def step(ins):
                n[0] += 1
                ins.then_inc(pool_step, 1)
                pool.wait_ge(pool_step, n[0])

            step(pool.memset(ident[:, :], 0.0))
            step(pool.memset(ones[:, :], 1.0))
            step(pool.memset(causal[:, :, :], 0.0))
            step(pool.memset(expo, -0.5))
            step(pool.affine_select(out=ident[:, :], in_=ident[:, :], compare_op=ALU.not_equal, fill=1.0,
                                    base=0, pattern=[[-1, P]], channel_multiplier=1))
            step(pool.affine_select(out=before[:, :], in_=ones[:, :], compare_op=ALU.is_gt, fill=0.0,
                                    base=0, pattern=[[1, P]], channel_multiplier=-1))
            for t in range(T):
                step(pool.affine_select(out=causal[:, t, :], in_=causal[:, t, :], compare_op=ALU.is_ge, fill=MASKED,
                                        base=t * P, pattern=[[-1, SEQ]], channel_multiplier=1))
            pool.memset(r_list[:, :, EXPERTS:16], UNUSED).then_inc(consts, 1)

            for l in range(DEPTH):
                for t in range(T):
                    k = T * l + t + 1
                    pool.wait_ge(ms_ready, k)
                    pool.tensor_tensor(rms[:, t, 2:4], rms[:, t, 0:2], expo.to_broadcast([P, 2]), ALU.pow).then_inc(rms_ready, 1)
                for s in range(2):
                    if l == 1 and s == 1:
                        pool_experts(pool)
                    for t in range(T):
                        k = T * (2 * l + s) + t + 1
                        pool.wait_ge(ln_var, k)
                        pool.tensor_tensor(rstd[:, t, 1:2], rstd[:, t, 0:1], expo, ALU.pow).then_inc(ln_rstd, 1)


        def load_ln(act, l, s):
            g, b = (("ln1_g", "ln1_b"), ("ln2_g", "ln2_b"))[s]
            if s == 0:
                act.wait_ge(qk_mm, 16 * (l + 1))
            else:
                act.wait_ge(ln_done, 2 * l + 1)
            act.dma_start(lnp[:, 0, :], a[g][l:l + 1, :].partition_broadcast(P)).then_inc(lnp_in, 16)
            act.dma_start(lnp[:, 1, :], a[b][l:l + 1, :].partition_broadcast(P)).then_inc(lnp_in, 16)

        def act_dense(act):
            def turned(g):
                c0, n = DENSE[g]
                for t in range(T):
                    act.wait_ge(h_tr, T * g + t + 1)
                    act.copy(hT[:, 0:n // P, t * P:(t + 1) * P],
                             bank[2 * t][:, 0:n].rearrange("p (k s) -> p k s", s=P)).then_inc(h_ev, 1)

            for g, (c0, n) in enumerate(DENSE):
                for t in range(T):
                    k = T * g + t
                    act.wait_ge(w1_mm, k + 1)
                    if g:
                        act.wait_ge(hid_ev, k - 1)
                    act.activation(silu[:, t, 0:n], bank[2 * t][:, 0:n], ACT.Silu).then_inc(silu_ev, 1)
                turned(g)

        def act_experts(act):
            act.wait_ge(chosen, 1)
            act.activation(r_exp, r_exp, ACT.Exp).then_inc(exp_done, 1)

            def job(j):
                for h in range(2):
                    act.wait_ge(gat_mm, 2 * j + (h + 1 + CREDIT))
                    act.copy(xeT[:, 4 * h:4 * h + 4, :], bank[6 + h][:, :].rearrange("p (k s) -> p k s", k=4)).then_inc(gat_ev, 1)

                def turned(g):
                    act.wait_ge(h_tr, T * DG + NG * j + g + 1)
                    act.copy(hT[:, :, 0:CAP], bank[6][:, :].rearrange("p (k s) -> p k s", k=4)).then_inc(h_ev, 1)

                for g in range(NG):
                    act.wait_ge(w1_mm, T * DG + NG * j + g + 1)
                    act.wait_ge(hid_ev, NG * j + (T * DG + max(g - 1, 0)))
                    if g:
                        turned(g - 1)
                    act.activation(silu[:, g % 2, :], bank[2 * (g % 2)][:, :], ACT.Silu).then_inc(silu_ev, 1)
                    if g == 3:
                        act.wait_ge(comb_tr, j + (1 + CREDIT))
                        act.wait_ge(sc_mm, 4 * j + CREDIT)
                        act.copy(combT, bank[7][:, 0:SEQ]).then_inc(comb_ev, 1)
                turned(NG - 1)
                act.wait_ge(w2_mm, DG + NG * j + NG)
                act.wait_ge(sc_mm, 4 * j + CREDIT)
                act.copy(oe[:, 0:W], bank[4][:, :])
                act.copy(oe[:, W:D], bank[5][:, :]).then_inc(oe_ev, 1)

            act.sem_inc(comb_ev, CREDIT)
            act.sem_inc(oe_ev, CREDIT)
            with act.Fori(0, EXPERTS) as e:
                job(e)
            crowded_experts(act, lambda j, e: job(j))

        @block.scalar
        def _(act):
            act.dma_start(posi[:, :], a["positions"].rearrange("o (t p) -> p (o t)", p=P), allow_slow_non_contiguous=True).then_inc(small_in, 16)
            act.dma_start(invf[:, :], a["inv_freq"].partition_broadcast(P)).then_inc(small_in, 16)
            for l in range(DEPTH):
                act.dma_start(gcol[:, l, 0:3], a["mla_q_norm"][l].rearrange("(k p) -> p k", p=P), allow_slow_non_contiguous=True).then_inc(small_in, 16)
                act.dma_start(gcol[:, l, 3:5], a["mla_kv_norm"][l].rearrange("(k p) -> p k", p=P), allow_slow_non_contiguous=True).then_inc(small_in, 16)
            act.dma_start(wr[:, :, :], a["moe_router"][0].rearrange("(k p) e -> p k e", p=P)).then_inc(small_in, 16)
            act.wait_ge(sin_in, 1)
            act.activation(trig[:, :, :], trig[:, :, :], ACT.Sin).then_inc(trig_done, 1)

            def turned_x(k):
                for t in range(T):
                    for h in range(2):
                        n = 2 * t + h
                        act.wait_ge(x_tr, 4 * k + n + 1)
                        act.copy(xT[:, 4 * h:4 * h + 4, t * P:(t + 1) * P],
                                 bank[n][:, :].rearrange("p (k s) -> p k s", k=4)).then_inc(x_ev, 1)

            turned_x(0)
            for l in range(DEPTH):
                def chunk(c):
                    c0, n = CHUNKS[c]
                    for t in range(T):
                        k = T * c + t
                        act.wait_ge(proj_mm, T * NCH * l + k + 1)
                        src, dst = bank[k % 4], proj[:, t, c0:c0 + n]
                        raw = max(0, min(n, C_GA - c0))
                        if raw == n:
                            act.copy(dst, src[:, 0:n]).then_inc(proj_ev, 1)
                        elif raw == 0:
                            act.activation(dst, src[:, 0:n], ACT.Sigmoid).then_inc(proj_ev, 1)
                        else:
                            act.copy(dst[:, 0:raw], src[:, 0:raw])
                            act.activation(dst[:, raw:n], src[:, raw:n], ACT.Sigmoid).then_inc(proj_ev, 1)

                for c in range(5):
                    chunk(c)
                    if c == 1:
                        for t in range(T):
                            if l or t:
                                act.wait_ge(sq_done, T * l + t)
                            act.wait_ge(proj_ev, T * NCH * l + 4)
                            if l:
                                act.wait_ge(rms_ready, T * (l - 1) + t + 1)
                            act.activation(junk[:, 0:Q_LORA], proj[:, t, C_Q:C_KV], ACT.Square, accum_out=rms[:, t, 0:1]).then_inc(act_step, 1)
                            act.wait_ge(act_step, T * l + t + 1)
                            act.activation(junk[:, 0:KV_LORA], proj[:, t, C_KV:C_KR], ACT.Square, accum_out=rms[:, t, 1:2]).then_inc(sq_done, 1)
                chunk(5)
                for t in range(T):
                    act.wait_ge(idx_tr, T * l + t + 1)
                    act.copy(iT[:, :, t * P:(t + 1) * P],
                             bank[4 + t][:, 0:3 * P].rearrange("p (k s) -> p k s", k=3)).then_inc(idx_ev, 1)
                chunk(6)
                for h in range(IDX_HEADS):
                    k = IDX_HEADS * l + h
                    act.wait_ge(dots_mm, k + 1)
                    if h >= 4:
                        act.wait_ge(scored, k - 3)
                    act.activation(relu[:, h % 4, :], bank[4 + h % 4][:, 0:384], ACT.Relu,
                                   scale=float(IDX_HEADS * IDX_DIM) ** -0.5).then_inc(relu_ev, 1)
                for t in range(T):
                    act.wait_ge(c_tr, T * l + t + 1)
                    act.wait_ge(small_in, 7 * 16)
                    for k in range(5):
                        b = bank[4 + 2 * t + k // 4]
                        ins = act.activation(cT[:, k, t * P:(t + 1) * P], b[:, (k % 4) * P:(k % 4 + 1) * P], ACT.Copy,
                                             scale=gcol[:, l, k:k + 1])
                    ins.then_inc(c_ev, 1)
                chunk(7)
                chunk(8)
                for t in range(T):
                    for h in range(2):
                        act.wait_ge(uq_mm, 4 * l + 2 * t + h + 1)
                        act.copy(qm[:, t, h * 384:(h + 1) * 384], bank[4 + 2 * t + h][:, 0:384]).then_inc(uq_ev, 1)
                for i in range(2):
                    for t in range(T):
                        act.wait_ge(dsa_tr, 4 * l + 2 * i + t + 1)
                        act.copy(dT[:, i, :, t * P:(t + 1) * P],
                                 bank[2 * i + t][:, :].rearrange("p (k s) -> p k s", k=4)).then_inc(dsa_ev, 1)
                for t in range(T):
                    for h in range(2):
                        act.wait_ge(mq_tr, 4 * l + 2 * t + h + 1)
                        act.copy(qTm[:, 4 * h:4 * h + 4, t * P:(t + 1) * P],
                                 bank[4 + 2 * t + h][0:QK, :].rearrange("p (k s) -> p k s", k=4)).then_inc(mq_ev, 1)

                def exps(u):
                    k = 16 * l + u
                    scale = float(QK if u < 8 else DH) ** -0.5
                    act.wait_ge(row_max, k + 1)
                    act.activation(sm[:, u % NSM, 0:P], sm[:, u % NSM, 0:P], ACT.Exp, bias=mx[:, u, 0:1], scale=scale,
                                   accum_out=den[:, u, 0:1])
                    act.activation(sm[:, u % NSM, P:384], sm[:, u % NSM, P:384], ACT.Exp, bias=mx[:, u, 1:2], scale=scale,
                                   accum_out=den[:, u, 1:2]).then_inc(probs, 1)

                def turned_probs(u):
                    k = 16 * l + u
                    act.wait_ge(p_tr, k + 1)
                    if u >= NPT:
                        act.wait_ge(pv_mm, k - NPT + 1)
                    act.copy(pT[:, u % NPT, :], bank[2 + u % 2][:, 0:384]).then_inc(p_ev, 1)

                for i in range(16 + 1):
                    if i < 16:
                        exps(i)
                    if i >= 1:
                        turned_probs(i - 1)
                for m in range(2):
                    for t in range(T):
                        act.wait_ge(o_tr, 4 * l + 2 * m + t + 1)
                        act.copy(oT[:, m, :, t * P:(t + 1) * P],
                                 bank[2 * m + t][:, :].rearrange("p (k s) -> p k s", k=4)).then_inc(oT_ev, 1)
                for t in range(T):
                    for h in range(2):
                        act.wait_ge(m_tr, 4 * l + 2 * t + h + 1)
                        act.copy(xT[:, 4 * h:4 * h + 4, t * P:(t + 1) * P],
                                 bank[2 * t + h][:, :].rearrange("p (k s) -> p k s", k=4)).then_inc(m_ev, 1)
                load_ln(act, l, 0)
                turned_x(2 * l + 1)
                load_ln(act, l, 1)
                if l == 0:
                    act_dense(act)
                    turned_x(2)
                else:
                    act_experts(act)


        def dve_dense(dve, step):
            for g, (c0, n) in enumerate(DENSE):
                for t in range(T):
                    k = T * g + t + 1
                    dve.wait_ge(silu_ev, k)
                    dve.wait_ge(w3_mm, k)
                    if g:
                        dve.wait_ge(h_tr, k - T)
                    dve.tensor_tensor(hid[:, t, 0:n], silu[:, t, 0:n], bank[1 + 2 * t][:, 0:n], ALU.mult).then_inc(hid_ev, 1)
            dve.wait_ge(w2_mm, DG)
            for t in range(T):
                for h in range(2):
                    step(dve.scalar_tensor_tensor(out=x[:, t, h * W:(h + 1) * W], in0=x[:, t, h * W:(h + 1) * W], scalar=ALPHA,
                                                  in1=bank[4 + 2 * t + h][:, :], op0=ALU.mult, op1=ALU.add))

        def dve_experts(dve, step):
            for t in range(T):
                lg = bank[6 + t]
                dve.wait_ge(route_mm, t + 1)
                step(dve.tensor_copy(r_list[:, t, 0:EXPERTS], lg[:, 0:EXPERTS]))
                step(dve.max(r_top[:, t, :], r_list[:, t, 0:EXPERTS]))
                dve.tensor_copy(r_keys[:, t, 0:2], r_top[:, t, 0:2])
                step(dve.memset(r_keys[:, t, 2:8], UNUSED))
                step(dve.match_replace(out=r_list[:, t, :], in_to_replace=r_keys[:, t, :], in_values=r_list[:, t, :],
                                       imm_value=TAKEN))
                step(dve.tensor_scalar(r_sel[:, t, :], r_list[:, t, 0:EXPERTS], TAKEN * 0.5, None, ALU.is_lt))
                step(dve.tensor_scalar(r_one[:, t, 0:1], r_top[:, t, 0:1], -1.0, None, ALU.mult))
                step(dve.tensor_scalar(r_exp[:, t, :], lg[:, 0:EXPERTS], r_one[:, t, 0:1], None, ALU.add))
            dve.memset(flags[:, :], 0.0).then_inc(chosen, 1)
            dve.wait_ge(chosen, 1)
            dve.wait_ge(exp_done, 1)
            for t in range(T):
                step(dve.tensor_tensor(r_exp[:, t, :], r_exp[:, t, :], r_sel[:, t, :], ALU.mult))
                step(dve.reduce_sum(r_one[:, t, 1:2], r_exp[:, t, :], AX_X))
                step(dve.reciprocal(r_one[:, t, 2:3], r_one[:, t, 1:2]))
                step(dve.tensor_scalar(r_comb[:, t, :], r_exp[:, t, :], r_one[:, t, 2:3], None, ALU.mult))
            dve.wait_ge(pos_mm, 1)
            for t in range(T):
                step(dve.tensor_scalar(r_pos[:, t, :], bank[6][:, t * EXPERTS:(t + 1) * EXPERTS], 1.0, None, ALU.add))
                step(dve.tensor_tensor(r_pos[:, t, :], r_pos[:, t, :], r_sel[:, t, :], ALU.mult))
                step(dve.tensor_scalar(r_pos[:, t, :], r_pos[:, t, :], -1.0, None, ALU.add))
            E = EXPERTS
            over, s1, s2, s4 = (flags[0:1, i * 16:(i + 1) * 16] for i in range(4))
            step(dve.tensor_scalar(over[:, E:2 * E], bank[6][0:1, 2 * E:3 * E], float(CAP), None, ALU.is_gt))
            for src, dst, by in ((over, s1, 1), (s1, s2, 2), (s2, s4, 4)):
                step(dve.tensor_tensor(dst[:, E:2 * E], src[:, E:2 * E], src[:, E - by:2 * E - by], ALU.add))
            step(dve.tensor_copy(jobs[0:1, 0:E], over[:, E:2 * E]))
            step(dve.tensor_tensor(jobs[0:1, E:2 * E], s4[:, E:2 * E], over[:, E:2 * E], ALU.subtract))
            dve.tensor_copy(jobs[0:1, 2 * E:2 * E + 1], s4[:, 2 * E - 1:2 * E]).then_inc(routed, 1)
            for t in range(T):
                step(dve.tensor_scalar(y[:, t, :], x[:, t, :], ALPHA, None, ALU.mult))

            def job(j):
                for g in range(NG):
                    k = NG * j + (T * DG + g + 1)
                    dve.wait_ge(silu_ev, k)
                    dve.wait_ge(w3_mm, k)
                    dve.wait_ge(h_tr, k - (2 if g else 1))
                    dve.tensor_tensor(hid[:, g % 2, :], silu[:, g % 2, :], bank[1 + 2 * (g % 2)][:, :], ALU.mult).then_inc(hid_ev, 1)
                dve.wait_ge(y_add, 4 * j + CREDIT)
                for t in range(T):
                    for h in range(2):
                        q = 2 * t + h
                        dve.wait_ge(sc_mm, 4 * j + (q + 1 + CREDIT))
                        dve.tensor_tensor(y[:, t, h * W:(h + 1) * W], y[:, t, h * W:(h + 1) * W], bank[q][:, :], ALU.add).then_inc(y_add, 1)

            dve.sem_inc(y_add, CREDIT)
            with dve.Fori(0, EXPERTS) as e:
                job(e)
            crowded_experts(dve, lambda j, e: job(j))
            extra = dve.value_load(jobs[0:1, 2 * EXPERTS:2 * EXPERTS + 1], min_val=0, max_val=4)
            dve.wait_ge(y_add, 4 * extra + (4 * EXPERTS + CREDIT))

        @block.vector
        def _(dve):
            n = [0]

            def step(ins):
                n[0] += 1
                ins.then_inc(dve_step, 1)
                dve.wait_ge(dve_step, n[0])

            dve.wait_ge(small_in, 7 * 16)
            step(dve.tensor_copy(posf[:, :], posi[:, :]))
            hi, mid, lo = split_2pi()
            for t in range(T):
                for h in range(2):
                    ins = dve.tensor_scalar(trig[:, t, h * NF:(h + 1) * NF], invf[:, :], posf[:, t:t + 1], None, ALU.mult)
            step(ins)
            for h in range(2):
                cols = slice(h * NF, (h + 1) * NF)
                step(dve.tensor_scalar(turns[:, :, cols], trig[:, :, cols], 1.0 / TWO_PI, 0.25 * h, ALU.mult, ALU.add))
            step(dve.tensor_scalar(turns[:, :, :], turns[:, :, :], ROUND, None, ALU.add))
            step(dve.tensor_scalar(turns[:, :, :], turns[:, :, :], ROUND, None, ALU.subtract))
            for part in (hi, mid, lo):
                step(dve.scalar_tensor_tensor(out=trig[:, :, :], in0=turns[:, :, :], scalar=-part, in1=trig[:, :, :],
                                              op0=ALU.mult, op1=ALU.add))
            step(dve.tensor_scalar(trig[:, :, NF:2 * NF], trig[:, :, NF:2 * NF], HALF_PI, None, ALU.add))
            dve.tensor_scalar(trig[:, :, :], trig[:, :, :], PI_F, -PI_F, ALU.min, ALU.max).then_inc(sin_in, 1)
            dve.wait_ge(trig_done, 1)
            for tab, f0, nf in ((rope32, 0, RQ), (rope64, RQ, RD)):
                s_, c_ = trig[:, :, f0:f0 + nf], trig[:, :, NF + f0:NF + f0 + nf]
                dve.tensor_copy(tab[:, :, 0, 0:nf], c_)
                dve.tensor_copy(tab[:, :, 0, nf:2 * nf], c_)
                dve.tensor_scalar(tab[:, :, 1, 0:nf], s_, -1.0, None, ALU.mult)
                step(dve.tensor_copy(tab[:, :, 1, nf:2 * nf], s_))

            def rope(v, t, heads, d, tab, done=None):
                h2 = d // 2
                c_ = tab[:, t, 0:1, :].to_broadcast([P, heads, d])
                A = ropeA[:, 0:heads * d].rearrange("p (h d) -> p h d", h=heads)
                B = ropeB[:, 0:heads * d].rearrange("p (h d) -> p h d", h=heads)
                dve.tensor_tensor(A, v, c_, ALU.mult)
                dve.tensor_tensor(B[:, :, 0:h2], v[:, :, h2:d], tab[:, t, 1:2, 0:h2].to_broadcast([P, heads, h2]), ALU.mult)
                step(dve.tensor_tensor(B[:, :, h2:d], v[:, :, 0:h2], tab[:, t, 1:2, h2:d].to_broadcast([P, heads, h2]), ALU.mult))
                ins = dve.tensor_tensor(v, A, B, ALU.add)
                if done is None:
                    step(ins)
                else:
                    ins.then_inc(done[0], 1)
                    dve.wait_ge(done[0], done[1])

            def heads_of(v, heads):
                return v.rearrange("p (h d) -> p h d", h=heads)

            def layer_norm(k, src, l, s):
                for t in range(T):
                    for h in range(2):
                        ins = dve.bn_stats(stat[:, t, h, :], src[:, t, h * W:(h + 1) * W])
                    step(ins)
                    step(dve.bn_aggr(mv[:, t, :], stat[:, t, :, :].rearrange("p a b -> p (a b)")))
                    dve.tensor_scalar(rstd[:, t, 0:1], mv[:, t, 1:2], EPS, None, ALU.add).then_inc(ln_var, 1)
                for t in range(T):
                    dve.wait_ge(ln_rstd, T * k + t + 1)
                    step(dve.tensor_scalar(x[:, t, :], src[:, t, :], mv[:, t, 0:1], rstd[:, t, 1:2], ALU.subtract, ALU.mult))
                    dve.wait_ge(lnp_in, 32 * (k + 1))
                    step(dve.tensor_tensor(x[:, t, :], x[:, t, :], lnp[:, 0, :], ALU.mult))
                    ins = dve.tensor_tensor(x[:, t, :], x[:, t, :], lnp[:, 1, :], ALU.add)
                    if t == T - 1:
                        ins.then_inc(ln_done, 1)
                        dve.wait_ge(ln_done, k + 1)
                    else:
                        step(ins)

            dve.wait_ge(consts, 1)
            for l in range(DEPTH):
                base = T * NCH * l
                for t in range(T):
                    dve.wait_ge(sq_done, T * l + t + 1)
                    step(dve.tensor_scalar(rms[:, t, 0:1], rms[:, t, 0:1], 1.0 / Q_LORA, EPS, ALU.mult, ALU.add))
                    dve.tensor_scalar(rms[:, t, 1:2], rms[:, t, 1:2], 1.0 / KV_LORA, EPS, ALU.mult, ALU.add).then_inc(ms_ready, 1)
                for t in range(T):
                    dve.wait_ge(rms_ready, T * l + t + 1)
                    dve.tensor_scalar(proj[:, t, C_Q:C_KV], proj[:, t, C_Q:C_KV], rms[:, t, 2:3], None, ALU.mult)
                    dve.tensor_scalar(proj[:, t, C_KV:C_KR], proj[:, t, C_KV:C_KR], rms[:, t, 3:4], None, ALU.mult).then_inc(lat_norm, 1)
                dve.wait_ge(proj_ev, base + 10)
                for t in range(T):
                    rope(heads_of(proj[:, t, C_IQ:C_IK], IDX_HEADS), t, IDX_HEADS, IDX_DIM, rope32)
                    rope(heads_of(proj[:, t, C_IK:C_IW], 1), t, 1, IDX_DIM, rope32)
                    ik4 = score[:, t, 0:P].rearrange("p (r d) -> p r d", r=4)
                    dve.tensor_copy(ik4, proj[:, t:t + 1, C_IK:C_IW].to_broadcast([P, 4, IDX_DIM])).then_inc(idx_roped, 1)
                for t in range(T):
                    rope(heads_of(proj[:, t, C_KR:C_DQ], 1), t, 1, ROPE, rope32, (kr_roped, T * l + t + 1))
                for t in range(T):
                    rope(heads_of(proj[:, t, C_DQ:C_DK], HEADS), t, HEADS, DH, rope64)
                    rope(heads_of(proj[:, t, C_DK:C_DV], HEADS), t, HEADS, DH, rope64, (dsa_roped, T * l + t + 1))
                dve.wait_ge(idx_tr, T * (l + 1))
                for h in range(IDX_HEADS):
                    dve.wait_ge(relu_ev, IDX_HEADS * l + h + 1)
                    for t in range(T):
                        keys = (t + 1) * P
                        part = relu[:, h % 4, t * P:t * P + keys]
                        prev = causal[:, t, 0:keys] if h == 0 else score[:, t, 0:keys]
                        ins = dve.scalar_tensor_tensor(out=score[:, t, 0:keys], in0=part, scalar=proj[:, t, C_IW + h:C_IW + h + 1],
                                                       in1=prev, op0=ALU.mult, op1=ALU.add)
                    ins.then_inc(scored, 1)
                    dve.wait_ge(scored, IDX_HEADS * l + h + 1)
                for r in range(N_SEL // 8):
                    for t in range(T):
                        ins = dve.max(top8[:, t, :], score[:, t, 0:(t + 1) * P])
                    step(ins)
                    for t in range(T):
                        keys = (t + 1) * P
                        ins = dve.match_replace(out=score[:, t, 0:keys], in_to_replace=top8[:, t, :],
                                                in_values=score[:, t, 0:keys], imm_value=TAKEN)
                    step(ins)
                for t in range(T):
                    keys = (t + 1) * P
                    step(dve.tensor_scalar(select[:, t, 0:keys], score[:, t, 0:keys], TAKEN * 0.5, MASKED, ALU.is_gt, ALU.mult))
                    ins = dve.tensor_tensor(select[:, t, 0:keys], select[:, t, 0:keys], causal[:, t, 0:keys], ALU.add)
                    step(ins)
                for t in range(T):
                    for h in range(2):
                        dve.wait_ge(ukv_mm, 4 * l + 2 * t + h + 1)
                        src = bank[2 * t + h][:, :].rearrange("p (h d) -> p h d", h=4)
                        dve.tensor_copy(heads_of(km[:, t, :], HEADS)[:, 4 * h:4 * h + 4, 0:NOPE], src[:, :, 0:NOPE])
                        dve.tensor_copy(heads_of(vm[:, t, :], HEADS)[:, 4 * h:4 * h + 4, :], src[:, :, NOPE:P]).then_inc(ukv_ev, 1)
                    dve.tensor_copy(heads_of(km[:, t, :], HEADS)[:, :, NOPE:QK],
                                    proj[:, t:t + 1, C_KR:C_DQ].to_broadcast([P, HEADS, ROPE])).then_inc(kr_put, 1)
                dve.wait_ge(uq_ev, 4 * (l + 1))
                for t in range(T):
                    rope(heads_of(qm[:, t, :], HEADS)[:, :, NOPE:QK], t, HEADS, ROPE, rope32, (qm_roped, T * l + t + 1))
                for t in range(T):
                    for h in range(2):
                        dve.wait_ge(mk_tr, 4 * l + 2 * t + h + 1)
                        dve.tensor_copy(kTm[:, 4 * h:4 * h + 4, t * P:(t + 1) * P],
                                        bank[2 * t + h][0:QK, :].rearrange("p (k s) -> p k s", k=4)).then_inc(mk_ev, 1)

                def maxima(u):
                    k = 16 * l + u
                    mask = causal if u < 8 else select
                    scale = float(QK if u < 8 else DH) ** -0.5
                    dve.wait_ge(qk_mm, k + 1)
                    if u >= NSM:
                        dve.wait_ge(p_tr, k - NSM + 1)
                    for t in range(T):
                        lo_, keys = t * P, (t + 1) * P
                        ins = dve.tensor_tensor_reduce(sm[:, u % NSM, lo_:lo_ + keys], bank[u % 2][:, lo_:lo_ + keys],
                                                       mask[:, t, 0:keys], 1.0, FLOOR, ALU.add, ALU.max, mx[:, u, t:t + 1])
                    step(ins)
                    dve.tensor_scalar(mx[:, u, :], mx[:, u, :], -scale, None, ALU.mult).then_inc(row_max, 1)

                def norm_heads(m):
                    dve.wait_ge(pv_mm, 16 * l + 8 * (m + 1))
                    for t in range(T):
                        step(dve.reciprocal(rden[:, t, :], den[:, 8 * m:8 * m + 8, t]))
                        dve.tensor_tensor(heads_of(o_tok[m][t], HEADS), heads_of(bank[4 + 2 * m + t][:, :], HEADS),
                                          rden[:, t, :].unsqueeze(2).to_broadcast([P, HEADS, VDIM]), ALU.mult).then_inc(o_ev, 1)

                for u in range(16):
                    maxima(u)
                    if u == 12:
                        norm_heads(0)
                norm_heads(1)
                for t in range(T):
                    for h in range(2):
                        k = 2 * t + h
                        ga, gb = proj[:, t, C_GA + h * W:C_GA + (h + 1) * W], proj[:, t, C_GB + h * W:C_GB + (h + 1) * W]
                        dve.wait_ge(y_mm, 4 * l + k + 1)
                        dve.tensor_tensor(ga, ga, bank[4 + 2 * (k % 2)][:, :], ALU.mult)
                        step(dve.tensor_tensor(gb, gb, bank[5 + 2 * (k % 2)][:, :], ALU.mult))
                        dve.tensor_tensor(ga, ga, gb, ALU.add).then_inc(merged, 1)
                for h in range(2):
                    for t in range(T):
                        dve.wait_ge(out_mm, 4 * l + 2 * h + t + 1)
                        step(dve.scalar_tensor_tensor(out=x[:, t, h * W:(h + 1) * W], in0=x[:, t, h * W:(h + 1) * W], scalar=ALPHA,
                                                      in1=bank[4 + 2 * h + t][:, :], op0=ALU.mult, op1=ALU.add))
                layer_norm(2 * l, x, l, 0)
                if l == 0:
                    dve_dense(dve, step)
                    layer_norm(1, x, 0, 1)
                else:
                    dve_experts(dve, step)
                    layer_norm(3, y, 1, 1)


        def pe_mixer(pe, l, tp, turn_x):
            base = T * NCH * l

            def chunk(c):
                c0, n = CHUNKS[c]
                w = as_weights(slot(("in", l, c)), KD, n)
                arrived(pe, ("in", l, c))
                for t in range(T):
                    k = T * c + t
                    if k >= 4:
                        pe.wait_ge(proj_ev, base + k - 3)
                    for i in range(KD):
                        ins = pe.matmul(bank[k % 4][:, 0:n], xT[:, i, t * P:(t + 1) * P], w[:, i, :],
                                        start=(i == 0), stop=(i == KD - 1))
                    ins.then_inc(proj_mm, 1)

            for c in range(6):
                chunk(c)
            for t in range(T):
                pe.wait_ge(idx_roped, T * l + t + 1)
                for i in range(2):
                    tp(bank[4 + t][:, i * P:(i + 1) * P], proj[:, t, C_IQ + i * P:C_IQ + (i + 1) * P])
                tp(bank[4 + t][:, 2 * P:3 * P], score[:, t, 0:P]).then_inc(idx_tr, 1)
            chunk(6)
            pe.wait_ge(idx_ev, T * (l + 1))
            for h in range(IDX_HEADS):
                r = IDX_DIM * (h % 4)
                rows = slice(r, r + IDX_DIM)
                if h >= 4:
                    pe.wait_ge(relu_ev, IDX_HEADS * l + h - 3)
                for t in range(T):
                    keys = (t + 1) * P
                    ins = pe.matmul(bank[4 + h % 4][:, t * P:t * P + keys], iT[rows, h // 4, t * P:(t + 1) * P],
                                    iT[rows, 2, 0:keys], start=True, stop=True)
                ins.then_inc(dots_mm, 1)
            pe.wait_ge(relu_ev, IDX_HEADS * (l + 1))
            for t in range(T):
                pe.wait_ge(lat_norm, T * l + t + 1)
                for k in range(5):
                    ins = tp(bank[4 + 2 * t + k // 4][:, (k % 4) * P:(k % 4 + 1) * P], proj[:, t, k * P:(k + 1) * P])
                ins.then_inc(c_tr, 1)
            chunk(7)
            chunk(8)
            pe.wait_ge(c_ev, T * (l + 1))
            arrived(pe, ("uq", l))
            wq = as_weights(slot(("uq", l)), 3, HEADS * QK)
            for t in range(T):
                for h in range(2):
                    for i in range(3):
                        ins = pe.matmul(bank[4 + 2 * t + h][:, 0:384], cT[:, i, t * P:(t + 1) * P], wq[:, i, h * 384:(h + 1) * 384],
                                        start=(i == 0), stop=(i == 2))
                    ins.then_inc(uq_mm, 1)
            pe.wait_ge(proj_ev, base + T * NCH)
            arrived(pe, ("ukv", l))
            wkv = as_weights(slot(("ukv", l)), 2, HEADS * P)
            for t in range(T):
                for h in range(2):
                    for i in range(2):
                        ins = pe.matmul(bank[2 * t + h][:, :], cT[:, 3 + i, t * P:(t + 1) * P], wkv[:, i, h * W:(h + 1) * W],
                                        start=(i == 0), stop=(i == 1))
                    ins.then_inc(ukv_mm, 1)
            pe.wait_ge(dsa_roped, T * (l + 1))
            pe.wait_ge(ukv_ev, 4 * (l + 1))
            for i, c0 in enumerate((C_DQ, C_DK)):
                for t in range(T):
                    for k in range(4):
                        ins = tp(bank[2 * i + t][:, k * P:(k + 1) * P], proj[:, t, c0 + k * P:c0 + (k + 1) * P])
                    ins.then_inc(dsa_tr, 1)
            for t in range(T):
                pe.wait_ge(qm_roped, T * l + t + 1)
                for h in range(2):
                    for k in range(4):
                        ins = tp(bank[4 + 2 * t + h][0:QK, k * P:(k + 1) * P], qm[:, t, (4 * h + k) * QK:(4 * h + k + 1) * QK])
                    ins.then_inc(mq_tr, 1)
            pe.wait_ge(dsa_ev, 4 * (l + 1))
            for t in range(T):
                pe.wait_ge(kr_put, T * l + t + 1)
                for h in range(2):
                    for k in range(4):
                        ins = tp(bank[2 * t + h][0:QK, k * P:(k + 1) * P], km[:, t, (4 * h + k) * QK:(4 * h + k + 1) * QK])
                    ins.then_inc(mk_tr, 1)
            pe.wait_ge(mq_ev, 4 * (l + 1))
            pe.wait_ge(mk_ev, 4 * (l + 1))

            def qk(u):
                h = u % 8
                if u >= 2:
                    pe.wait_ge(row_max, 16 * l + u - 1)
                for t in range(T):
                    keys = (t + 1) * P
                    if u < 8:
                        q, kk = qTm[:, h, t * P:(t + 1) * P], kTm[:, h, 0:keys]
                    else:
                        rows = slice(DH * (h % 2), DH * (h % 2) + DH)
                        q, kk = qTd[rows, h // 2, t * P:(t + 1) * P], kTd[rows, h // 2, 0:keys]
                    ins = pe.matmul(bank[u % 2][:, t * P:t * P + keys], q, kk, start=True, stop=True)
                ins.then_inc(qk_mm, 1)

            def turn_probs(u):
                pe.wait_ge(probs, 16 * l + u + 1)
                if u >= 2:
                    pe.wait_ge(p_ev, 16 * l + u - 1)
                for i in range(3):
                    ins = tp(bank[2 + u % 2][:, i * P:(i + 1) * P], sm[:, u % NSM, i * P:(i + 1) * P])
                ins.then_inc(p_tr, 1)

            def pv(u):
                h, m = u % 8, u // 8
                pe.wait_ge(p_ev, 16 * l + u + 1)

                def v(t):
                    if m == 0:
                        return vm[:, t, h * VDIM:(h + 1) * VDIM]
                    return proj[:, t, C_DV + h * DH:C_DV + (h + 1) * DH]

                cols = slice(h * VDIM, (h + 1) * VDIM)
                pe.matmul(bank[4 + 2 * m][:, cols], pT[:, u % NPT, 0:P], v(0), start=True, stop=True)
                pe.matmul(bank[5 + 2 * m][:, cols], pT[:, u % NPT, P:2 * P], v(0), start=True, stop=False)
                pe.matmul(bank[5 + 2 * m][:, cols], pT[:, u % NPT, 2 * P:3 * P], v(1), start=False, stop=True).then_inc(pv_mm, 1)

            for i in range(16 + 3):
                if i < 16:
                    qk(i)
                if 2 <= i < 18:
                    turn_probs(i - 2)
                if i >= 3:
                    pv(i - 3)
            pe.wait_ge(row_max, 16 * (l + 1))
            for m in range(2):
                for t in range(T):
                    pe.wait_ge(o_ev, 4 * l + 2 * m + t + 1)
                    for k in range(4):
                        ins = tp(bank[2 * m + t][:, k * P:(k + 1) * P], o_tok[m][t][:, k * P:(k + 1) * P])
                    ins.then_inc(o_tr, 1)
            pe.wait_ge(oT_ev, 4 * (l + 1))
            arrived(pe, ("oa", l))
            arrived(pe, ("ob", l))
            wo = [as_weights(slot((w, l)), 4, D) for w in ("oa", "ob")]
            for t in range(T):
                for h in range(2):
                    k = 2 * t + h
                    if k >= 2:
                        pe.wait_ge(merged, 4 * l + k - 1)
                    for m in range(2):
                        for i in range(4):
                            ins = pe.matmul(bank[4 + m + 2 * (k % 2)][:, :], oT[:, m, i, t * P:(t + 1) * P],
                                            wo[m][:, i, h * W:(h + 1) * W], start=(i == 0), stop=(i == 3))
                    ins.then_inc(y_mm, 1)
            pe.wait_ge(merged, 4 * (l + 1))
            turn_x(m_tr, lambda t, i: proj[:, t, C_GA + i * P:C_GA + (i + 1) * P])
            pe.wait_ge(m_ev, 4 * (l + 1))
            for h in range(2):
                arrived(pe, ("out", l, h))
                w = as_weights(slot(("out", l, h)), KD, W)
                for t in range(T):
                    for i in range(KD):
                        ins = pe.matmul(bank[4 + 2 * h + t][:, :], xT[:, i, t * P:(t + 1) * P], w[:, i, :],
                                        start=(i == 0), stop=(i == KD - 1))
                    ins.then_inc(out_mm, 1)

        def pe_dense(pe, tp):
            def up(g):
                c0, n = DENSE[g]
                arrived(pe, ("w1", g))
                arrived(pe, ("w3", g))
                for t in range(T):
                    if g:
                        pe.wait_ge(h_ev, T * (g - 1) + t + 1)
                    for b, w, done in ((2 * t, "w1", w1_mm), (2 * t + 1, "w3", w3_mm)):
                        wv = as_weights(slot((w, g)), KD, n)
                        for i in range(KD):
                            ins = pe.matmul(bank[b][:, 0:n], xT[:, i, t * P:(t + 1) * P], wv[:, i, :], start=(i == 0), stop=(i == KD - 1))
                        ins.then_inc(done, 1)

            def turn(g):
                c0, n = DENSE[g]
                for t in range(T):
                    pe.wait_ge(hid_ev, T * g + t + 1)
                    for i in range(n // P):
                        ins = tp(bank[2 * t][:, i * P:(i + 1) * P], hid[:, t, i * P:(i + 1) * P])
                    ins.then_inc(h_tr, 1)

            def down(g):
                c0, n = DENSE[g]
                arrived(pe, ("w2", g))
                pe.wait_ge(h_ev, T * (g + 1))
                wv = as_weights(slot(("w2", g)), n // P, D)
                for t in range(T):
                    for h in range(2):
                        for i in range(n // P):
                            ins = pe.matmul(bank[4 + 2 * t + h][:, :], hT[:, i, t * P:(t + 1) * P], wv[:, i, h * W:(h + 1) * W],
                                            start=(g == 0 and i == 0), stop=(g == len(DENSE) - 1 and i == n // P - 1))
                ins.then_inc(w2_mm, 1)

            for g in range(len(DENSE)):
                up(g)
                if g:
                    down(g - 1)
                turn(g)
            down(len(DENSE) - 1)

        def pe_experts(pe, tp):
            pe.wait_ge(small_in, 7 * 16)
            for t in range(T):
                for i in range(KD):
                    ins = pe.matmul(bank[6 + t][:, 0:EXPERTS], xT[:, i, t * P:(t + 1) * P], wr[:, i, :], start=(i == 0), stop=(i == KD - 1))
                ins.then_inc(route_mm, 1)
            pe.wait_ge(chosen, 1)
            b = bank[6]
            pe.matmul(b[:, 0:EXPERTS], before[:, :], r_sel[:, 0, :], start=True, stop=True)
            pe.matmul(b[:, EXPERTS:2 * EXPERTS], ones[:, :], r_sel[:, 0, :], start=True, stop=False)
            pe.matmul(b[:, EXPERTS:2 * EXPERTS], before[:, :], r_sel[:, 1, :], start=False, stop=True)
            pe.matmul(b[:, 2 * EXPERTS:3 * EXPERTS], ones[:, :], r_sel[:, 0, :], start=True, stop=False)
            pe.matmul(b[:, 2 * EXPERTS:3 * EXPERTS], ones[:, :], r_sel[:, 1, :], start=False, stop=True).then_inc(pos_mm, 1)
            pe.wait_ge(routed, 1)

            def job(j):
                g0, d0 = T * DG, DG
                pe.wait_ge(pick_put, j + 1)
                pe.wait_ge(h_ev, g0 + NG * j)
                pe.wait_ge(comb_ev, j + CREDIT)
                for h in range(2):
                    for i in range(4):
                        for t in range(T):
                            ins = pe.matmul(bank[6 + h][:, i * P:(i + 1) * P], x[:, t, (4 * h + i) * P:(4 * h + i + 1) * P],
                                            pick[:, t, :], start=(t == 0), stop=(t == T - 1))
                    ins.then_inc(gat_mm, 1)
                pe.wait_ge(gat_ev, 2 * j + 2)

                def up(g, which):
                    bk = bank[2 * (g % 2) + which]
                    w = as_weights(moe_slot(3 * g + which), KD, W)
                    moe_arrived(pe, j, 3 * g + which)
                    if g < 2:
                        pe.wait_ge(y_add, 4 * j + CREDIT)
                    else:
                        pe.wait_ge(hid_ev, g0 + NG * j + g - 1)
                    for i in range(KD):
                        ins = pe.matmul(bk[:, :], xeT[:, i, :], w[:, i, :], start=(i == 0), stop=(i == KD - 1))
                    ins.then_inc((w1_mm, w3_mm)[which], 1)

                def turn(g):
                    pe.wait_ge(hid_ev, g0 + NG * j + g + 1)
                    pe.wait_ge(h_ev, g0 + NG * j + g)
                    for i in range(4):
                        ins = tp(bank[6][:, i * P:(i + 1) * P], hid[:, g % 2, i * P:(i + 1) * P])
                    ins.then_inc(h_tr, 1)

                def down(g):
                    pe.wait_ge(h_ev, g0 + NG * j + g + 1)
                    if g == 0:
                        pe.wait_ge(oe_ev, j + CREDIT)
                    moe_arrived(pe, j, 3 * g + 2)
                    w = as_weights(moe_slot(3 * g + 2), 4, D)
                    for h in range(2):
                        for i in range(4):
                            ins = pe.matmul(bank[4 + h][:, :], hT[:, i, 0:CAP], w[:, i, h * W:(h + 1) * W],
                                            start=(g == 0 and i == 0), stop=(g == NG - 1 and i == 3))
                    ins.then_inc(w2_mm, 1)

                for g in range(NG):
                    up(g, 0)
                    if g:
                        turn(g - 1)
                    up(g, 1)
                    if g:
                        down(g - 1)
                    if g == 2:
                        pe.wait_ge(comb_put, j + (1 + CREDIT))
                        for t in range(T):
                            ins = tp(bank[7][:, t * P:(t + 1) * P], comb_at[:, t, :])
                        ins.then_inc(comb_tr, 1)
                turn(NG - 1)
                down(NG - 1)
                pe.wait_ge(oe_ev, j + (1 + CREDIT))
                pe.wait_ge(comb_ev, j + (1 + CREDIT))
                for t in range(T):
                    for h in range(2):
                        pe.matmul(bank[2 * t + h][:, :], combT[:, t * P:(t + 1) * P], oe[:, h * W:(h + 1) * W],
                                  start=True, stop=True).then_inc(sc_mm, 1)

            for ready in (gat_mm, comb_tr, sc_mm):
                pe.sem_inc(ready, CREDIT)
            with pe.Fori(0, EXPERTS) as e:
                job(e)
            crowded_experts(pe, lambda j, e: job(j))

        @block.tensor
        def _(pe):
            def tp(dst, src):
                return pe.transpose(dst, src, ident[:, :])

            def turn_x(k, src):
                for t in range(T):
                    for h in range(2):
                        for i in range(4):
                            ins = tp(bank[2 * t + h][:, i * P:(i + 1) * P], src(t, 4 * h + i))
                        ins.then_inc(k, 1)

            def x_block(t, i):
                return x[:, t, i * P:(i + 1) * P]

            pe.wait_ge(consts, 1)
            pe.wait_ge(x_in, 16)
            turn_x(x_tr, x_block)
            pe.wait_ge(x_ev, 4)
            for l in range(DEPTH):
                pe_mixer(pe, l, tp, turn_x)
                pe.wait_ge(ln_done, 2 * l + 1)
                turn_x(x_tr, x_block)
                pe.wait_ge(x_ev, 4 * (2 * l + 2))
                if l == 0:
                    pe_dense(pe, tp)
                    pe.wait_ge(ln_done, 2)
                    turn_x(x_tr, x_block)
                    pe.wait_ge(x_ev, 12)
                else:
                    pe_experts(pe, tp)


_INS = ["x", "positions", "w_in", "mla_q_norm", "w_uq", "mla_kv_norm", "w_ukv", "w_o_mla", "w_o_dsa", "w_out",
        "ln1_g", "ln1_b", "ln2_g", "ln2_b", "dense_w1", "dense_w3", "dense_w2", "moe_router", "moe_w1", "moe_w3", "moe_w2"]


def kernel(**inputs):
    import numpy as np
    import concourse.bacc as bacc
    from concourse.bass_utils import run_bass_kernel_spmd

    nc = bacc.Bacc("TRN2", target_bir_lowering=False, num_devices=1, dynamic_dma_scratch_size=1024)
    arrays, a = {}, {}
    freq = [np.power(np.float32(THETA), -np.arange(0, d, 2, dtype=np.float32) / np.float32(d)) for d in (ROPE, DH)]
    given = {name: np.ascontiguousarray(inputs[name]) for name in _INS}
    given["inv_freq"] = np.concatenate(freq).astype(np.float32)[None, :]
    for name, v in given.items():
        arrays[name + "_dram"] = v
        a[name] = nc.dram_tensor(name + "_dram", v.shape, mybir.dt.from_np(v.dtype), kind="ExternalInput").ap()
    out = nc.dram_tensor("out_dram", (1, SEQ, D), F32, kind="ExternalOutput").ap()
    build(nc, a, out)
    r = run_bass_kernel_spmd(nc, [arrays], core_ids=[0])
    return r.results[0]["out_dram"]
```

```python
from contextlib import ExitStack

import concourse.bass as bass
from concourse import mybir

ALU = mybir.AluOpType
ACT = mybir.ActivationFunctionType
F32 = mybir.dt.float32
F32R = mybir.dt.float32r
I32 = mybir.dt.int32
AX_X = mybir.AxisListType.X

P = 128
D = 1024
SEQ = 256
T = SEQ // P
DEPTH = 2
KD = D // P
HEADS = 8
NOPE, ROPE, VDIM = 64, 32, 64
QK = NOPE + ROPE
Q_LORA, KV_LORA = 384, 256
DH = 64
IDX_HEADS, IDX_DIM = 8, 32
N_SEL = min(256, SEQ // 4)
D_FF = 2816
EXPERTS = 8
D_FFE = 3584
EPS = 1e-5
ALPHA = (2 * DEPTH) ** 0.25
THETA = 10000.0

C_Q = 0
C_KV = C_Q + Q_LORA
C_KR = C_KV + KV_LORA
C_DQ = C_KR + ROPE
C_DK = C_DQ + HEADS * DH
C_DV = C_DK + HEADS * DH
C_IQ = C_DV + HEADS * DH
C_IK = C_IQ + IDX_HEADS * IDX_DIM
C_IW = C_IK + IDX_DIM
C_GA = C_IW + IDX_HEADS
C_GB = C_GA + D
D_IN = C_GB + D

W = 512
CHUNKS = [(c, min(W, D_IN - c)) for c in range(0, D_IN, W)]
NCH = len(CHUNKS)
DENSE = [(c, min(W, D_FF - c)) for c in range(0, D_FF, W)]
NG = D_FFE // W
CAP = P
MASKED = -1e30
TAKEN = -3e38
FLOOR = -3.2e38
CREDIT = 1
UNUSED = 3e38
ROUND = 1.5 * 2 ** 23
TWO_PI = 6.283185307179586
HALF_PI = TWO_PI / 4
PI_F = 3.1415925
RQ = ROPE // 2
RD = DH // 2
NF = RQ + RD

UNIT = 4 * W
RAW = 7
SPLIT = 3
HEAD, REST = 0, 1
DG = len(DENSE)
PER_DENSE = 6 * DG


def ffn_units(groups):
    units = []
    for g in range(groups):
        units += [("w1", g, 0), ("w1", g, 1), ("w3", g, 0), ("w3", g, 1)]
        if g:
            units += [("w2", g - 1, 0), ("w2", g - 1, 1)]
    return units + [("w2", groups - 1, 0), ("w2", groups - 1, 1)]


def mixer_units(l):
    return ([("in", l, c, k) for c in range(NCH) for k in range(2)] + [("uq", l, 0), ("uq", l, 1), ("ukv", l)]
            + [(w, l, h) for h in range(2) for w in ("oa", "ob")] + [("out", l, h, k) for h in range(2) for k in range(2)])


MIXER = len(mixer_units(0))
LAYER = MIXER + PER_DENSE
STREAM = mixer_units(0) + ffn_units(DG) + mixer_units(1)
JOB = ffn_units(NG)
FIRST = len(STREAM)
PER_JOB = len(JOB)
HALVES = NCH + 2
assert PER_JOB % RAW == 0 and PER_JOB % SPLIT == 0 and len(ffn_units(DG)) == PER_DENSE


def split_2pi():
    import numpy as np

    def short(v):
        return float((np.float32(v).view(np.uint32) & np.uint32(0xFFFFC000)).view(np.float32))

    hi = short(TWO_PI)
    mid = short(TWO_PI - hi)
    return hi, mid, TWO_PI - hi - mid


def build(nc, a, out):
    ctx = ExitStack()
    with ctx:
        def sb(name, shape, dt=F32):
            return ctx.enter_context(nc.sbuf_tensor(name, shape, dt))

        def sem(name):
            return ctx.enter_context(nc.semaphore(name))

        where = [(nc.sbuf_base + 63) // 64 * 64]

        def region(size):
            where[0] += size
            return where[0] - size

        def put(name, shape, at, dt=F32):
            return nc.alloc_sbuf_tensor_at(name, shape, dt, offset=at)

        def fixed(name, shape, dt=F32):
            size = 4
            for n in shape[1:]:
                size *= n
            return put(name, shape, region((size + 31) // 32 * 32), dt)

        raw = fixed("raw", [P, RAW, UNIT])
        split = fixed("split", [P, SPLIT, 2, UNIT], F32R)
        x = fixed("x", [P, T, D])
        r_xT = region(2 * KD * SEQ * 4)
        xT = put("xT", [P, 2, KD, SEQ], r_xT, F32R)
        qm = put("qm", [P, T, HEADS * QK], r_xT)
        r_proj = region(T * D_IN * 4)
        proj = put("proj", [P, T, D_IN], r_proj)
        r_att = region((2 * 5 * SEQ + 2 * W) * 4)
        cT = put("cT", [P, 2, 5, SEQ], r_att, F32R)
        ropeA = put("ropeA", [P, W], r_att + 2 * 5 * SEQ * 4)
        ropeB = put("ropeB", [P, W], r_att + (2 * 5 * SEQ + W) * 4)
        NSM, NPT = 4, 3
        sm = put("sm", [P, NSM, 384], r_att)
        pT = put("pT", [P, NPT, 384], r_att + NSM * 384 * 4)
        junk = put("junk", [P, Q_LORA], r_att)
        trig = put("trig", [P, T, 2 * NF], r_att + 4096)
        turns = put("turns", [P, T, 2 * NF], r_att + 5120)
        invf = put("invf", [P, NF], r_att + 6144)
        posi = put("posi", [P, T], r_att + 6400, I32)
        posf = put("posf", [P, T], r_att + 6432)
        r_km = region(T * HEADS * QK * 4)
        km = put("km", [P, T, HEADS * QK], r_km)
        r_vm = region(T * HEADS * VDIM * 4)
        vm = put("vm", [P, T, HEADS * VDIM], r_vm)
        r_qT = region(HEADS * SEQ * 4)
        r_kT = region(HEADS * SEQ * 4)
        qTm = put("qTm", [QK, HEADS, SEQ], r_qT)
        kTm = put("kTm", [QK, HEADS, SEQ], r_kT)
        oT = put("oT", [P, 2, 2, 4, SEQ], r_qT, F32R)
        relu = put("relu", [P, 4, 384], r_kT)
        lnp = put("lnp", [P, 2, D], r_kT)
        r_dT = region(2 * 4 * SEQ * 4)
        dT = put("dT", [P, 2, 4, SEQ], r_dT)
        qTd, kTd = dT[:, 0], dT[:, 1]
        iT = dT[:, 0, 0:3, :]
        causal = fixed("causal", [P, T, SEQ])
        select = fixed("select", [P, T, SEQ])
        score = fixed("score", [P, T, SEQ])
        o_tok = [[proj[:, t, C_DQ + m * W:C_DQ + (m + 1) * W] for t in range(T)] for m in range(2)]

        silu = put("silu", [P, T, W], r_proj)
        hid = put("hid", [P, T, W], r_proj + 4096)
        hT = put("hT", [P, 2, 4, SEQ], r_proj + 8192, F32R)
        xeT = put("xeT", [P, 2, KD, CAP], r_proj + 16384, F32R)
        y = put("y", [P, T, D], r_proj + 24576)
        oe = put("oe", [P, D], r_dT)
        pick = put("pick", [P, T, CAP], r_km)
        comb_at = put("comb_at", [P, T, CAP], r_km + 1024)
        combT = put("combT", [P, SEQ], r_km + 2048)
        slot_no = put("slot_no", [P, 2 * CAP], r_km + 3072)
        before = put("before", [P, P], r_km + 4096)
        ones = put("ones", [P, P], r_km + 4608)
        wr = put("wr", [P, KD * EXPERTS], r_km + 5120)
        wrs = put("wrs", [P, 2, KD * EXPERTS], r_km + 5376, F32R)
        small = put("small", [P, 192], r_vm)
        rt = small[:, 0:160].rearrange("p (t n) -> p t n", t=T)
        r_list, r_top, r_keys = rt[:, :, 0:16], rt[:, :, 16:24], rt[:, :, 24:32]
        r_sel, r_exp, r_comb, r_pos, r_cnt = (rt[:, :, 32 + 8 * i:40 + 8 * i] for i in range(5))
        r_one = rt[:, :, 72:76]
        cur = small[:, 160:164]

        ident = fixed("ident", [P, P])
        rope32 = fixed("rope32", [P, T, 2, ROPE])
        rope64 = fixed("rope64", [P, T, 2, DH])
        gcol = fixed("gcol", [P, DEPTH, 5])
        expo = fixed("expo", [P, 1])
        stat = fixed("stat", [P, T, 2, 6])
        mv = fixed("mv", [P, T, 2])
        rstd = fixed("rstd", [P, T, 2])
        rms = fixed("rms", [P, T, 4])
        top8 = fixed("top8", [P, T, 8])
        mx = fixed("mx", [P, 16, T])
        den = fixed("den", [P, 16, T])
        rden = fixed("rden", [P, T, HEADS])
        flags = fixed("flags", [1, 64])
        jobs = fixed("jobs", [1, 32], I32)
        assert where[0] <= nc.sbuf_usable_end

        bank = [ctx.enter_context(nc.psum_tensor(f"bank{i}", [P, W], F32)) for i in range(8)]

        landed = [sem(f"landed{i}") for i in range(RAW)]
        heads_made, rests_made = sem("unit_heads_made"), sem("unit_rests_made")
        x_in, small_in, router_in, lnp_in, out_done = (sem(n) for n in ("x_in", "small_in", "router_in", "lnp_in", "out_done"))
        half_mm, ya_mm, w1_half, w3_half = (sem(n) for n in ("first_halves_mm", "mla_branch_mm", "w1_first_half_mm", "w3_first_half_mm"))
        c_rest, o_rest, m_rest, x_rest, h_rest, gat_rest, wr_ready = (
            sem(n) for n in ("latents_rest", "heads_rest", "merged_rest", "x_rest", "hidden_rest", "gathered_rest", "router_split"))
        consts = sem("consts_ready")
        sin_in, trig_done, tables = sem("sin_in_ready"), sem("trig_done"), sem("rope_tables_ready")
        proj_mm, proj_ev = sem("proj_mm"), sem("proj_evacuated")
        idx_roped, dsa_roped, kr_roped, qm_roped = (sem(n) for n in ("idx_roped", "dsa_roped", "kr_roped", "qm_roped"))
        idx_tr, idx_ev, dots_mm, relu_ev, scored, selected = (
            sem(n) for n in ("idx_turned", "idx_evacuated", "dots_mm", "relu_ready", "head_scored", "keys_selected"))
        sq_done, ms_ready, rms_ready, lat_norm, c_tr, c_ev = (
            sem(n) for n in ("squares_summed", "mean_square_ready", "rms_ready", "latents_normed", "latents_turned", "latents_evacuated"))
        uq_mm, uq_ev, ukv_mm, ukv_ev, kr_put = (sem(n) for n in ("uq_mm", "uq_evacuated", "ukv_mm", "ukv_evacuated", "key_rope_placed"))
        dsa_tr, dsa_ev, mq_tr, mq_ev, mk_tr, mk_ev = (
            sem(n) for n in ("dsa_turned", "dsa_evacuated", "mla_q_turned", "mla_q_evacuated", "mla_k_turned", "mla_k_evacuated"))
        qk_mm, row_max, probs, p_tr, p_ev, pv_mm, o_ev = (
            sem(n) for n in ("qk_mm", "row_max_ready", "probs_ready", "probs_turned", "probs_evacuated", "pv_mm", "heads_normed"))
        o_tr, oT_ev, y_mm, merged, m_tr, m_ev, out_mm = (
            sem(n) for n in ("heads_turned", "heads_evacuated", "branches_mm", "merged", "merged_turned", "merged_evacuated", "out_mm"))
        ln_var, ln_rstd, ln_done, x_tr, x_ev = (sem(n) for n in ("ln_variance", "ln_rstd", "ln_done", "x_turned", "x_evacuated"))
        w1_mm, w3_mm, silu_ev, hid_ev, h_tr, h_ev, w2_mm = (
            sem(n) for n in ("w1_mm", "w3_mm", "silu_ready", "hidden_ready", "hidden_turned", "hidden_evacuated", "w2_mm"))
        route_mm, chosen, exp_done, pos_mm, routed = (
            sem(n) for n in ("router_mm", "experts_chosen", "router_exp_done", "positions_mm", "routed"))
        slot_ids, cur_put, pick_put, comb_put = (sem(n) for n in ("slot_ids_ready", "expert_column_ready", "pick_ready", "combine_ready"))
        gat_mm, gat_ev, comb_tr, comb_ev, oe_ev, sc_mm, y_add = (
            sem(n) for n in ("gather_mm", "gather_evacuated", "combine_turned", "combine_evacuated", "expert_out_ready", "scatter_mm", "y_added"))
        pool_passed = sem("pool_passed_wait")
        dve_step, act_step, pool_step = sem("dve_step"), sem("act_step"), sem("pool_step")

        def number(unit):
            return STREAM.index(unit)

        def used_up(unit):
            kind = unit[0]
            if kind in ("w1", "w3"):
                full, half = (w1_mm, w1_half) if kind == "w1" else (w3_mm, w3_half)
                return (full, T * (unit[1] + 1)) if unit[2] else (half, unit[1] + 1)
            if kind == "w2":
                return w2_mm, 2 * unit[1] + unit[2] + 1
            l = unit[1]
            if kind == "in":
                return (proj_mm, T * NCH * l + T * (unit[2] + 1)) if unit[3] else (half_mm, HALVES * l + unit[2] + 1)
            if kind == "out":
                return (out_mm, 4 * l + 2 * (unit[2] + 1)) if unit[3] else (half_mm, HALVES * l + NCH + unit[2] + 1)
            if kind == "uq":
                return uq_mm, 4 * l + 2 * (unit[2] + 1)
            if kind == "ukv":
                return ukv_mm, 4 * (l + 1)
            return (ya_mm, 2 * l + unit[2] + 1) if kind == "oa" else (y_mm, 4 * l + 2 * (unit[2] + 1))

        def job_used_up(j, m):
            kind, g, half = JOB[m]
            past = 0 if m >= 0 else NG
            if kind == "w2":
                return w2_mm, 2 * NG * j + (2 * (DG - past) + 2 * g + half + 1)
            if half:
                return (w1_mm if kind == "w1" else w3_mm), NG * j + (T * DG - past + g + 1)
            return (w1_half if kind == "w1" else w3_half), NG * j + (DG - past + g + 1)

        def by_k(w, c, n, k0, k):
            return w[k0 * P:(k0 + k) * P, c:c + n].rearrange("(k p) n -> p k n", p=P)

        def source(unit):
            kind = unit[0]
            if kind == "in":
                c, n = CHUNKS[unit[2]]
                return by_k(a["w_in"][unit[1]], c, n, 4 * unit[3], 4), 4, n
            if kind == "out":
                return by_k(a["w_out"][unit[1]], unit[2] * W, W, 4 * unit[3], 4), 4, W
            if kind == "uq":
                return by_k(a["w_uq"][unit[1]], unit[2] * 384, 384, 0, 3), 3, 384
            if kind == "ukv":
                return by_k(a["w_ukv"][unit[1]], 0, 2 * W, 0, 2), 2, 2 * W
            if kind in ("oa", "ob"):
                return by_k(a[{"oa": "w_o_mla", "ob": "w_o_dsa"}[kind]][unit[1]], unit[2] * W, W, 0, 4), 4, W
            c, n = DENSE[unit[1]]
            if kind == "w2":
                return by_k(a["dense_w2"][0], unit[2] * W, W, c // P, n // P), n // P, W
            return by_k(a["dense_" + kind][0], c, n, 4 * unit[2], 4), 4, n

        def as_weights(view, k, n):
            return view[:, 0:k * n].rearrange("p (k n) -> p k n", k=k)

        def halves(n, k, cols):
            return [as_weights(split[:, n % SPLIT, i, :], k, cols) for i in (HEAD, REST)]

        def make_head(act, n):
            unit = STREAM[n]
            _, k, cols = source(unit)
            act.wait_ge(landed[n % RAW], 16 * (n // RAW + 1))
            if n >= SPLIT:
                act.wait_ge(*used_up(STREAM[n - SPLIT]))
            act.copy(split[:, n % SPLIT, HEAD, 0:k * cols], raw[:, n % RAW, 0:k * cols]).then_inc(heads_made, 1)

        def make_rest(dve, n):
            _, k, cols = source(STREAM[n])
            dve.wait_ge(heads_made, n + 1)
            dve.tensor_tensor(split[:, n % SPLIT, REST, 0:k * cols], raw[:, n % RAW, 0:k * cols],
                              split[:, n % SPLIT, HEAD, 0:k * cols].bitcast(F32), ALU.subtract).then_inc(rests_made, 1)

        def job_head(act, j, m):
            n = FIRST + m
            act.wait_ge(landed[n % RAW], j * (16 * PER_JOB // RAW) + 16 * (n // RAW + 1))
            if m < SPLIT:
                act.wait_ge(*used_up(STREAM[n - SPLIT]))
            act.wait_ge(*job_used_up(j, m - SPLIT))
            act.copy(split[:, n % SPLIT, HEAD, :], raw[:, n % RAW, :]).then_inc(heads_made, 1)

        def job_rest(dve, j, m):
            n = FIRST + m
            dve.wait_ge(heads_made, PER_JOB * j + (n + 1))
            dve.tensor_tensor(split[:, n % SPLIT, REST, :], raw[:, n % RAW, :],
                              split[:, n % SPLIT, HEAD, :].bitcast(F32), ALU.subtract).then_inc(rests_made, 1)

        block = ctx.enter_context(nc.Block())

        def crowded_experts(eng, body):
            many = eng.value_load(jobs[0:1, 2 * EXPERTS:2 * EXPERTS + 1], min_val=0, max_val=4)
            with eng.If(many > 0):
                with eng.Fori(0, EXPERTS) as e:
                    crowded = eng.value_load(jobs[0:1, bass.ds(e, 1)], min_val=0, max_val=1)
                    with eng.If(crowded > 0):
                        rank = eng.value_load(jobs[0:1, bass.ds(e + EXPERTS, 1)], min_val=0, max_val=4)
                        body(rank + EXPERTS, e)


        @block.sync
        def _(sp):
            sp.dma_start(x[:, :, :], a["x"][0].rearrange("(t p) d -> p t d", p=P)).then_inc(x_in, 16)
            for n, unit in enumerate(STREAM):
                if n >= RAW:
                    sp.wait_ge(rests_made, n - RAW + 1)
                src, k, cols = source(unit)
                sp.dma_start(as_weights(raw[:, n % RAW, :], k, cols), src).then_inc(landed[n % RAW], 16)

            def expert_stream(j, e):
                for m, (kind, g, half) in enumerate(JOB):
                    n = FIRST + m
                    w = a["moe_" + kind][0][e]
                    src = by_k(w, half * W, W, 4 * g, 4) if kind == "w2" else by_k(w, g * W, W, 4 * half, 4)
                    sp.wait_ge(rests_made, PER_JOB * j + (n - RAW + 1))
                    sp.dma_start(as_weights(raw[:, n % RAW, :], 4, W), src).then_inc(landed[n % RAW], 16)

            with sp.Fori(0, EXPERTS) as e:
                expert_stream(e, e)

            sp.wait_ge(routed, 1)
            crowded_experts(sp, expert_stream)
            sp.wait_ge(ln_done, 2 * DEPTH)
            sp.dma_start(out[0].rearrange("(t p) d -> p t d", p=P), x[:, :, :]).then_inc(out_done, 16)
            sp.wait_ge(out_done, 16)


        def pool_experts(pool):
            pool.wait_ge(merged, 4 * DEPTH)
            pool.memset(r_list[:, :, EXPERTS:16], UNUSED).then_inc(slot_ids, 1)
            pool.memset(ones[:, :], 1.0).then_inc(slot_ids, 1)
            pool.wait_ge(slot_ids, 2)
            pool.affine_select(out=before[:, :], in_=ones[:, :], compare_op=ALU.is_gt, fill=0.0,
                               base=0, pattern=[[1, P]], channel_multiplier=-1).then_inc(slot_ids, 1)
            pool.iota(slot_no[:, :], pattern=[[1, 2 * CAP]], base=0, channel_multiplier=0,
                      allow_small_or_imprecise_dtypes=True).then_inc(slot_ids, 1)
            pool.wait_ge(slot_ids, 4)
            pool.wait_ge(routed, 1)

            def one_hots(j, e, half):
                ids = slot_no[:, half * CAP:(half + 1) * CAP]
                pool.wait_ge(comb_put, j + CREDIT)
                pool.tensor_copy(cur[:, 0:2], r_pos[:, :, bass.ds(e, 1)].rearrange("p t n -> p (t n)"))
                pool.tensor_copy(cur[:, 2:4], r_comb[:, :, bass.ds(e, 1)].rearrange("p t n -> p (t n)")).then_inc(cur_put, 1)
                pool.wait_ge(cur_put, j + 1)
                pool.wait_ge(gat_mm, 2 * j + CREDIT)
                pool.sem_inc(pool_passed, 1)
                for t in range(T):
                    ins = pool.tensor_scalar(pick[:, t, :], ids, cur[:, t:t + 1], None, ALU.is_equal)
                ins.then_inc(pick_put, 1)
                pool.wait_ge(pick_put, j + 1)
                pool.wait_ge(comb_tr, j + CREDIT)
                for t in range(T):
                    ins = pool.tensor_tensor(comb_at[:, t, :], pick[:, t, :], cur[:, 2 + t:3 + t].to_broadcast([P, CAP]), ALU.mult)
                ins.then_inc(comb_put, 1)

            pool.sem_inc(comb_put, CREDIT)
            with pool.Fori(0, EXPERTS) as e:
                one_hots(e, e, 0)
            crowded_experts(pool, lambda j, e: one_hots(j, e, 1))

        @block.gpsimd
        def _(pool):
            n = [0]

            def step(ins):
                n[0] += 1
                ins.then_inc(pool_step, 1)
                pool.wait_ge(pool_step, n[0])

            step(pool.memset(ident[:, :], 0.0))
            step(pool.memset(causal[:, :, :], 0.0))
            step(pool.memset(expo[:, :], -0.5))
            step(pool.affine_select(out=ident[:, :], in_=ident[:, :], compare_op=ALU.not_equal, fill=1.0,
                                    base=0, pattern=[[-1, P]], channel_multiplier=1))
            for t in range(T):
                step(pool.affine_select(out=causal[:, t, :], in_=causal[:, t, :], compare_op=ALU.is_ge, fill=MASKED,
                                        base=t * P, pattern=[[-1, SEQ]], channel_multiplier=1))
            pool.sem_inc(consts, 1)

            for l in range(DEPTH):
                for t in range(T):
                    k = T * l + t + 1
                    pool.wait_ge(ms_ready, k)
                    pool.tensor_tensor(rms[:, t, 2:4], rms[:, t, 0:2], expo[:, :].to_broadcast([P, 2]), ALU.pow).then_inc(rms_ready, 1)
                for s in range(2):
                    if l == 1 and s == 1:
                        pool_experts(pool)
                    for t in range(T):
                        k = T * (2 * l + s) + t + 1
                        pool.wait_ge(ln_var, k)
                        pool.tensor_tensor(rstd[:, t, 1:2], rstd[:, t, 0:1], expo[:, :], ALU.pow).then_inc(ln_rstd, 1)


        def load_ln(act, l, s):
            g, b = (("ln1_g", "ln1_b"), ("ln2_g", "ln2_b"))[s]
            if s == 0:
                act.wait_ge(y_mm, 4 * (l + 1))
            else:
                act.wait_ge(ln_done, 2 * l + 1)
            act.dma_start(lnp[:, 0, :], a[g][l:l + 1, :].partition_broadcast(P)).then_inc(lnp_in, 16)
            act.dma_start(lnp[:, 1, :], a[b][l:l + 1, :].partition_broadcast(P)).then_inc(lnp_in, 16)

        def blocks(b, k):
            return b[:, 0:k * P].rearrange("p (k s) -> p k s", k=k)

        def act_dense(act):
            def silus(g):
                n = DENSE[g][1]
                for t in range(T):
                    k = T * g + t
                    act.wait_ge(w1_mm, k + 1)
                    if g:
                        act.wait_ge(hid_ev, k - 1)
                    act.activation(silu[:, t, 0:n], bank[2 * t][:, 0:n], ACT.Silu).then_inc(silu_ev, 1)

            def turned(g):
                k = DENSE[g][1] // P
                for t in range(T):
                    act.wait_ge(h_tr, T * g + t + 1)
                    act.copy(hT[:, HEAD, 0:k, t * P:(t + 1) * P], blocks(bank[2 * t], k)).then_inc(h_ev, 1)

            for m, (kind, g, half) in enumerate(ffn_units(DG)):
                if (kind, half) == ("w1", 1):
                    silus(g)
                if (kind, half) == ("w2", 1) and g + 1 < DG:
                    turned(g + 1)
                if (kind, g, half) == ("w3", 0, 1):
                    turned(0)
                make_head(act, MIXER + m + SPLIT)

        def act_experts(act):
            act.wait_ge(slot_ids, 4)
            act.dma_start(wr[:, :].rearrange("p (k e) -> p k e", k=KD), a["moe_router"][0].rearrange("(k p) e -> p k e", p=P)).then_inc(router_in, 16)
            act.wait_ge(router_in, 16)
            act.copy(wrs[:, HEAD, :], wr[:, :]).then_inc(wr_ready, 1)
            act.wait_ge(chosen, 1)
            act.activation(r_exp, r_exp, ACT.Exp).then_inc(exp_done, 1)

            def job(j):
                def turned(g):
                    act.wait_ge(h_tr, NG * j + (T * DG + g + 1))
                    act.copy(hT[:, HEAD, :, 0:CAP], blocks(bank[6], 4)).then_inc(h_ev, 1)

                for m in range(SPLIT):
                    job_head(act, j, m)
                for h in range(2):
                    act.wait_ge(gat_mm, 2 * j + (h + 1 + CREDIT))
                    act.copy(xeT[:, HEAD, 4 * h:4 * h + 4, :], blocks(bank[6 + h], 4)).then_inc(gat_ev, 1)
                for m, (kind, g, half) in enumerate(JOB):
                    up_end = (kind, half) == ("w1", 1)
                    if up_end:
                        act.wait_ge(w1_mm, NG * j + (T * DG + g + 1))
                        act.wait_ge(hid_ev, NG * j + (T * DG + max(g - 1, 0)))
                        act.activation(silu[:, g % 2, :], bank[2 * (g % 2)][:, :], ACT.Silu).then_inc(silu_ev, 1)
                    if m + SPLIT < PER_JOB:
                        job_head(act, j, m + SPLIT)
                    if up_end and g:
                        turned(g - 1)
                    if (kind, g, half) == ("w2", 1, 1):
                        act.wait_ge(comb_tr, j + (1 + CREDIT))
                        act.wait_ge(sc_mm, 4 * j + CREDIT)
                        act.copy(combT[:, :], bank[7][:, 0:SEQ]).then_inc(comb_ev, 1)
                    if (kind, g, half) == ("w2", NG - 2, 1):
                        turned(NG - 1)
                act.wait_ge(w2_mm, 2 * NG * j + 2 * (DG + NG) - 1)
                act.wait_ge(sc_mm, 4 * j + CREDIT)
                act.copy(oe[:, 0:W], bank[4][:, :]).then_inc(oe_ev, 1)
                act.wait_ge(w2_mm, 2 * NG * j + 2 * (DG + NG))
                act.copy(oe[:, W:D], bank[5][:, :]).then_inc(oe_ev, 1)

            act.sem_inc(comb_ev, CREDIT)
            act.sem_inc(oe_ev, CREDIT)
            with act.Fori(0, EXPERTS) as e:
                job(e)
            crowded_experts(act, lambda j, e: job(j))

        @block.scalar
        def _(act):
            act.dma_start(posi[:, :], a["positions"].rearrange("o (t p) -> p (o t)", p=P), allow_slow_non_contiguous=True).then_inc(small_in, 16)
            act.dma_start(invf[:, :], a["inv_freq"].partition_broadcast(P)).then_inc(small_in, 16)
            for l in range(DEPTH):
                act.dma_start(gcol[:, l, 0:3], a["mla_q_norm"][l].rearrange("(k p) -> p k", p=P), allow_slow_non_contiguous=True).then_inc(small_in, 16)
                act.dma_start(gcol[:, l, 3:5], a["mla_kv_norm"][l].rearrange("(k p) -> p k", p=P), allow_slow_non_contiguous=True).then_inc(small_in, 16)
            act.wait_ge(sin_in, 1)
            act.activation(trig[:, :, :], trig[:, :, :], ACT.Sin).then_inc(trig_done, 1)

            def turned_x(k):
                for t in range(T):
                    for h in range(2):
                        n = 2 * t + h
                        act.wait_ge(x_tr, 4 * k + n + 1)
                        act.copy(xT[:, HEAD, 4 * h:4 * h + 4, t * P:(t + 1) * P], blocks(bank[n], 4)).then_inc(x_ev, 1)

            for n in range(SPLIT):
                make_head(act, n)
            turned_x(0)
            for l in range(DEPTH):
                first = LAYER * l

                def head(m):
                    if first + m < FIRST:
                        make_head(act, first + m)

                def chunk(c):
                    c0, n = CHUNKS[c]
                    for t in range(T):
                        k = T * c + t
                        act.wait_ge(proj_mm, T * NCH * l + k + 1)
                        src, dst = bank[k % 4], proj[:, t, c0:c0 + n]
                        raw_cols = max(0, min(n, C_GA - c0))
                        if raw_cols == n:
                            act.copy(dst, src[:, 0:n]).then_inc(proj_ev, 1)
                        elif raw_cols == 0:
                            act.activation(dst, src[:, 0:n], ACT.Sigmoid).then_inc(proj_ev, 1)
                        else:
                            act.copy(dst[:, 0:raw_cols], src[:, 0:raw_cols])
                            act.activation(dst[:, raw_cols:n], src[:, raw_cols:n], ACT.Sigmoid).then_inc(proj_ev, 1)

                def squares():
                    for t in range(T):
                        if l or t:
                            act.wait_ge(sq_done, T * l + t)
                        act.wait_ge(proj_ev, T * NCH * l + 4)
                        if l:
                            act.wait_ge(rms_ready, T * (l - 1) + t + 1)
                        act.activation(junk[:, 0:Q_LORA], proj[:, t, C_Q:C_KV], ACT.Square, accum_out=rms[:, t, 0:1]).then_inc(act_step, 1)
                        act.wait_ge(act_step, T * l + t + 1)
                        act.activation(junk[:, 0:KV_LORA], proj[:, t, C_KV:C_KR], ACT.Square, accum_out=rms[:, t, 1:2]).then_inc(sq_done, 1)

                def indexer_turned():
                    for t in range(T):
                        act.wait_ge(idx_tr, T * l + t + 1)
                        act.copy(iT[:, :, t * P:(t + 1) * P], blocks(bank[4 + t], 3)).then_inc(idx_ev, 1)

                def relus(heads):
                    for h in heads:
                        k = IDX_HEADS * l + h
                        act.wait_ge(dots_mm, k + 1)
                        if h >= 4:
                            act.wait_ge(scored, k - 3)
                        act.activation(relu[:, h % 4, :], bank[4 + h % 4][:, 0:384], ACT.Relu,
                                       scale=float(IDX_HEADS * IDX_DIM) ** -0.5).then_inc(relu_ev, 1)

                def latents_turned():
                    for t in range(T):
                        act.wait_ge(c_tr, T * l + t + 1)
                        act.wait_ge(small_in, 6 * 16)
                        for k in range(5):
                            b = bank[4 + 2 * t + k // 4]
                            ins = act.activation(cT[:, HEAD, k, t * P:(t + 1) * P], b[:, (k % 4) * P:(k % 4 + 1) * P], ACT.Copy,
                                                 scale=gcol[:, l, k:k + 1])
                        ins.then_inc(c_ev, 1)

                for m in range(2 * NCH):
                    head(m + SPLIT)
                    if m % 2:
                        chunk(m // 2)
                    if m == 3:
                        squares()
                    if m == 11:
                        indexer_turned()
                    if m == 13:
                        relus(range(0, 4))
                    if m == 14:
                        relus(range(4, 8))
                    if m == 15:
                        latents_turned()
                for h in range(2):
                    head(2 * NCH + h + SPLIT)
                    for t in range(T):
                        act.wait_ge(uq_mm, 4 * l + 2 * h + t + 1)
                        act.copy(qm[:, t, h * 384:(h + 1) * 384], bank[4 + 2 * t + h][:, 0:384]).then_inc(uq_ev, 1)
                head(2 * NCH + 2 + SPLIT)
                for i in range(2):
                    for t in range(T):
                        act.wait_ge(dsa_tr, 4 * l + 2 * i + t + 1)
                        act.copy(dT[:, i, :, t * P:(t + 1) * P], blocks(bank[2 * i + t], 4)).then_inc(dsa_ev, 1)
                for t in range(T):
                    for h in range(2):
                        act.wait_ge(mq_tr, 4 * l + 2 * t + h + 1)
                        act.copy(qTm[:, 4 * h:4 * h + 4, t * P:(t + 1) * P],
                                 bank[4 + 2 * t + h][0:QK, :].rearrange("p (k s) -> p k s", k=4)).then_inc(mq_ev, 1)

                def exps(u):
                    k = 16 * l + u
                    scale = float(QK if u < 8 else DH) ** -0.5
                    act.wait_ge(row_max, k + 1)
                    act.activation(sm[:, u % NSM, 0:P], sm[:, u % NSM, 0:P], ACT.Exp, bias=mx[:, u, 0:1], scale=scale,
                                   accum_out=den[:, u, 0:1])
                    act.activation(sm[:, u % NSM, P:384], sm[:, u % NSM, P:384], ACT.Exp, bias=mx[:, u, 1:2], scale=scale,
                                   accum_out=den[:, u, 1:2]).then_inc(probs, 1)

                def turned_probs(u):
                    k = 16 * l + u
                    act.wait_ge(p_tr, k + 1)
                    if u >= NPT:
                        act.wait_ge(pv_mm, k - NPT + 1)
                    act.copy(pT[:, u % NPT, :], bank[2 + u % 2][:, 0:384]).then_inc(p_ev, 1)

                for i in range(16 + 1):
                    if i < 16:
                        exps(i)
                    if i >= 1:
                        turned_probs(i - 1)
                for m in range(2):
                    for t in range(T):
                        act.wait_ge(o_tr, 4 * l + 2 * m + t + 1)
                        act.copy(oT[:, HEAD, m, :, t * P:(t + 1) * P], blocks(bank[2 * m + t], 4)).then_inc(oT_ev, 1)
                for m in range(21, 25):
                    head(m + SPLIT)
                load_ln(act, l, 0)
                for t in range(T):
                    for h in range(2):
                        act.wait_ge(m_tr, 4 * l + 2 * t + h + 1)
                        act.copy(xT[:, HEAD, 4 * h:4 * h + 4, t * P:(t + 1) * P], blocks(bank[2 * t + h], 4)).then_inc(m_ev, 1)
                for m in range(25, 29):
                    head(m + SPLIT)
                turned_x(2 * l + 1)
                load_ln(act, l, 1)
                if l == 0:
                    act_dense(act)
                    turned_x(2)
                else:
                    act_experts(act)

        def rest_of(dve, dst, src, done):
            return dve.tensor_tensor(dst[REST], src, dst[HEAD].bitcast(F32), ALU.subtract).then_inc(done, 1)

        def dve_dense(dve, step):
            def hidden(g):
                n = DENSE[g][1]
                for t in range(T):
                    k = T * g + t + 1
                    dve.wait_ge(silu_ev, k)
                    dve.wait_ge(w3_mm, k)
                    if g:
                        dve.wait_ge(h_tr, k - T)
                    dve.tensor_tensor(hid[:, t, 0:n], silu[:, t, 0:n], bank[1 + 2 * t][:, 0:n], ALU.mult).then_inc(hid_ev, 1)

            def turned(g):
                k = DENSE[g][1] // P
                for t in range(T):
                    dve.wait_ge(h_ev, T * g + t + 1)
                    rest_of(dve, [hT[:, i, 0:k, t * P:(t + 1) * P] for i in (HEAD, REST)], blocks(bank[2 * t], k), h_rest)

            for m, (kind, g, half) in enumerate(ffn_units(DG)):
                if (kind, half) == ("w3", 1):
                    hidden(g)
                if (kind, half) == ("w2", 1) and g + 1 < DG:
                    turned(g + 1)
                if (kind, g, half) == ("w3", 0, 1):
                    turned(0)
                if m < PER_DENSE - 1:
                    make_rest(dve, MIXER + m + SPLIT)
            dve.wait_ge(w2_mm, 2 * DG)
            for t in range(T):
                for h in range(2):
                    step(dve.scalar_tensor_tensor(out=x[:, t, h * W:(h + 1) * W], in0=x[:, t, h * W:(h + 1) * W], scalar=ALPHA,
                                                  in1=bank[4 + 2 * t + h][:, :], op0=ALU.mult, op1=ALU.add))

        def dve_experts(dve, step):
            dve.wait_ge(wr_ready, 1)
            dve.tensor_tensor(wrs[:, REST, :], wr[:, :], wrs[:, HEAD, :].bitcast(F32), ALU.subtract).then_inc(wr_ready, 1)
            dve.wait_ge(slot_ids, 4)
            for t in range(T):
                lg = bank[6 + t]
                dve.wait_ge(route_mm, t + 1)
                step(dve.tensor_copy(r_list[:, t, 0:EXPERTS], lg[:, 0:EXPERTS]))
                step(dve.max(r_top[:, t, :], r_list[:, t, 0:EXPERTS]))
                dve.tensor_copy(r_keys[:, t, 0:2], r_top[:, t, 0:2])
                step(dve.memset(r_keys[:, t, 2:8], UNUSED))
                step(dve.match_replace(out=r_list[:, t, :], in_to_replace=r_keys[:, t, :], in_values=r_list[:, t, :],
                                       imm_value=TAKEN))
                step(dve.tensor_scalar(r_sel[:, t, :], r_list[:, t, 0:EXPERTS], TAKEN * 0.5, None, ALU.is_lt))
                step(dve.tensor_scalar(r_one[:, t, 0:1], r_top[:, t, 0:1], -1.0, None, ALU.mult))
                step(dve.tensor_scalar(r_exp[:, t, :], lg[:, 0:EXPERTS], r_one[:, t, 0:1], None, ALU.add))
            dve.memset(flags[:, :], 0.0).then_inc(chosen, 1)
            dve.wait_ge(chosen, 1)
            dve.wait_ge(exp_done, 1)
            for t in range(T):
                step(dve.tensor_tensor(r_exp[:, t, :], r_exp[:, t, :], r_sel[:, t, :], ALU.mult))
                step(dve.reduce_sum(r_one[:, t, 1:2], r_exp[:, t, :], AX_X))
                step(dve.reciprocal(r_one[:, t, 2:3], r_one[:, t, 1:2]))
                step(dve.tensor_scalar(r_comb[:, t, :], r_exp[:, t, :], r_one[:, t, 2:3], None, ALU.mult))
            dve.wait_ge(pos_mm, 1)
            for t in range(T):
                step(dve.tensor_scalar(r_pos[:, t, :], bank[6][:, t * EXPERTS:(t + 1) * EXPERTS], 1.0, None, ALU.add))
                step(dve.tensor_tensor(r_pos[:, t, :], r_pos[:, t, :], r_sel[:, t, :], ALU.mult))
                step(dve.tensor_scalar(r_pos[:, t, :], r_pos[:, t, :], -1.0, None, ALU.add))
            E = EXPERTS
            over, s1, s2, s4 = (flags[0:1, i * 16:(i + 1) * 16] for i in range(4))
            step(dve.tensor_scalar(over[:, E:2 * E], bank[6][0:1, 2 * E:3 * E], float(CAP), None, ALU.is_gt))
            for src, dst, by in ((over, s1, 1), (s1, s2, 2), (s2, s4, 4)):
                step(dve.tensor_tensor(dst[:, E:2 * E], src[:, E:2 * E], src[:, E - by:2 * E - by], ALU.add))
            step(dve.tensor_copy(jobs[0:1, 0:E], over[:, E:2 * E]))
            step(dve.tensor_tensor(jobs[0:1, E:2 * E], s4[:, E:2 * E], over[:, E:2 * E], ALU.subtract))
            dve.tensor_copy(jobs[0:1, 2 * E:2 * E + 1], s4[:, 2 * E - 1:2 * E]).then_inc(routed, 1)
            for t in range(T):
                step(dve.tensor_scalar(y[:, t, :], x[:, t, :], ALPHA, None, ALU.mult))

            def job(j):
                for m in range(SPLIT):
                    job_rest(dve, j, m)
                for h in range(2):
                    dve.wait_ge(gat_ev, 2 * j + (h + 1))
                    rest_of(dve, [xeT[:, i, 4 * h:4 * h + 4, :] for i in (HEAD, REST)], blocks(bank[6 + h], 4), gat_rest)

                def hidden(g):
                    k = T * DG + g + 1
                    dve.wait_ge(silu_ev, NG * j + k)
                    dve.wait_ge(w3_mm, NG * j + k)
                    dve.wait_ge(h_tr, NG * j + (k - (2 if g else 1)))
                    dve.tensor_tensor(hid[:, g % 2, :], silu[:, g % 2, :], bank[1 + 2 * (g % 2)][:, :], ALU.mult).then_inc(hid_ev, 1)

                def turned(g):
                    dve.wait_ge(h_ev, NG * j + (T * DG + g + 1))
                    rest_of(dve, [hT[:, i, :, 0:CAP] for i in (HEAD, REST)], blocks(bank[6], 4), h_rest)

                for m, (kind, g, half) in enumerate(JOB):
                    if (kind, half) == ("w3", 1):
                        hidden(g)
                    if m + SPLIT < PER_JOB:
                        job_rest(dve, j, m + SPLIT)
                    if (kind, half) == ("w1", 1) and g:
                        turned(g - 1)
                    if (kind, g, half) == ("w2", NG - 2, 1):
                        turned(NG - 1)
                dve.wait_ge(y_add, 4 * j + CREDIT)
                for h in range(2):
                    for t in range(T):
                        dve.wait_ge(sc_mm, 4 * j + (2 * h + t + 1 + CREDIT))
                        dve.tensor_tensor(y[:, t, h * W:(h + 1) * W], y[:, t, h * W:(h + 1) * W], bank[2 * t + h][:, :], ALU.add).then_inc(y_add, 1)

            dve.sem_inc(y_add, CREDIT)
            with dve.Fori(0, EXPERTS) as e:
                job(e)
            crowded_experts(dve, lambda j, e: job(j))
            extra = dve.value_load(jobs[0:1, 2 * EXPERTS:2 * EXPERTS + 1], min_val=0, max_val=4)
            dve.wait_ge(y_add, 4 * extra + (4 * EXPERTS + CREDIT))

        @block.vector
        def _(dve):
            n = [0]

            def step(ins):
                n[0] += 1
                ins.then_inc(dve_step, 1)
                dve.wait_ge(dve_step, n[0])

            dve.wait_ge(small_in, 6 * 16)
            step(dve.tensor_copy(posf[:, :], posi[:, :]))
            hi, mid, lo = split_2pi()
            for t in range(T):
                for h in range(2):
                    ins = dve.tensor_scalar(trig[:, t, h * NF:(h + 1) * NF], invf[:, :], posf[:, t:t + 1], None, ALU.mult)
            step(ins)
            for h in range(2):
                cols = slice(h * NF, (h + 1) * NF)
                step(dve.tensor_scalar(turns[:, :, cols], trig[:, :, cols], 1.0 / TWO_PI, 0.25 * h, ALU.mult, ALU.add))
            step(dve.tensor_scalar(turns[:, :, :], turns[:, :, :], ROUND, None, ALU.add))
            step(dve.tensor_scalar(turns[:, :, :], turns[:, :, :], ROUND, None, ALU.subtract))
            for part in (hi, mid, lo):
                step(dve.scalar_tensor_tensor(out=trig[:, :, :], in0=turns[:, :, :], scalar=-part, in1=trig[:, :, :],
                                              op0=ALU.mult, op1=ALU.add))
            step(dve.tensor_scalar(trig[:, :, NF:2 * NF], trig[:, :, NF:2 * NF], HALF_PI, None, ALU.add))
            dve.tensor_scalar(trig[:, :, :], trig[:, :, :], PI_F, -PI_F, ALU.min, ALU.max).then_inc(sin_in, 1)
            for unit in range(SPLIT):
                make_rest(dve, unit)
            dve.wait_ge(trig_done, 1)
            for tab, f0, nf in ((rope32, 0, RQ), (rope64, RQ, RD)):
                s_, c_ = trig[:, :, f0:f0 + nf], trig[:, :, NF + f0:NF + f0 + nf]
                dve.tensor_copy(tab[:, :, 0, 0:nf], c_)
                dve.tensor_copy(tab[:, :, 0, nf:2 * nf], c_)
                dve.tensor_scalar(tab[:, :, 1, 0:nf], s_, -1.0, None, ALU.mult)
                step(dve.tensor_copy(tab[:, :, 1, nf:2 * nf], s_))

            def rope(v, t, heads, d, tab, done=None):
                h2 = d // 2
                c_ = tab[:, t, 0:1, :].to_broadcast([P, heads, d])
                A = ropeA[:, 0:heads * d].rearrange("p (h d) -> p h d", h=heads)
                B = ropeB[:, 0:heads * d].rearrange("p (h d) -> p h d", h=heads)
                dve.tensor_tensor(A, v, c_, ALU.mult)
                dve.tensor_tensor(B[:, :, 0:h2], v[:, :, h2:d], tab[:, t, 1:2, 0:h2].to_broadcast([P, heads, h2]), ALU.mult)
                step(dve.tensor_tensor(B[:, :, h2:d], v[:, :, 0:h2], tab[:, t, 1:2, h2:d].to_broadcast([P, heads, h2]), ALU.mult))
                ins = dve.tensor_tensor(v, A, B, ALU.add)
                if done is None:
                    step(ins)
                else:
                    ins.then_inc(done[0], 1)
                    dve.wait_ge(done[0], done[1])

            def rest_x(k):
                for t in range(T):
                    for h in range(2):
                        dve.wait_ge(x_ev, 4 * k + 2 * t + h + 1)
                        rest_of(dve, [xT[:, i, 4 * h:4 * h + 4, t * P:(t + 1) * P] for i in (HEAD, REST)], blocks(bank[2 * t + h], 4), x_rest)

            def heads_of(v, heads):
                return v.rearrange("p (h d) -> p h d", h=heads)

            def layer_norm(k, src, while_power=()):
                for t in range(T):
                    for h in range(2):
                        ins = dve.bn_stats(stat[:, t, h, :], src[:, t, h * W:(h + 1) * W])
                    step(ins)
                    step(dve.bn_aggr(mv[:, t, :], stat[:, t, :, :].rearrange("p a b -> p (a b)")))
                    dve.tensor_scalar(rstd[:, t, 0:1], mv[:, t, 1:2], EPS, None, ALU.add).then_inc(ln_var, 1)
                for unit in while_power:
                    make_rest(dve, unit)
                for t in range(T):
                    dve.wait_ge(ln_rstd, T * k + t + 1)
                    step(dve.tensor_scalar(x[:, t, :], src[:, t, :], mv[:, t, 0:1], rstd[:, t, 1:2], ALU.subtract, ALU.mult))
                    dve.wait_ge(lnp_in, 32 * (k + 1))
                    step(dve.tensor_tensor(x[:, t, :], x[:, t, :], lnp[:, 0, :], ALU.mult))
                    ins = dve.tensor_tensor(x[:, t, :], x[:, t, :], lnp[:, 1, :], ALU.add)
                    if t == T - 1:
                        ins.then_inc(ln_done, 1)
                        dve.wait_ge(ln_done, k + 1)
                    else:
                        step(ins)

            dve.wait_ge(consts, 1)
            rest_x(0)
            for l in range(DEPTH):
                first = LAYER * l

                def rest(m):
                    if first + m < FIRST:
                        make_rest(dve, first + m)

                def latents():
                    for t in range(T):
                        dve.wait_ge(sq_done, T * l + t + 1)
                        step(dve.tensor_scalar(rms[:, t, 0:1], rms[:, t, 0:1], 1.0 / Q_LORA, EPS, ALU.mult, ALU.add))
                        dve.tensor_scalar(rms[:, t, 1:2], rms[:, t, 1:2], 1.0 / KV_LORA, EPS, ALU.mult, ALU.add).then_inc(ms_ready, 1)

                def latents_normed():
                    for t in range(T):
                        dve.wait_ge(rms_ready, T * l + t + 1)
                        dve.tensor_scalar(proj[:, t, C_Q:C_KV], proj[:, t, C_Q:C_KV], rms[:, t, 2:3], None, ALU.mult)
                        dve.tensor_scalar(proj[:, t, C_KV:C_KR], proj[:, t, C_KV:C_KR], rms[:, t, 3:4], None, ALU.mult).then_inc(lat_norm, 1)
                    for t in range(T):
                        rope(heads_of(proj[:, t, C_KR:C_DQ], 1), t, 1, ROPE, rope32)

                def ropes_dsa(t):
                    dve.wait_ge(proj_ev, T * NCH * l + 8)
                    rope(heads_of(proj[:, t, C_DQ:C_DK], HEADS), t, HEADS, DH, rope64)
                    rope(heads_of(proj[:, t, C_DK:C_DV], HEADS), t, HEADS, DH, rope64, (dsa_roped, T * l + t + 1))

                def ropes_indexer():
                    dve.wait_ge(proj_ev, T * NCH * l + 10)
                    for t in range(T):
                        rope(heads_of(proj[:, t, C_IQ:C_IK], IDX_HEADS), t, IDX_HEADS, IDX_DIM, rope32)
                        rope(heads_of(proj[:, t, C_IK:C_IW], 1), t, 1, IDX_DIM, rope32)
                        ik4 = score[:, t, 0:P].rearrange("p (r d) -> p r d", r=4)
                        dve.tensor_copy(ik4, proj[:, t:t + 1, C_IK:C_IW].to_broadcast([P, 4, IDX_DIM])).then_inc(idx_roped, 1)

                def scores(heads):
                    dve.wait_ge(idx_tr, T * (l + 1))
                    for h in heads:
                        dve.wait_ge(relu_ev, IDX_HEADS * l + h + 1)
                        for t in range(T):
                            keys = (t + 1) * P
                            part = relu[:, h % 4, t * P:t * P + keys]
                            prev = causal[:, t, 0:keys] if h == 0 else score[:, t, 0:keys]
                            ins = dve.scalar_tensor_tensor(out=score[:, t, 0:keys], in0=part, scalar=proj[:, t, C_IW + h:C_IW + h + 1],
                                                           in1=prev, op0=ALU.mult, op1=ALU.add)
                        ins.then_inc(scored, 1)
                        dve.wait_ge(scored, IDX_HEADS * l + h + 1)

                def best_keys(rounds):
                    for r in rounds:
                        for t in range(T):
                            ins = dve.max(top8[:, t, :], score[:, t, 0:(t + 1) * P])
                        step(ins)
                        for t in range(T):
                            keys = (t + 1) * P
                            ins = dve.match_replace(out=score[:, t, 0:keys], in_to_replace=top8[:, t, :],
                                                    in_values=score[:, t, 0:keys], imm_value=TAKEN)
                        step(ins)

                def selection():
                    for t in range(T):
                        keys = (t + 1) * P
                        step(dve.tensor_scalar(select[:, t, 0:keys], score[:, t, 0:keys], TAKEN * 0.5, MASKED, ALU.is_gt, ALU.mult))
                        step(dve.tensor_tensor(select[:, t, 0:keys], select[:, t, 0:keys], causal[:, t, 0:keys], ALU.add))

                def latents_rest():
                    for t in range(T):
                        dve.wait_ge(c_ev, T * l + t + 1)
                        for k in range(5):
                            at = slice(t * P, (t + 1) * P)
                            ins = dve.scalar_tensor_tensor(out=cT[:, REST, k, at], in0=bank[4 + 2 * t + k // 4][:, (k % 4) * P:(k % 4 + 1) * P],
                                                           scalar=gcol[:, l, k:k + 1], in1=cT[:, HEAD, k, at].bitcast(F32),
                                                           op0=ALU.mult, op1=ALU.subtract)
                        ins.then_inc(c_rest, 1)

                R = N_SEL // 8
                for m in range(2 * NCH):
                    rest(m + SPLIT)
                    if m == 3:
                        latents()
                    if m == 4:
                        latents_normed()
                    if m in (7, 8):
                        ropes_dsa(m - 7)
                    if m == 9:
                        ropes_indexer()
                    if m == 13:
                        scores(range(0, 4))
                    if m == 14:
                        scores(range(4, 8))
                    if m == 15:
                        latents_rest()
                        best_keys(range(0, R // 2))
                    if m == 16:
                        best_keys(range(R // 2, R))
                    if m == 17:
                        selection()
                rest(18 + SPLIT)
                for t in range(T):
                    for h in range(2):
                        dve.wait_ge(ukv_mm, 4 * l + 2 * t + h + 1)
                        src = bank[2 * t + h][:, :].rearrange("p (h d) -> p h d", h=4)
                        dve.tensor_copy(heads_of(km[:, t, :], HEADS)[:, 4 * h:4 * h + 4, 0:NOPE], src[:, :, 0:NOPE])
                        dve.tensor_copy(heads_of(vm[:, t, :], HEADS)[:, 4 * h:4 * h + 4, :], src[:, :, NOPE:P]).then_inc(ukv_ev, 1)
                    dve.tensor_copy(heads_of(km[:, t, :], HEADS)[:, :, NOPE:QK],
                                    proj[:, t:t + 1, C_KR:C_DQ].to_broadcast([P, HEADS, ROPE])).then_inc(kr_put, 1)
                dve.wait_ge(uq_ev, 4 * (l + 1))
                for t in range(T):
                    rope(heads_of(qm[:, t, :], HEADS)[:, :, NOPE:QK], t, HEADS, ROPE, rope32, (qm_roped, T * l + t + 1))
                for t in range(T):
                    for h in range(2):
                        dve.wait_ge(mk_tr, 4 * l + 2 * t + h + 1)
                        dve.tensor_copy(kTm[:, 4 * h:4 * h + 4, t * P:(t + 1) * P],
                                        bank[2 * t + h][0:QK, :].rearrange("p (k s) -> p k s", k=4)).then_inc(mk_ev, 1)

                def maxima(u):
                    k = 16 * l + u
                    mask = causal if u < 8 else select
                    scale = float(QK if u < 8 else DH) ** -0.5
                    dve.wait_ge(qk_mm, k + 1)
                    if u >= NSM:
                        dve.wait_ge(p_tr, k - NSM + 1)
                    for t in range(T):
                        lo_, keys = t * P, (t + 1) * P
                        ins = dve.tensor_tensor_reduce(sm[:, u % NSM, lo_:lo_ + keys], bank[u % 2][:, lo_:lo_ + keys],
                                                       mask[:, t, 0:keys], 1.0, FLOOR, ALU.add, ALU.max, mx[:, u, t:t + 1])
                    step(ins)
                    dve.tensor_scalar(mx[:, u, :], mx[:, u, :], -scale, None, ALU.mult).then_inc(row_max, 1)

                def norm_heads(m):
                    dve.wait_ge(pv_mm, 16 * l + 8 * (m + 1))
                    for t in range(T):
                        step(dve.reciprocal(rden[:, t, :], den[:, 8 * m:8 * m + 8, t]))
                        dve.tensor_tensor(heads_of(o_tok[m][t], HEADS), heads_of(bank[4 + 2 * m + t][:, :], HEADS),
                                          rden[:, t, :].unsqueeze(2).to_broadcast([P, HEADS, VDIM]), ALU.mult).then_inc(o_ev, 1)

                for u in range(16):
                    maxima(u)
                    if u == 4:
                        rest(19 + SPLIT)
                    if u == 8:
                        rest(20 + SPLIT)
                    if u == 12:
                        norm_heads(0)
                norm_heads(1)
                for m in range(2):
                    for t in range(T):
                        dve.wait_ge(oT_ev, 4 * l + 2 * m + t + 1)
                        rest_of(dve, [oT[:, i, m, :, t * P:(t + 1) * P] for i in (HEAD, REST)], blocks(bank[2 * m + t], 4), o_rest)
                for h in range(2):
                    rest(21 + 2 * h + SPLIT)
                    rest(22 + 2 * h + SPLIT)
                    for t in range(T):
                        ga, gb = proj[:, t, C_GA + h * W:C_GA + (h + 1) * W], proj[:, t, C_GB + h * W:C_GB + (h + 1) * W]
                        dve.wait_ge(y_mm, 4 * l + 2 * h + t + 1)
                        dve.tensor_tensor(ga, ga, bank[4 * (1 - h) + t][:, :], ALU.mult)
                        step(dve.tensor_tensor(gb, gb, bank[4 * (1 - h) + 2 + t][:, :], ALU.mult))
                        dve.tensor_tensor(ga, ga, gb, ALU.add).then_inc(merged, 1)
                for t in range(T):
                    for h in range(2):
                        dve.wait_ge(m_ev, 4 * l + 2 * t + h + 1)
                        rest_of(dve, [xT[:, i, 4 * h:4 * h + 4, t * P:(t + 1) * P] for i in (HEAD, REST)], blocks(bank[2 * t + h], 4), m_rest)
                for h in range(2):
                    if h == 0:
                        rest(25 + SPLIT)
                    for t in range(T):
                        dve.wait_ge(out_mm, 4 * l + 2 * h + t + 1)
                        step(dve.scalar_tensor_tensor(out=x[:, t, h * W:(h + 1) * W], in0=x[:, t, h * W:(h + 1) * W], scalar=ALPHA,
                                                      in1=bank[4 + 2 * h + t][:, :], op0=ALU.mult, op1=ALU.add))
                    if h == 0:
                        rest(26 + SPLIT)
                if l == 0:
                    layer_norm(0, x, [27 + SPLIT])
                    rest_x(1)
                    rest(28 + SPLIT)
                    dve_dense(dve, step)
                    layer_norm(1, x, [LAYER + SPLIT - 1])
                    rest_x(2)
                else:
                    layer_norm(2, x)
                    rest_x(3)
                    dve_experts(dve, step)
                    layer_norm(3, y)

        def product(pe, out_, act_, w, first, last):
            pe.matmul(out_, act_[REST], w[HEAD], start=first, stop=False)
            pe.matmul(out_, act_[HEAD], w[HEAD], start=False, stop=False)
            return pe.matmul(out_, act_[HEAD], w[REST], start=False, stop=last)

        def split_ready(pe, n):
            pe.wait_ge(rests_made, n + 1)

        def x_at(k, t):
            return [xT[:, i, k, t * P:(t + 1) * P] for i in (HEAD, REST)]

        def cols(w, k, c0=0, n=None):
            return [v[:, k, c0:(c0 + n if n else None)] for v in w]

        def pe_mixer(pe, l, tp, turn_x):
            base = T * NCH * l

            def unit(*u):
                n = number(u)
                split_ready(pe, n)
                return halves(n, *source(u)[1:])

            def chunk(c, half):
                n = CHUNKS[c][1]
                w = unit("in", l, c, half)
                for t in range(T):
                    k = T * c + t
                    if k >= 4 and half == 0:
                        pe.wait_ge(proj_ev, base + k - 3)
                    for i in range(4):
                        ins = product(pe, bank[k % 4][:, 0:n], x_at(4 * half + i, t), cols(w, i),
                                      half == 0 and i == 0, half == 1 and i == 3)
                    if half:
                        ins.then_inc(proj_mm, 1)
                if not half:
                    ins.then_inc(half_mm, 1)

            def dots(heads):
                for h in heads:
                    r = IDX_DIM * (h % 4)
                    rows = slice(r, r + IDX_DIM)
                    if h >= 4:
                        pe.wait_ge(relu_ev, IDX_HEADS * l + h - 3)
                    for t in range(T):
                        keys = (t + 1) * P
                        ins = pe.matmul(bank[4 + h % 4][:, t * P:t * P + keys], iT[rows, h // 4, t * P:(t + 1) * P],
                                        iT[rows, 2, 0:keys], start=True, stop=True)
                    ins.then_inc(dots_mm, 1)

            for c in range(6):
                chunk(c, 0)
                chunk(c, 1)
            for t in range(T):
                pe.wait_ge(idx_roped, T * l + t + 1)
                for i in range(2):
                    tp(bank[4 + t][:, i * P:(i + 1) * P], proj[:, t, C_IQ + i * P:C_IQ + (i + 1) * P])
                tp(bank[4 + t][:, 2 * P:3 * P], score[:, t, 0:P]).then_inc(idx_tr, 1)
            chunk(6, 0)
            chunk(6, 1)
            pe.wait_ge(idx_ev, T * (l + 1))
            dots(range(0, 4))
            chunk(7, 0)
            dots(range(4, 8))
            chunk(7, 1)
            pe.wait_ge(relu_ev, IDX_HEADS * (l + 1))
            for t in range(T):
                pe.wait_ge(lat_norm, T * l + t + 1)
                for k in range(5):
                    ins = tp(bank[4 + 2 * t + k // 4][:, (k % 4) * P:(k % 4 + 1) * P], proj[:, t, k * P:(k + 1) * P])
                ins.then_inc(c_tr, 1)
            chunk(8, 0)
            chunk(8, 1)
            pe.wait_ge(c_rest, T * (l + 1))

            def c_at(k, t):
                return [cT[:, i, k, t * P:(t + 1) * P] for i in (HEAD, REST)]

            for h in range(2):
                w = unit("uq", l, h)
                for t in range(T):
                    for i in range(3):
                        ins = product(pe, bank[4 + 2 * t + h][:, 0:384], c_at(i, t), cols(w, i), i == 0, i == 2)
                    ins.then_inc(uq_mm, 1)
            pe.wait_ge(proj_ev, base + T * NCH)
            w = unit("ukv", l)
            for t in range(T):
                for h in range(2):
                    for i in range(2):
                        ins = product(pe, bank[2 * t + h][:, :], c_at(3 + i, t), cols(w, i, h * W, W), i == 0, i == 1)
                    ins.then_inc(ukv_mm, 1)
            pe.wait_ge(dsa_roped, T * (l + 1))
            pe.wait_ge(ukv_ev, 4 * (l + 1))
            for i, c0 in enumerate((C_DQ, C_DK)):
                for t in range(T):
                    for k in range(4):
                        ins = tp(bank[2 * i + t][:, k * P:(k + 1) * P], proj[:, t, c0 + k * P:c0 + (k + 1) * P])
                    ins.then_inc(dsa_tr, 1)
            for t in range(T):
                pe.wait_ge(qm_roped, T * l + t + 1)
                for h in range(2):
                    for k in range(4):
                        ins = tp(bank[4 + 2 * t + h][0:QK, k * P:(k + 1) * P], qm[:, t, (4 * h + k) * QK:(4 * h + k + 1) * QK])
                    ins.then_inc(mq_tr, 1)
            pe.wait_ge(dsa_ev, 4 * (l + 1))
            for t in range(T):
                pe.wait_ge(kr_put, T * l + t + 1)
                for h in range(2):
                    for k in range(4):
                        ins = tp(bank[2 * t + h][0:QK, k * P:(k + 1) * P], km[:, t, (4 * h + k) * QK:(4 * h + k + 1) * QK])
                    ins.then_inc(mk_tr, 1)
            pe.wait_ge(mq_ev, 4 * (l + 1))
            pe.wait_ge(mk_ev, 4 * (l + 1))

            def qk(u):
                h = u % 8
                if u >= 2:
                    pe.wait_ge(row_max, 16 * l + u - 1)
                for t in range(T):
                    keys = (t + 1) * P
                    if u < 8:
                        q, kk = qTm[:, h, t * P:(t + 1) * P], kTm[:, h, 0:keys]
                    else:
                        rows = slice(DH * (h % 2), DH * (h % 2) + DH)
                        q, kk = qTd[rows, h // 2, t * P:(t + 1) * P], kTd[rows, h // 2, 0:keys]
                    ins = pe.matmul(bank[u % 2][:, t * P:t * P + keys], q, kk, start=True, stop=True)
                ins.then_inc(qk_mm, 1)

            def turn_probs(u):
                pe.wait_ge(probs, 16 * l + u + 1)
                if u >= 2:
                    pe.wait_ge(p_ev, 16 * l + u - 1)
                for i in range(3):
                    ins = tp(bank[2 + u % 2][:, i * P:(i + 1) * P], sm[:, u % NSM, i * P:(i + 1) * P])
                ins.then_inc(p_tr, 1)

            def pv(u):
                h, m = u % 8, u // 8
                pe.wait_ge(p_ev, 16 * l + u + 1)

                def v(t):
                    if m == 0:
                        return vm[:, t, h * VDIM:(h + 1) * VDIM]
                    return proj[:, t, C_DV + h * DH:C_DV + (h + 1) * DH]

                at = slice(h * VDIM, (h + 1) * VDIM)
                pe.matmul(bank[4 + 2 * m][:, at], pT[:, u % NPT, 0:P], v(0), start=True, stop=True)
                pe.matmul(bank[5 + 2 * m][:, at], pT[:, u % NPT, P:2 * P], v(0), start=True, stop=False)
                pe.matmul(bank[5 + 2 * m][:, at], pT[:, u % NPT, 2 * P:3 * P], v(1), start=False, stop=True).then_inc(pv_mm, 1)

            for i in range(16 + 3):
                if i < 16:
                    qk(i)
                if 2 <= i < 18:
                    turn_probs(i - 2)
                if i >= 3:
                    pv(i - 3)
            pe.wait_ge(row_max, 16 * (l + 1))
            for m in range(2):
                for t in range(T):
                    pe.wait_ge(o_ev, 4 * l + 2 * m + t + 1)
                    for k in range(4):
                        ins = tp(bank[2 * m + t][:, k * P:(k + 1) * P], o_tok[m][t][:, k * P:(k + 1) * P])
                    ins.then_inc(o_tr, 1)
            pe.wait_ge(o_rest, 4 * (l + 1))
            for h in range(2):
                for m, name in enumerate(("oa", "ob")):
                    w = unit(name, l, h)
                    for t in range(T):
                        for i in range(4):
                            ins = product(pe, bank[4 * (1 - h) + 2 * m + t][:, :], [oT[:, s_, m, i, t * P:(t + 1) * P] for s_ in (HEAD, REST)],
                                          cols(w, i), i == 0, i == 3)
                        if m:
                            ins.then_inc(y_mm, 1)
                    if m == 0:
                        ins.then_inc(ya_mm, 1)
            pe.wait_ge(merged, 4 * (l + 1))
            turn_x(m_tr, lambda t, i: proj[:, t, C_GA + i * P:C_GA + (i + 1) * P])
            pe.wait_ge(m_rest, 4 * (l + 1))
            for h in range(2):
                for half in range(2):
                    w = unit("out", l, h, half)
                    for t in range(T):
                        for i in range(4):
                            ins = product(pe, bank[4 + 2 * h + t][:, :], x_at(4 * half + i, t), cols(w, i),
                                          half == 0 and i == 0, half == 1 and i == 3)
                        if half:
                            ins.then_inc(out_mm, 1)
                    if not half:
                        ins.then_inc(half_mm, 1)

        def pe_dense(pe, tp):
            def turn(g):
                for t in range(T):
                    pe.wait_ge(hid_ev, T * g + t + 1)
                    for i in range(DENSE[g][1] // P):
                        ins = tp(bank[2 * t][:, i * P:(i + 1) * P], hid[:, t, i * P:(i + 1) * P])
                    ins.then_inc(h_tr, 1)

            for m, (kind, g, half) in enumerate(ffn_units(DG)):
                n = MIXER + m
                split_ready(pe, n)
                w = halves(n, *source(STREAM[n])[1:])
                n_hid = DENSE[g][1]
                if kind == "w2":
                    pe.wait_ge(h_rest, T * (g + 1))
                    for t in range(T):
                        for i in range(n_hid // P):
                            ins = product(pe, bank[4 + 2 * t + half][:, :], [hT[:, s_, i, t * P:(t + 1) * P] for s_ in (HEAD, REST)],
                                          cols(w, i), g == 0 and i == 0, g == DG - 1 and i == n_hid // P - 1)
                    ins.then_inc(w2_mm, 1)
                    if half == 1 and g + 1 < DG:
                        turn(g + 1)
                else:
                    full, first_half, b = (w1_mm, w1_half, 0) if kind == "w1" else (w3_mm, w3_half, 1)
                    for t in range(T):
                        if g and kind == "w1" and half == 0:
                            pe.wait_ge(h_rest, T * (g - 1) + t + 1)
                        for i in range(4):
                            ins = product(pe, bank[2 * t + b][:, 0:n_hid], x_at(4 * half + i, t), cols(w, i),
                                          half == 0 and i == 0, half == 1 and i == 3)
                        if half:
                            ins.then_inc(full, 1)
                    if not half:
                        ins.then_inc(first_half, 1)
                    if (kind, g, half) == ("w3", 0, 1):
                        turn(0)

        def pe_experts(pe, tp):
            pe.wait_ge(wr_ready, 2)
            w = [wrs[:, i, :].rearrange("p (k e) -> p k e", k=KD) for i in (HEAD, REST)]
            for t in range(T):
                for i in range(KD):
                    ins = product(pe, bank[6 + t][:, 0:EXPERTS], x_at(i, t), cols(w, i), i == 0, i == KD - 1)
                ins.then_inc(route_mm, 1)
            pe.wait_ge(chosen, 1)
            b = bank[6]
            E = EXPERTS
            pe.matmul(b[:, 0:E], before[:, :], r_sel[:, 0, :], start=True, stop=True)
            pe.matmul(b[:, E:2 * E], ones[:, :], r_sel[:, 0, :], start=True, stop=False)
            pe.matmul(b[:, E:2 * E], before[:, :], r_sel[:, 1, :], start=False, stop=True)
            pe.matmul(b[:, 2 * E:3 * E], ones[:, :], r_sel[:, 0, :], start=True, stop=False)
            pe.matmul(b[:, 2 * E:3 * E], ones[:, :], r_sel[:, 1, :], start=False, stop=True).then_inc(pos_mm, 1)
            pe.wait_ge(routed, 1)

            def job(j):
                g0 = T * DG
                pe.wait_ge(pick_put, j + 1)
                pe.wait_ge(h_rest, NG * j + g0)
                pe.wait_ge(comb_ev, j + CREDIT)
                for h in range(2):
                    for i in range(4):
                        for t in range(T):
                            ins = pe.matmul(bank[6 + h][:, i * P:(i + 1) * P], x[:, t, (4 * h + i) * P:(4 * h + i + 1) * P],
                                            pick[:, t, :], start=(t == 0), stop=(t == T - 1))
                    ins.then_inc(gat_mm, 1)
                pe.wait_ge(gat_rest, 2 * j + 2)

                def turn(g):
                    pe.wait_ge(hid_ev, NG * j + (g0 + g + 1))
                    pe.wait_ge(h_rest, NG * j + (g0 + g))
                    for i in range(4):
                        ins = tp(bank[6][:, i * P:(i + 1) * P], hid[:, g % 2, i * P:(i + 1) * P])
                    ins.then_inc(h_tr, 1)

                for m, (kind, g, half) in enumerate(JOB):
                    n = FIRST + m
                    w = halves(n, 4, W)
                    if kind == "w2":
                        if half == 0:
                            pe.wait_ge(h_rest, NG * j + (g0 + g + 1))
                            if g == 0:
                                pe.wait_ge(oe_ev, 2 * j + CREDIT)
                    elif half == 0:
                        if g < 2:
                            pe.wait_ge(y_add, 4 * j + CREDIT)
                        else:
                            pe.wait_ge(hid_ev, NG * j + (g0 + g - 1))
                    pe.wait_ge(rests_made, PER_JOB * j + (n + 1))
                    if kind == "w2":
                        for i in range(4):
                            ins = product(pe, bank[4 + half][:, :], [hT[:, s_, i, 0:CAP] for s_ in (HEAD, REST)], cols(w, i),
                                          g == 0 and i == 0, g == NG - 1 and i == 3)
                        ins.then_inc(w2_mm, 1)
                    else:
                        full, first_half, b1 = (w1_mm, w1_half, 0) if kind == "w1" else (w3_mm, w3_half, 1)
                        for i in range(4):
                            ins = product(pe, bank[2 * (g % 2) + b1][:, :], [xeT[:, s_, 4 * half + i, :] for s_ in (HEAD, REST)],
                                          cols(w, i), half == 0 and i == 0, half == 1 and i == 3)
                        ins.then_inc(full if half else first_half, 1)
                    if (kind, half) == ("w1", 1) and g:
                        turn(g - 1)
                    if (kind, g, half) == ("w2", 1, 1):
                        pe.wait_ge(comb_put, j + (1 + CREDIT))
                        for t in range(T):
                            ins = tp(bank[7][:, t * P:(t + 1) * P], comb_at[:, t, :])
                        ins.then_inc(comb_tr, 1)
                    if (kind, g, half) == ("w2", NG - 2, 1):
                        turn(NG - 1)
                pe.wait_ge(comb_ev, j + (1 + CREDIT))
                for h in range(2):
                    pe.wait_ge(oe_ev, 2 * j + (h + 1 + CREDIT))
                    for t in range(T):
                        pe.matmul(bank[2 * t + h][:, :], combT[:, t * P:(t + 1) * P], oe[:, h * W:(h + 1) * W],
                                  start=True, stop=True).then_inc(sc_mm, 1)

            for ready in (gat_mm, comb_tr, sc_mm):
                pe.sem_inc(ready, CREDIT)
            with pe.Fori(0, EXPERTS) as e:
                job(e)
            crowded_experts(pe, lambda j, e: job(j))

        @block.tensor
        def _(pe):
            def tp(dst, src):
                return pe.transpose(dst, src, ident[:, :])

            def turn_x(k, src):
                for t in range(T):
                    for h in range(2):
                        for i in range(4):
                            ins = tp(bank[2 * t + h][:, i * P:(i + 1) * P], src(t, 4 * h + i))
                        ins.then_inc(k, 1)

            def x_block(t, i):
                return x[:, t, i * P:(i + 1) * P]

            pe.wait_ge(consts, 1)
            pe.wait_ge(x_in, 16)
            turn_x(x_tr, x_block)
            pe.wait_ge(x_rest, 4)
            for l in range(DEPTH):
                pe_mixer(pe, l, tp, turn_x)
                pe.wait_ge(ln_done, 2 * l + 1)
                turn_x(x_tr, x_block)
                pe.wait_ge(x_rest, 4 * (2 * l + 2))
                if l == 0:
                    pe_dense(pe, tp)
                    pe.wait_ge(ln_done, 2)
                    turn_x(x_tr, x_block)
                    pe.wait_ge(x_rest, 12)
                else:
                    pe_experts(pe, tp)


_INS = ["x", "positions", "w_in", "mla_q_norm", "w_uq", "mla_kv_norm", "w_ukv", "w_o_mla", "w_o_dsa", "w_out",
        "ln1_g", "ln1_b", "ln2_g", "ln2_b", "dense_w1", "dense_w3", "dense_w2", "moe_router", "moe_w1", "moe_w3", "moe_w2"]


def kernel(**inputs):
    import numpy as np
    import concourse.bacc as bacc
    from concourse.bass_utils import run_bass_kernel_spmd

    nc = bacc.Bacc("TRN2", target_bir_lowering=False, num_devices=1, dynamic_dma_scratch_size=1024)
    arrays, a = {}, {}
    freq = [np.power(np.float32(THETA), -np.arange(0, d, 2, dtype=np.float32) / np.float32(d)) for d in (ROPE, DH)]
    given = {name: np.ascontiguousarray(inputs[name]) for name in _INS}
    given["inv_freq"] = np.concatenate(freq).astype(np.float32)[None, :]
    for name, v in given.items():
        arrays[name + "_dram"] = v
        a[name] = nc.dram_tensor(name + "_dram", v.shape, mybir.dt.from_np(v.dtype), kind="ExternalInput").ap()
    out = nc.dram_tensor("out_dram", (1, SEQ, D), F32, kind="ExternalOutput").ap()
    build(nc, a, out)
    r = run_bass_kernel_spmd(nc, [arrays], core_ids=[0])
    return r.results[0]["out_dram"]
```

```python
from contextlib import ExitStack

import concourse.bass as bass
from concourse import mybir

ALU = mybir.AluOpType
ACT = mybir.ActivationFunctionType
F32 = mybir.dt.float32
F32R = mybir.dt.float32r
I32 = mybir.dt.int32
AX_X = mybir.AxisListType.X

P = 128
D = 1024
SEQ = 256
T = SEQ // P
DEPTH = 2
KD = D // P
HEADS = 8
NOPE, ROPE, VDIM = 64, 32, 64
QK = NOPE + ROPE
Q_LORA, KV_LORA = 384, 256
DH = 64
IDX_HEADS, IDX_DIM = 8, 32
N_SEL = min(256, SEQ // 4)
D_FF = 2816
EXPERTS = 8
D_FFE = 3584
EPS = 1e-5
ALPHA = (2 * DEPTH) ** 0.25
THETA = 10000.0

C_Q = 0
C_KV = C_Q + Q_LORA
C_KR = C_KV + KV_LORA
C_DQ = C_KR + ROPE
C_DK = C_DQ + HEADS * DH
C_DV = C_DK + HEADS * DH
C_IQ = C_DV + HEADS * DH
C_IK = C_IQ + IDX_HEADS * IDX_DIM
C_IW = C_IK + IDX_DIM
C_GA = C_IW + IDX_HEADS
C_GB = C_GA + D
D_IN = C_GB + D

W = 512
STARTS = sorted(range(0, D_IN, W), key=lambda c: not c <= C_IQ < c + W)
CHUNKS = [(c, min(W, D_IN - c)) for c in STARTS]
NCH = len(CHUNKS)
assert STARTS[0] + W >= C_GA


def chunks_to(col):
    return 1 + sum(c < col for c in STARTS[1:])


DENSE = [(0, D_FF % W)] + [(c, W) for c in range(D_FF % W, D_FF, W)]
NG = D_FFE // W
CAP = P
MASKED = -1e30
TAKEN = -3e38
FLOOR = -3.2e38
SCATTER = ((2, 3), (1, 4))
CREDIT = 1
UNUSED = 3e38
ROUND = 1.5 * 2 ** 23
TWO_PI = 6.283185307179586
HALF_PI = TWO_PI / 4
PI_F = 3.1415925
RQ = ROPE // 2
RD = DH // 2
NF = RQ + RD

UNIT = 4 * W
RAW = 7
SPLIT = 3
HEAD, REST = 0, 1
DG = len(DENSE)
PER_DENSE = 6 * DG


def ffn_units(groups):
    units = []
    for g in range(groups):
        units += [("w1", g, 0), ("w1", g, 1), ("w3", g, 0), ("w3", g, 1)]
        if g:
            units += [("w2", g - 1, 0), ("w2", g - 1, 1)]
    return units + [("w2", groups - 1, 0), ("w2", groups - 1, 1)]


def mixer_units(l):
    return ([("in", l, c, k) for c in range(NCH) for k in range(2)] + [("uq", l, 0), ("uq", l, 1), ("ukv", l)]
            + [(w, l, h) for h in range(2) for w in ("oa", "ob")] + [("out", l, h, k) for k in range(2) for h in range(2)])


MIXER = len(mixer_units(0))
LAYER = MIXER + PER_DENSE
STREAM = mixer_units(0) + ffn_units(DG) + mixer_units(1)
JOB = ffn_units(NG)
FIRST = len(STREAM)
PER_JOB = len(JOB)
HALVES = NCH + 2
EARLY = [FIRST + SPLIT - 1 + RAW + i for i in range(6)]
assert PER_JOB % RAW == 0 and PER_JOB % SPLIT == 0 and len(ffn_units(DG)) == PER_DENSE


def split_2pi():
    import numpy as np

    def short(v):
        return float((np.float32(v).view(np.uint32) & np.uint32(0xFFFFC000)).view(np.float32))

    hi = short(TWO_PI)
    mid = short(TWO_PI - hi)
    return hi, mid, TWO_PI - hi - mid


def build(nc, a, out):
    ctx = ExitStack()
    with ctx:
        def sb(name, shape, dt=F32):
            return ctx.enter_context(nc.sbuf_tensor(name, shape, dt))

        def sem(name):
            return ctx.enter_context(nc.semaphore(name))

        where = [(nc.sbuf_base + 63) // 64 * 64]

        def region(size):
            where[0] += size
            return where[0] - size

        def put(name, shape, at, dt=F32):
            return nc.alloc_sbuf_tensor_at(name, shape, dt, offset=at)

        def fixed(name, shape, dt=F32):
            size = 4
            for n in shape[1:]:
                size *= n
            return put(name, shape, region((size + 31) // 32 * 32), dt)

        raw = fixed("raw", [P, RAW, UNIT])
        split = fixed("split", [P, SPLIT, 2, UNIT], F32R)
        x = fixed("x", [P, T, D])
        r_xT = region(2 * KD * SEQ * 4)
        xT = put("xT", [P, 2, KD, SEQ], r_xT, F32R)
        qm = put("qm", [P, T, HEADS * QK], r_xT)
        r_proj = region(T * D_IN * 4)
        proj = put("proj", [P, T, D_IN], r_proj)
        r_att = region((2 * 5 * SEQ + 2 * W) * 4)
        cT = put("cT", [P, 2, 5, SEQ], r_att, F32R)
        ropeA = put("ropeA", [P, W], r_att + 2 * 5 * SEQ * 4)
        ropeB = put("ropeB", [P, W], r_att + (2 * 5 * SEQ + W) * 4)
        NSM, NPT = 4, 3
        sm = put("sm", [P, NSM, 384], r_att)
        pT = put("pT", [P, NPT, 384], r_att + NSM * 384 * 4)
        junk = put("junk", [P, Q_LORA], r_att)
        trig = put("trig", [P, T, 2 * NF], r_att + 4096)
        turns = put("turns", [P, T, 2 * NF], r_att + 5120)
        invf = put("invf", [P, NF], r_att + 6144)
        posi = put("posi", [P, T], r_att + 6400, I32)
        posf = put("posf", [P, T], r_att + 6432)
        r_km = region(T * HEADS * QK * 4)
        km = put("km", [P, T, HEADS * QK], r_km)
        r_vm = region(T * HEADS * VDIM * 4)
        vm = put("vm", [P, T, HEADS * VDIM], r_vm)
        r_qT = region(HEADS * SEQ * 4)
        r_kT = region(HEADS * SEQ * 4)
        qTm = put("qTm", [QK, HEADS, SEQ], r_qT)
        kTm = put("kTm", [QK, HEADS, SEQ], r_kT)
        oT = put("oT", [P, 2, 2, 4, SEQ], r_qT, F32R)
        relu = put("relu", [P, 4, 384], r_kT)
        lnp = put("lnp", [P, 2, D], r_kT)
        r_dT = region(2 * 4 * SEQ * 4)
        early = [put(f"early{i}", [P, UNIT], at) for i, at in enumerate(
            (r_att, r_qT, r_dT, r_proj + 24576, r_xT, r_xT + UNIT * 4))]
        dT = put("dT", [P, 2, 4, SEQ], r_dT)
        qTd, kTd = dT[:, 0], dT[:, 1]
        iT = dT[:, 0, 0:3, :]
        causal = fixed("causal", [P, T, SEQ])
        select = fixed("select", [P, T, SEQ])
        score = fixed("score", [P, T, SEQ])
        o_tok = [[proj[:, t, C_DQ + m * W:C_DQ + (m + 1) * W] for t in range(T)] for m in range(2)]

        silu = put("silu", [P, T, W], r_proj)
        hid = put("hid", [P, T, W], r_proj + 4096)
        hT = put("hT", [P, 2, 4, SEQ], r_proj + 8192, F32R)
        xeT = put("xeT", [P, 2, KD, CAP], r_proj + 16384, F32R)
        y = put("y", [P, T, D], r_proj + 24576)
        hT_odd = put("hT_odd", [P, 2, 4, SEQ], r_proj + 16384, F32R)
        oe = put("oe", [P, D], r_dT)
        pick = put("pick", [P, T, CAP], r_km)
        comb_at = put("comb_at", [P, T, CAP], r_km + 1024)
        combT = put("combT", [P, SEQ], r_km + 2048)
        slot_no = put("slot_no", [P, 2 * CAP], r_km + 3072)
        before = put("before", [P, P], r_km + 4096)
        ones = put("ones", [P, P], r_km + 4608)
        wr = put("wr", [P, KD * EXPERTS], r_km + 5120)
        wrs = put("wrs", [P, 2, KD * EXPERTS], r_km + 5376, F32R)
        logitsT = put("logitsT", [EXPERTS, SEQ], r_vm + 1024)
        small = put("small", [P, 192], r_vm)
        rt = small[:, 0:160].rearrange("p (t n) -> p t n", t=T)
        r_list, r_top, r_keys = rt[:, :, 0:16], rt[:, :, 16:24], rt[:, :, 24:32]
        r_sel, r_exp, r_comb, r_pos = (rt[:, :, 32 + 8 * i:40 + 8 * i] for i in range(4))
        r_one = rt[:, :, 72:76]
        cur = small[:, 160:164]

        ident = fixed("ident", [P, P])
        rope32 = fixed("rope32", [P, T, 2, ROPE])
        rope64 = fixed("rope64", [P, T, 2, DH])
        gcol = fixed("gcol", [P, DEPTH, 5])
        expo = fixed("expo", [P, 1])
        stat = fixed("stat", [P, T, 2, 6])
        mv = fixed("mv", [P, T, 2])
        rstd = fixed("rstd", [P, T, 2])
        rms = fixed("rms", [P, T, 4])
        top8 = fixed("top8", [P, T, 8])
        mx = fixed("mx", [P, 16, T])
        den = fixed("den", [P, 16, T])
        rden = fixed("rden", [P, T, HEADS])
        flags = fixed("flags", [1, 64])
        jobs = fixed("jobs", [1, 32], I32)
        assert where[0] <= nc.sbuf_usable_end

        bank = [ctx.enter_context(nc.psum_tensor(f"bank{i}", [P, W], F32)) for i in range(8)]

        landed = [sem(f"landed{i}") for i in range(RAW)]
        landed_early = [sem(f"landed_early{i}") for i in range(len(EARLY))]
        heads_made, rests_made = sem("unit_heads_made"), sem("unit_rests_made")
        x_in, small_in, router_in, lnp_in, out_done = (sem(n) for n in ("x_in", "small_in", "router_in", "lnp_in", "out_done"))
        half_mm, w2_tile, ya_mm, w1_half, w3_half = (sem(n) for n in ("first_halves_mm", "w2_first_tile_mm", "mla_branch_mm", "w1_first_half_mm", "w3_first_half_mm"))
        c_rest, o_rest, m_rest, x_rest, h_rest, gat_rest, wr_ready = (
            sem(n) for n in ("latents_rest", "heads_rest", "merged_rest", "x_rest", "hidden_rest", "gathered_rest", "router_split"))
        consts = sem("consts_ready")
        sin_in, trig_done, tables = sem("sin_in_ready"), sem("trig_done"), sem("rope_tables_ready")
        proj_mm, proj_ev = sem("proj_mm"), sem("proj_evacuated")
        idx_roped, dsa_roped, qm_roped = (sem(n) for n in ("idx_roped", "dsa_roped", "qm_roped"))
        idx_tr, idx_ev, dots_mm, relu_ev, scored, selected = (
            sem(n) for n in ("idx_turned", "idx_evacuated", "dots_mm", "relu_ready", "head_scored", "keys_selected"))
        sq_done, ms_ready, rms_ready, lat_norm, c_tr, c_ev = (
            sem(n) for n in ("squares_summed", "mean_square_ready", "rms_ready", "latents_normed", "latents_turned", "latents_evacuated"))
        uq_mm, uq_ev, ukv_mm, ukv_ev, kr_put = (sem(n) for n in ("uq_mm", "uq_evacuated", "ukv_mm", "ukv_evacuated", "key_rope_placed"))
        dsa_tr, dsa_ev, mq_tr, mq_ev, mk_tr, mk_ev = (
            sem(n) for n in ("dsa_turned", "dsa_evacuated", "mla_q_turned", "mla_q_evacuated", "mla_k_turned", "mla_k_evacuated"))
        qk_mm, row_max, probs, p_tr, p_ev, pv_mm, o_ev = (
            sem(n) for n in ("qk_mm", "row_max_ready", "probs_ready", "probs_turned", "probs_evacuated", "pv_mm", "heads_normed"))
        o_tr, oT_ev, y_mm, merged, m_tr, m_ev, out_mm = (
            sem(n) for n in ("heads_turned", "heads_evacuated", "branches_mm", "merged", "merged_turned", "merged_evacuated", "out_mm"))
        ln_var, ln_rstd, ln_done, x_tr, x_ev = (sem(n) for n in ("ln_variance", "ln_rstd", "ln_done", "x_turned", "x_evacuated"))
        w1_mm, w3_mm, silu_ev, hid_ev, h_tr, h_ev, w2_mm = (
            sem(n) for n in ("w1_mm", "w3_mm", "silu_ready", "hidden_ready", "hidden_turned", "hidden_evacuated", "w2_mm"))
        route_mm, logits_ev, logits_tr, chosen, exp_done, pos_mm, placed, routed = (
            sem(n) for n in ("router_mm", "logits_evacuated", "logits_turned", "experts_chosen", "router_exp_done", "positions_mm", "places_ready", "routed"))
        slot_ids, cur_put, pick_put, comb_put = (sem(n) for n in ("slot_ids_ready", "expert_column_ready", "pick_ready", "combine_ready"))
        gat_mm, gat_ev, comb_tr, comb_ev, oe_ev, sc_mm, y_add = (
            sem(n) for n in ("gather_mm", "gather_evacuated", "combine_turned", "combine_evacuated", "expert_out_ready", "scatter_mm", "y_added"))
        pool_passed = sem("pool_passed_wait")
        dve_step, act_step, pool_step = sem("dve_step"), sem("act_step"), sem("pool_step")

        def number(unit):
            return STREAM.index(unit)

        def used_up(unit):
            kind = unit[0]
            if kind in ("w1", "w3"):
                full, half = (w1_mm, w1_half) if kind == "w1" else (w3_mm, w3_half)
                return (full, T * (unit[1] + 1)) if unit[2] else (half, unit[1] + 1)
            if kind == "w2":
                return w2_mm, 2 * unit[1] + unit[2] + 1
            l = unit[1]
            if kind == "in":
                return (proj_mm, T * NCH * l + T * (unit[2] + 1)) if unit[3] else (half_mm, HALVES * l + unit[2] + 1)
            if kind == "out":
                return (out_mm, 4 * l + 2 * (unit[2] + 1)) if unit[3] else (half_mm, HALVES * l + NCH + unit[2] + 1)
            if kind == "uq":
                return uq_mm, 4 * l + 2 * (unit[2] + 1)
            if kind == "ukv":
                return ukv_mm, 4 * (l + 1)
            return (ya_mm, 2 * l + unit[2] + 1) if kind == "oa" else (y_mm, 4 * l + 2 * (unit[2] + 1))

        def job_used_up(j, m):
            kind, g, half = JOB[m]
            past = 0 if m >= 0 else NG
            if kind == "w2":
                return w2_mm, 2 * NG * j + (2 * (DG - past) + 2 * g + half + 1)
            if half:
                return (w1_mm if kind == "w1" else w3_mm), NG * j + (T * DG - past + g + 1)
            return (w1_half if kind == "w1" else w3_half), NG * j + (DG - past + g + 1)

        def by_k(w, c, n, k0, k):
            return w[k0 * P:(k0 + k) * P, c:c + n].rearrange("(k p) n -> p k n", p=P)

        def source(unit):
            kind = unit[0]
            if kind == "in":
                c, n = CHUNKS[unit[2]]
                return by_k(a["w_in"][unit[1]], c, n, 4 * unit[3], 4), 4, n
            if kind == "out":
                return by_k(a["w_out"][unit[1]], unit[2] * W, W, 4 * unit[3], 4), 4, W
            if kind == "uq":
                return by_k(a["w_uq"][unit[1]], unit[2] * 384, 384, 0, 3), 3, 384
            if kind == "ukv":
                return by_k(a["w_ukv"][unit[1]], 0, 2 * W, 0, 2), 2, 2 * W
            if kind in ("oa", "ob"):
                return by_k(a[{"oa": "w_o_mla", "ob": "w_o_dsa"}[kind]][unit[1]], unit[2] * W, W, 0, 4), 4, W
            c, n = DENSE[unit[1]]
            if kind == "w2":
                return by_k(a["dense_w2"][0], unit[2] * W, W, c // P, n // P), n // P, W
            return by_k(a["dense_" + kind][0], c, n, 4 * unit[2], 4), 4, n

        def shape_of(n):
            return source(STREAM[n])[1:] if n < FIRST else (4, W)

        def as_weights(view, k, n):
            return view[:, 0:k * n].rearrange("p (k n) -> p k n", k=k)

        def is_early(n, j):
            return type(j) is int and n in EARLY

        def ring_turn(n, j):
            return n if type(j) is int and n < EARLY[0] else n - len(EARLY)

        def landing(n, j):
            return early[EARLY.index(n)] if is_early(n, j) else raw[:, ring_turn(n, j) % RAW, :]

        def slot_before(n, j):
            before_ = ring_turn(n, j) - RAW
            return before_ if type(j) is int and before_ < EARLY[0] else before_ + len(EARLY)

        def halves(n, k, cols):
            return [as_weights(split[:, n % SPLIT, i, :], k, cols) for i in (HEAD, REST)]

        def make_head(act, n):
            k, cols = shape_of(n)
            act.wait_ge(landed[n % RAW], 16 * (n // RAW + 1))
            if n >= SPLIT:
                act.wait_ge(*used_up(STREAM[n - SPLIT]))
            act.copy(split[:, n % SPLIT, HEAD, 0:k * cols], raw[:, n % RAW, 0:k * cols]).then_inc(heads_made, 1)

        def make_rest(dve, n):
            k, cols = shape_of(n)
            dve.wait_ge(heads_made, n + 1)
            dve.tensor_tensor(split[:, n % SPLIT, REST, 0:k * cols], raw[:, n % RAW, 0:k * cols],
                              split[:, n % SPLIT, HEAD, 0:k * cols].bitcast(F32), ALU.subtract).then_inc(rests_made, 1)

        def job_head(act, j, m):
            n = FIRST + m
            if is_early(n, j):
                act.wait_ge(landed_early[EARLY.index(n)], 16)
            else:
                r = ring_turn(n, j)
                act.wait_ge(landed[r % RAW], j * (16 * PER_JOB // RAW) + 16 * (r // RAW + 1))
            act.wait_ge(*job_used_up(j, m - SPLIT))
            act.copy(split[:, n % SPLIT, HEAD, :], landing(n, j)[:, :]).then_inc(heads_made, 1)

        def job_rest(dve, j, m):
            n = FIRST + m
            dve.wait_ge(heads_made, PER_JOB * j + (n + 1))
            dve.tensor_tensor(split[:, n % SPLIT, REST, :], landing(n, j)[:, :],
                              split[:, n % SPLIT, HEAD, :].bitcast(F32), ALU.subtract).then_inc(rests_made, 1)

        block = ctx.enter_context(nc.Block())

        def crowded_experts(eng, body):
            eng.wait_ge(routed, 1)
            many = eng.value_load(jobs[0:1, 2 * EXPERTS:2 * EXPERTS + 1], min_val=0, max_val=4)
            with eng.If(many > 0):
                with eng.Fori(0, EXPERTS) as e:
                    crowded = eng.value_load(jobs[0:1, bass.ds(e, 1)], min_val=0, max_val=1)
                    with eng.If(crowded > 0):
                        rank = eng.value_load(jobs[0:1, bass.ds(e + EXPERTS, 1)], min_val=0, max_val=4)
                        body(rank + EXPERTS, e)
            return many

        def all_jobs(eng, job):
            job(0, True)
            with eng.Fori(1, EXPERTS) as e:
                job(e, False)
            return crowded_experts(eng, lambda j, e: job(j, False))

        @block.sync
        def _(sp):
            sp.dma_start(x[:, :, :], a["x"][0].rearrange("(t p) d -> p t d", p=P)).then_inc(x_in, 16)
            for n, unit in enumerate(STREAM):
                if n >= RAW:
                    sp.wait_ge(rests_made, n - RAW + 1)
                src, k, cols = source(unit)
                sp.dma_start(as_weights(raw[:, n % RAW, :], k, cols), src).then_inc(landed[n % RAW], 16)

            last_use = [(y_mm, 4 * DEPTH)] * 3 + [(m_tr, 4 * DEPTH)] + [(route_mm, 1)] * 2

            def expert_stream(j, e):
                for m, (kind, g, half) in enumerate(JOB):
                    n = FIRST + m
                    w = a["moe_" + kind][0][e]
                    src = by_k(w, half * W, W, 4 * g, 4) if kind == "w2" else by_k(w, g * W, W, 4 * half, 4)
                    if is_early(n, j):
                        sp.wait_ge(*last_use[EARLY.index(n)])
                        done = landed_early[EARLY.index(n)]
                    else:
                        sp.wait_ge(rests_made, PER_JOB * j + (slot_before(n, j) + 1))
                        done = landed[ring_turn(n, j) % RAW]
                    sp.dma_start(as_weights(landing(n, j), 4, W), src).then_inc(done, 16)

            expert_stream(0, 0)
            with sp.Fori(1, EXPERTS) as e:
                expert_stream(e, e)

            crowded_experts(sp, expert_stream)
            for t in range(T):
                sp.wait_ge(ln_done, T * (2 * DEPTH - 1) + t + 1)
                sp.dma_start(out[0, t * P:(t + 1) * P, :], x[:, t, :]).then_inc(out_done, 16)
            sp.wait_ge(out_done, T * 16)


        def slot_constants(pool):
            pool.wait_ge(merged, 4 * DEPTH)
            pool.memset(r_list[:, :, EXPERTS:16], UNUSED).then_inc(slot_ids, 1)
            pool.memset(ones[:, :], 1.0).then_inc(slot_ids, 1)
            pool.wait_ge(slot_ids, 2)
            pool.affine_select(out=before[:, :], in_=ones[:, :], compare_op=ALU.is_gt, fill=0.0,
                               base=0, pattern=[[1, P]], channel_multiplier=-1).then_inc(slot_ids, 1)
            pool.iota(slot_no[:, :], pattern=[[1, 2 * CAP]], base=0, channel_multiplier=0,
                      allow_small_or_imprecise_dtypes=True).then_inc(slot_ids, 1)
            pool.wait_ge(slot_ids, 4)

        def pool_experts(pool):
            pool.wait_ge(placed, 1)

            def one_hots(j, e, half):
                ids = slot_no[:, half * CAP:(half + 1) * CAP]
                pool.wait_ge(comb_put, j + CREDIT)
                pool.tensor_copy(cur[:, 0:2], r_pos[:, :, bass.ds(e, 1)].rearrange("p t n -> p (t n)"))
                pool.tensor_copy(cur[:, 2:4], r_comb[:, :, bass.ds(e, 1)].rearrange("p t n -> p (t n)")).then_inc(cur_put, 1)
                pool.wait_ge(cur_put, j + 1)
                pool.wait_ge(gat_mm, 2 * j + CREDIT)
                pool.sem_inc(pool_passed, 1)
                for t in range(T):
                    ins = pool.tensor_scalar(pick[:, t, :], ids, cur[:, t:t + 1], None, ALU.is_equal)
                ins.then_inc(pick_put, 1)
                pool.wait_ge(pick_put, j + 1)
                pool.wait_ge(comb_tr, j + CREDIT)
                for t in range(T):
                    ins = pool.tensor_tensor(comb_at[:, t, :], pick[:, t, :], cur[:, 2 + t:3 + t].to_broadcast([P, CAP]), ALU.mult)
                ins.then_inc(comb_put, 1)

            pool.sem_inc(comb_put, CREDIT)
            with pool.Fori(0, EXPERTS) as e:
                one_hots(e, e, 0)
            crowded_experts(pool, lambda j, e: one_hots(j, e, 1))

        @block.gpsimd
        def _(pool):
            n = [0]

            def step(ins):
                n[0] += 1
                ins.then_inc(pool_step, 1)
                pool.wait_ge(pool_step, n[0])

            step(pool.memset(ident[:, :], 0.0))
            step(pool.memset(causal[:, :, :], 0.0))
            step(pool.memset(expo[:, :], -0.5))
            step(pool.affine_select(out=ident[:, :], in_=ident[:, :], compare_op=ALU.not_equal, fill=1.0,
                                    base=0, pattern=[[-1, P]], channel_multiplier=1))
            for t in range(T):
                step(pool.affine_select(out=causal[:, t, :], in_=causal[:, t, :], compare_op=ALU.is_ge, fill=MASKED,
                                        base=t * P, pattern=[[-1, SEQ]], channel_multiplier=1))
            pool.sem_inc(consts, 1)

            for l in range(DEPTH):
                for t in range(T):
                    k = T * l + t + 1
                    pool.wait_ge(ms_ready, k)
                    pool.tensor_tensor(rms[:, t, 2:4], rms[:, t, 0:2], expo[:, :].to_broadcast([P, 2]), ALU.pow).then_inc(rms_ready, 1)
                if l == 1:
                    slot_constants(pool)
                for s in range(2):
                    if l == 1 and s == 1:
                        pool_experts(pool)
                    for t in range(T):
                        k = T * (2 * l + s) + t + 1
                        pool.wait_ge(ln_var, k)
                        pool.tensor_tensor(rstd[:, t, 1:2], rstd[:, t, 0:1], expo[:, :], ALU.pow).then_inc(ln_rstd, 1)


        def load_ln(act, l, s):
            g, b = (("ln1_g", "ln1_b"), ("ln2_g", "ln2_b"))[s]
            if s == 0:
                act.wait_ge(y_mm, 4 * (l + 1))
            else:
                act.wait_ge(ln_done, T * (2 * l + 1))
            act.dma_start(lnp[:, 0, :], a[g][l:l + 1, :].partition_broadcast(P)).then_inc(lnp_in, 16)
            act.dma_start(lnp[:, 1, :], a[b][l:l + 1, :].partition_broadcast(P)).then_inc(lnp_in, 16)

        def blocks(b, k):
            return b[:, 0:k * P].rearrange("p (k s) -> p k s", k=k)

        def hT_of(g):
            return hT_odd if g % 2 else hT

        def slots_of(g):
            return slice(g % 2 * CAP, (g % 2 + 1) * CAP)

        def act_dense(act):
            def silus(g):
                n = DENSE[g][1]
                for t in range(T):
                    k = T * g + t
                    act.wait_ge(w1_mm, k + 1)
                    if g:
                        act.wait_ge(hid_ev, k - 1)
                    act.activation(silu[:, t, 0:n], bank[2 * t][:, 0:n], ACT.Silu).then_inc(silu_ev, 1)

            def turned(g):
                k = DENSE[g][1] // P
                for t in range(T):
                    act.wait_ge(h_tr, T * g + t + 1)
                    act.copy(hT_of(g)[:, HEAD, 0:k, t * P:(t + 1) * P], blocks(bank[2 * t], k)).then_inc(h_ev, 1)

            for m, (kind, g, half) in enumerate(ffn_units(DG)):
                if (kind, half) == ("w1", 1):
                    silus(g)
                if (kind, half) == ("w2", 0) and g + 1 < DG:
                    turned(g + 1)
                if (kind, g, half) == ("w3", 0, 1):
                    turned(0)
                if m < PER_DENSE - 1:
                    make_head(act, MIXER + m + SPLIT)

        def router_weights(act):
            act.wait_ge(slot_ids, 4)
            act.dma_start(wr[:, :].rearrange("p (k e) -> p k e", k=KD), a["moe_router"][0].rearrange("(k p) e -> p k e", p=P)).then_inc(router_in, 16)
            act.wait_ge(router_in, 16)
            act.copy(wrs[:, HEAD, :], wr[:, :]).then_inc(wr_ready, 1)

        def act_experts(act):
            act.wait_ge(chosen, 1)
            act.activation(r_exp, r_exp, ACT.Exp).then_inc(exp_done, 1)

            def expert_out(j, h):
                act.wait_ge(w2_mm, 2 * NG * j + (2 * (DG + NG) - 1 + h))
                act.wait_ge(sc_mm, 4 * j + CREDIT)
                act.copy(oe[:, h * W:(h + 1) * W], bank[4 + h][:, :]).then_inc(oe_ev, 1)

            def job(j, is_first):
                def turned(g):
                    act.wait_ge(h_tr, NG * j + (T * DG + g + 1))
                    act.copy(hT[:, HEAD, :, slots_of(g)], blocks(bank[6], 4)).then_inc(h_ev, 1)

                if not is_first:
                    for h in range(2):
                        job_head(act, j, h)
                        expert_out(j - 1, h)
                for h in range(2):
                    act.wait_ge(gat_mm, 2 * j + (h + 1 + CREDIT))
                    act.copy(xeT[:, HEAD, 4 * h:4 * h + 4, :], blocks(bank[6 + h], 4)).then_inc(gat_ev, 1)
                if not is_first:
                    job_head(act, j, 2)
                for m, (kind, g, half) in enumerate(JOB):
                    up_end = (kind, half) == ("w1", 1)
                    if up_end:
                        act.wait_ge(w1_mm, NG * j + (T * DG + g + 1))
                        act.wait_ge(hid_ev, NG * j + (T * DG + max(g - 1, 0)))
                        act.activation(silu[:, g % 2, :], bank[2 * (g % 2)][:, :], ACT.Silu).then_inc(silu_ev, 1)
                    if (kind, g, half) == ("w2", NG - 2, 0):
                        turned(NG - 1)
                    if m + SPLIT < PER_JOB:
                        job_head(act, j, m + SPLIT)
                    if up_end and g:
                        turned(g - 1)
                    if (kind, g, half) == ("w2", 1, 1):
                        act.wait_ge(comb_tr, j + (1 + CREDIT))
                        act.wait_ge(sc_mm, 4 * j + CREDIT)
                        act.copy(combT[:, :], bank[7][:, 0:SEQ]).then_inc(comb_ev, 1)

            act.sem_inc(comb_ev, CREDIT)
            act.sem_inc(oe_ev, CREDIT)
            extra = all_jobs(act, job)
            for h in range(2):
                expert_out(extra + (EXPERTS - 1), h)

        @block.scalar
        def _(act):
            act.dma_start(posi[:, :], a["positions"].rearrange("o (t p) -> p (o t)", p=P), allow_slow_non_contiguous=True).then_inc(small_in, 16)
            act.dma_start(invf[:, :], a["inv_freq"].partition_broadcast(P)).then_inc(small_in, 16)
            for l in range(DEPTH):
                act.dma_start(gcol[:, l, 0:3], a["mla_q_norm"][l].rearrange("(k p) -> p k", p=P), allow_slow_non_contiguous=True).then_inc(small_in, 16)
                act.dma_start(gcol[:, l, 3:5], a["mla_kv_norm"][l].rearrange("(k p) -> p k", p=P), allow_slow_non_contiguous=True).then_inc(small_in, 16)
            def turned_x(k, between):
                for t in range(T):
                    for h in range(2):
                        n = 2 * t + h
                        act.wait_ge(x_tr, 4 * k + n + 1)
                        act.copy(xT[:, HEAD, 4 * h:4 * h + 4, t * P:(t + 1) * P], blocks(bank[n], 4)).then_inc(x_ev, 1)
                    if t == 0:
                        make_head(act, between)

            turned_x(0, 0)
            for n in range(1, SPLIT):
                make_head(act, n)
            for l in range(DEPTH):
                first = LAYER * l

                def head(m):
                    make_head(act, first + m)

                def chunk(c):
                    c0, n = CHUNKS[c]
                    for t in range(T):
                        k = T * c + t
                        act.wait_ge(proj_mm, T * NCH * l + k + 1)
                        src, dst = bank[k % 4], proj[:, t, c0:c0 + n]
                        raw_cols = max(0, min(n, C_GA - c0))
                        if raw_cols == n:
                            act.copy(dst, src[:, 0:n]).then_inc(proj_ev, 1)
                        elif raw_cols == 0:
                            act.activation(dst, src[:, 0:n], ACT.Sigmoid).then_inc(proj_ev, 1)
                        else:
                            act.copy(dst[:, 0:raw_cols], src[:, 0:raw_cols])
                            act.activation(dst[:, raw_cols:n], src[:, raw_cols:n], ACT.Sigmoid).then_inc(proj_ev, 1)

                def squares():
                    for t in range(T):
                        if l or t:
                            act.wait_ge(sq_done, T * l + t)
                        act.wait_ge(proj_ev, T * (NCH * l + chunks_to(C_KR)))
                        if l:
                            act.wait_ge(rms_ready, T * (l - 1) + t + 1)
                        act.activation(junk[:, 0:Q_LORA], proj[:, t, C_Q:C_KV], ACT.Square, accum_out=rms[:, t, 0:1]).then_inc(act_step, 1)
                        act.wait_ge(act_step, T * l + t + 1)
                        act.activation(junk[:, 0:KV_LORA], proj[:, t, C_KV:C_KR], ACT.Square, accum_out=rms[:, t, 1:2]).then_inc(sq_done, 1)

                def indexer_turned():
                    for t in range(T):
                        act.wait_ge(idx_tr, T * l + t + 1)
                        act.copy(iT[:, :, t * P:(t + 1) * P], blocks(bank[4 + t], 3)).then_inc(idx_ev, 1)

                def relus(heads):
                    for h in heads:
                        k = IDX_HEADS * l + h
                        act.wait_ge(dots_mm, k + 1)
                        if h >= 4:
                            act.wait_ge(scored, k - 3)
                        act.activation(relu[:, h % 4, :], bank[4 + h % 4][:, 0:384], ACT.Relu,
                                       scale=float(IDX_HEADS * IDX_DIM) ** -0.5).then_inc(relu_ev, 1)

                def latents_turned():
                    for t in range(T):
                        act.wait_ge(c_tr, T * l + t + 1)
                        act.wait_ge(small_in, 6 * 16)
                        for k in range(5):
                            b = bank[4 + 2 * t + k // 4]
                            ins = act.activation(cT[:, HEAD, k, t * P:(t + 1) * P], b[:, (k % 4) * P:(k % 4 + 1) * P], ACT.Copy,
                                                 scale=gcol[:, l, k:k + 1])
                        ins.then_inc(c_ev, 1)

                for m in range(2 * NCH):
                    head(m + SPLIT)
                    if m % 2:
                        chunk(m // 2)
                    if l == 0 and m == 1:
                        act.wait_ge(sin_in, 1)
                        act.activation(trig[:, :, :], trig[:, :, :], ACT.Sin).then_inc(trig_done, 1)
                    if m == 3:
                        indexer_turned()
                    if m == 5:
                        relus(range(0, 4))
                        squares()
                    if m == 6:
                        relus(range(4, 8))
                    if m == 11:
                        latents_turned()
                for h in range(2):
                    head(2 * NCH + h + SPLIT)
                    for t in range(T):
                        act.wait_ge(uq_mm, 4 * l + 2 * h + t + 1)
                        act.copy(qm[:, t, h * 384:(h + 1) * 384], bank[4 + 2 * t + h][:, 0:384]).then_inc(uq_ev, 1)
                head(2 * NCH + 2 + SPLIT)
                for i in range(2):
                    for t in range(T):
                        act.wait_ge(dsa_tr, 4 * l + 2 * i + t + 1)
                        act.copy(dT[:, i, :, t * P:(t + 1) * P], blocks(bank[2 * i + t], 4)).then_inc(dsa_ev, 1)
                for t in range(T):
                    for h in range(2):
                        act.wait_ge(mq_tr, 4 * l + 2 * t + h + 1)
                        act.copy(qTm[:, 4 * h:4 * h + 4, t * P:(t + 1) * P],
                                 bank[4 + 2 * t + h][0:QK, :].rearrange("p (k s) -> p k s", k=4)).then_inc(mq_ev, 1)

                def exps(u):
                    k = 16 * l + u
                    scale = float(QK if u < 8 else DH) ** -0.5
                    act.wait_ge(row_max, k + 1)
                    act.activation(sm[:, u % NSM, 0:P], sm[:, u % NSM, 0:P], ACT.Exp, bias=mx[:, u, 0:1], scale=scale,
                                   accum_out=den[:, u, 0:1])
                    act.activation(sm[:, u % NSM, P:384], sm[:, u % NSM, P:384], ACT.Exp, bias=mx[:, u, 1:2], scale=scale,
                                   accum_out=den[:, u, 1:2]).then_inc(probs, 1)

                def turned_probs(u):
                    k = 16 * l + u
                    act.wait_ge(p_tr, k + 1)
                    if u >= NPT:
                        act.wait_ge(pv_mm, k - NPT + 1)
                    act.copy(pT[:, u % NPT, :], bank[2 + u % 2][:, 0:384]).then_inc(p_ev, 1)

                for i in range(16 + 1):
                    if i < 16:
                        exps(i)
                    if i >= 1:
                        turned_probs(i - 1)
                for m in range(2):
                    for t in range(T):
                        act.wait_ge(o_tr, 4 * l + 2 * m + t + 1)
                        act.copy(oT[:, HEAD, m, :, t * P:(t + 1) * P], blocks(bank[2 * m + t], 4)).then_inc(oT_ev, 1)

                def turned_merged(h):
                    for t in range(T):
                        act.wait_ge(m_tr, 4 * l + 2 * h + t + 1)
                        act.copy(xT[:, HEAD, 4 * h:4 * h + 4, t * P:(t + 1) * P], blocks(bank[4 * (1 - h) + t], 4)).then_inc(m_ev, 1)

                for m in range(21, 28):
                    head(m + SPLIT)
                    if m == 23:
                        turned_merged(0)
                    if m == 24:
                        load_ln(act, l, 0)
                    if m == 25:
                        turned_merged(1)
                        if l == 1:
                            router_weights(act)
                turned_x(2 * l + 1, first + 28 + SPLIT)
                load_ln(act, l, 1)
                if l == 0:
                    act_dense(act)
                    turned_x(2, LAYER + SPLIT - 1)
                else:
                    act_experts(act)

        def rest_of(dve, dst, src, done):
            return dve.tensor_tensor(dst[REST], src, dst[HEAD].bitcast(F32), ALU.subtract).then_inc(done, 1)

        def dve_dense(dve, step, layer_norm, first_half_stats, add_residual):
            def hidden(g):
                n = DENSE[g][1]
                for t in range(T):
                    k = T * g + t + 1
                    dve.wait_ge(silu_ev, k)
                    dve.wait_ge(w3_mm, k)
                    if g:
                        dve.wait_ge(h_tr, k - T)
                    dve.tensor_tensor(hid[:, t, 0:n], silu[:, t, 0:n], bank[1 + 2 * t][:, 0:n], ALU.mult).then_inc(hid_ev, 1)

            def turned(g):
                k = DENSE[g][1] // P
                for t in range(T):
                    dve.wait_ge(h_ev, T * g + t + 1)
                    rest_of(dve, [hT_of(g)[:, i, 0:k, t * P:(t + 1) * P] for i in (HEAD, REST)], blocks(bank[2 * t], k), h_rest)

            for m, (kind, g, half) in enumerate(ffn_units(DG)):
                if (kind, half) == ("w3", 1):
                    hidden(g)
                if (kind, half) == ("w2", 0) and g + 1 < DG:
                    turned(g + 1)
                if (kind, g, half) == ("w3", 0, 1):
                    turned(0)
                if m == PER_DENSE - 2:
                    dve.wait_ge(w2_mm, 2 * DG - 1)
                    first_half_stats(lambda t: add_residual(t, 0, 4 + 2 * t))
                if m < PER_DENSE - 2:
                    make_rest(dve, MIXER + m + SPLIT)

            def second_half(t):
                dve.wait_ge(*((w2_mm, 2 * DG) if t else (w2_tile, 2 * DG)))
                add_residual(t, 1, 5 + 2 * t)

            layer_norm(1, x, second_half, 2)

        def dve_experts(dve, step):
            dve.wait_ge(slot_ids, 4)
            lg = bank[7][:, 0:T * EXPERTS].rearrange("p (t e) -> p t e", t=T)
            step(dve.memset(r_keys[:, :, 2:8], UNUSED))
            dve.wait_ge(route_mm, 1)
            dve.tensor_copy(logitsT[:, :], bank[6][0:EXPERTS, 0:SEQ]).then_inc(logits_ev, 1)
            dve.wait_ge(logits_tr, 1)
            step(dve.tensor_copy(r_list[:, :, 0:EXPERTS], lg))
            for t in range(T):
                ins = dve.max(r_top[:, t, :], r_list[:, t, 0:EXPERTS])
            step(ins)
            step(dve.tensor_copy(r_keys[:, :, 0:2], r_top[:, :, 0:2]))
            for t in range(T):
                ins = dve.match_replace(out=r_list[:, t, :], in_to_replace=r_keys[:, t, :], in_values=r_list[:, t, :],
                                        imm_value=TAKEN)
            step(ins)
            step(dve.tensor_scalar(r_sel, r_list[:, :, 0:EXPERTS], TAKEN * 0.5, None, ALU.is_lt))
            dve.tensor_tensor(r_exp, lg, r_top[:, :, 0:1].to_broadcast([P, T, EXPERTS]), ALU.subtract).then_inc(chosen, 1)
            step(dve.memset(flags[:, :], 0.0))
            dve.wait_ge(pos_mm, 1)
            pos = bank[6][:, 0:T * EXPERTS].rearrange("p (t e) -> p t e", t=T)
            step(dve.scalar_tensor_tensor(out=r_pos, in0=pos, scalar=1.0, in1=r_sel, op0=ALU.add, op1=ALU.mult))
            step(dve.tensor_scalar(r_pos, r_pos, -1.0, None, ALU.add))
            E = EXPERTS
            over, s1, s2, s4 = (flags[0:1, i * 16:(i + 1) * 16] for i in range(4))
            step(dve.tensor_scalar(over[:, E:2 * E], bank[6][0:1, 2 * E:3 * E], float(CAP), None, ALU.is_gt))
            dve.wait_ge(exp_done, 1)
            step(dve.tensor_tensor(r_exp, r_exp, r_sel, ALU.mult))
            step(dve.reduce_sum(r_one[:, :, 1:2], r_exp, AX_X))
            step(dve.reciprocal(r_one[:, :, 2:3], r_one[:, :, 1:2]))
            dve.tensor_tensor(r_comb, r_exp, r_one[:, :, 2:3].to_broadcast([P, T, EXPERTS]), ALU.mult).then_inc(placed, 1)
            make_rest(dve, FIRST + SPLIT - 1)
            for src, dst, by in ((over, s1, 1), (s1, s2, 2), (s2, s4, 4)):
                step(dve.tensor_tensor(dst[:, E:2 * E], src[:, E:2 * E], src[:, E - by:2 * E - by], ALU.add))
            step(dve.tensor_copy(jobs[0:1, 0:E], over[:, E:2 * E]))
            step(dve.tensor_tensor(jobs[0:1, E:2 * E], s4[:, E:2 * E], over[:, E:2 * E], ALU.subtract))
            step(dve.tensor_copy(jobs[0:1, 2 * E:2 * E + 1], s4[:, 2 * E - 1:2 * E]))
            dve.sem_inc(routed, 1)

            def add_up(j):
                for h in range(2):
                    for t in range(T):
                        dve.wait_ge(sc_mm, 4 * j + (2 * h + t + 1 + CREDIT))
                        dve.tensor_tensor(y[:, t, h * W:(h + 1) * W], y[:, t, h * W:(h + 1) * W], bank[SCATTER[h][t]][:, :], ALU.add).then_inc(y_add, 1)

            def job(j, is_first):
                if not is_first:
                    for m in range(2):
                        job_rest(dve, j, m)
                for h in range(2):
                    dve.wait_ge(gat_ev, 2 * j + (h + 1))
                    rest_of(dve, [xeT[:, i, 4 * h:4 * h + 4, :] for i in (HEAD, REST)], blocks(bank[6 + h], 4), gat_rest)
                if not is_first:
                    dve.wait_ge(y_add, 4 * j - 4 + CREDIT)
                    add_up(j - 1)
                    job_rest(dve, j, 2)

                def hidden(g):
                    k = T * DG + g + 1
                    dve.wait_ge(silu_ev, NG * j + k)
                    dve.wait_ge(w3_mm, NG * j + k)
                    dve.wait_ge(h_tr, NG * j + (k - (2 if g else 1)))
                    dve.tensor_tensor(hid[:, g % 2, :], silu[:, g % 2, :], bank[1 + 2 * (g % 2)][:, :], ALU.mult).then_inc(hid_ev, 1)

                def turned(g):
                    dve.wait_ge(h_ev, NG * j + (T * DG + g + 1))
                    rest_of(dve, [hT[:, i, :, slots_of(g)] for i in (HEAD, REST)], blocks(bank[6], 4), h_rest)

                for m, (kind, g, half) in enumerate(JOB):
                    if (kind, half) == ("w3", 1):
                        hidden(g)
                    if (kind, g, half) == ("w2", NG - 2, 0):
                        turned(NG - 1)
                    if m + SPLIT < PER_JOB:
                        job_rest(dve, j, m + SPLIT)
                    if (kind, half) == ("w1", 1) and g:
                        turned(g - 1)
                if is_first:
                    for t in range(T):
                        step(dve.tensor_scalar(y[:, t, :], x[:, t, :], ALPHA, None, ALU.mult))

            dve.sem_inc(y_add, CREDIT)
            extra = all_jobs(dve, job)
            add_up(extra + (EXPERTS - 1))
            dve.wait_ge(y_add, 4 * extra + (4 * EXPERTS + CREDIT))

        @block.vector
        def _(dve):
            n = [0]

            def step(ins):
                n[0] += 1
                ins.then_inc(dve_step, 1)
                dve.wait_ge(dve_step, n[0])

            def angles():
                dve.wait_ge(small_in, 6 * 16)
                step(dve.tensor_copy(posf[:, :], posi[:, :]))
                hi, mid, lo = split_2pi()
                for t in range(T):
                    for h in range(2):
                        ins = dve.tensor_scalar(trig[:, t, h * NF:(h + 1) * NF], invf[:, :], posf[:, t:t + 1], None, ALU.mult)
                step(ins)
                for h in range(2):
                    cols = slice(h * NF, (h + 1) * NF)
                    step(dve.tensor_scalar(turns[:, :, cols], trig[:, :, cols], 1.0 / TWO_PI, 0.25 * h, ALU.mult, ALU.add))
                step(dve.tensor_scalar(turns[:, :, :], turns[:, :, :], ROUND, None, ALU.add))
                step(dve.tensor_scalar(turns[:, :, :], turns[:, :, :], ROUND, None, ALU.subtract))
                for part in (hi, mid, lo):
                    step(dve.scalar_tensor_tensor(out=trig[:, :, :], in0=turns[:, :, :], scalar=-part, in1=trig[:, :, :],
                                                  op0=ALU.mult, op1=ALU.add))
                step(dve.tensor_scalar(trig[:, :, NF:2 * NF], trig[:, :, NF:2 * NF], HALF_PI, None, ALU.add))
                dve.tensor_scalar(trig[:, :, :], trig[:, :, :], PI_F, -PI_F, ALU.min, ALU.max).then_inc(sin_in, 1)

            def rope_tables():
                dve.wait_ge(trig_done, 1)
                for tab, f0, nf in ((rope32, 0, RQ), (rope64, RQ, RD)):
                    s_, c_ = trig[:, :, f0:f0 + nf], trig[:, :, NF + f0:NF + f0 + nf]
                    dve.tensor_copy(tab[:, :, 0, 0:nf], c_)
                    dve.tensor_copy(tab[:, :, 0, nf:2 * nf], c_)
                    dve.tensor_scalar(tab[:, :, 1, 0:nf], s_, -1.0, None, ALU.mult)
                    step(dve.tensor_copy(tab[:, :, 1, nf:2 * nf], s_))

            def rope(v, t, heads, d, tab, done=None):
                h2 = d // 2
                c_ = tab[:, t, 0:1, :].to_broadcast([P, heads, d])
                A = ropeA[:, 0:heads * d].rearrange("p (h d) -> p h d", h=heads)
                B = ropeB[:, 0:heads * d].rearrange("p (h d) -> p h d", h=heads)
                dve.tensor_tensor(A, v, c_, ALU.mult)
                dve.tensor_tensor(B[:, :, 0:h2], v[:, :, h2:d], tab[:, t, 1:2, 0:h2].to_broadcast([P, heads, h2]), ALU.mult)
                step(dve.tensor_tensor(B[:, :, h2:d], v[:, :, 0:h2], tab[:, t, 1:2, h2:d].to_broadcast([P, heads, h2]), ALU.mult))
                ins = dve.tensor_tensor(v, A, B, ALU.add)
                if done is None:
                    step(ins)
                else:
                    ins.then_inc(done[0], 1)
                    dve.wait_ge(done[0], done[1])

            def rest_x(k, t, h):
                dve.wait_ge(x_ev, 4 * k + 2 * t + h + 1)
                rest_of(dve, [xT[:, i, 4 * h:4 * h + 4, t * P:(t + 1) * P] for i in (HEAD, REST)], blocks(bank[2 * t + h], 4), x_rest)

            def add_residual(t, h, b):
                step(dve.scalar_tensor_tensor(out=x[:, t, h * W:(h + 1) * W], in0=x[:, t, h * W:(h + 1) * W], scalar=ALPHA,
                                              in1=bank[b][:, :], op0=ALU.mult, op1=ALU.add))

            def heads_of(v, heads):
                return v.rearrange("p (h d) -> p h d", h=heads)

            def half_stats(src, t, h):
                step(dve.bn_stats(stat[:, t, h, :], src[:, t, h * W:(h + 1) * W]))

            def first_half_stats(add, src=x):
                for t in range(T):
                    add(t)
                    half_stats(src, t, 0)

            def layer_norm(k, src, second_half, turned=None):
                def statistics(t):
                    second_half(t)
                    half_stats(src, t, 1)
                    step(dve.bn_aggr(mv[:, t, :], stat[:, t, :, :].rearrange("p a b -> p (a b)")))
                    dve.tensor_scalar(rstd[:, t, 0:1], mv[:, t, 1:2], EPS, None, ALU.add).then_inc(ln_var, 1)

                def centre(t):
                    dve.wait_ge(lnp_in, 32 * (k + 1))
                    step(dve.scalar_tensor_tensor(out=x[:, t, :], in0=src[:, t, :], scalar=mv[:, t, 0:1], in1=lnp[:, 0, :],
                                                  op0=ALU.subtract, op1=ALU.mult))

                def scale(t):
                    dve.wait_ge(ln_rstd, T * k + t + 1)
                    dve.scalar_tensor_tensor(out=x[:, t, :], in0=x[:, t, :], scalar=rstd[:, t, 1:2], in1=lnp[:, 1, :],
                                             op0=ALU.mult, op1=ALU.add).then_inc(ln_done, 1)

                statistics(0)
                centre(0)
                scale(0)
                statistics(1)
                if turned is not None:
                    for h in range(2):
                        rest_x(turned, 0, h)
                centre(1)
                scale(1)
                if turned is not None:
                    for h in range(2):
                        rest_x(turned, 1, h)

            for t in range(T):
                for h in range(2):
                    rest_x(0, t, h)
                if t == 0:
                    make_rest(dve, 0)
            for unit in range(1, SPLIT):
                make_rest(dve, unit)
            angles()
            dve.wait_ge(consts, 1)
            for l in range(DEPTH):
                first = LAYER * l

                def rest(m):
                    make_rest(dve, first + m)

                def latents():
                    for t in range(T):
                        dve.wait_ge(sq_done, T * l + t + 1)
                        step(dve.tensor_scalar(rms[:, t, 0:1], rms[:, t, 0:1], 1.0 / Q_LORA, EPS, ALU.mult, ALU.add))
                        dve.tensor_scalar(rms[:, t, 1:2], rms[:, t, 1:2], 1.0 / KV_LORA, EPS, ALU.mult, ALU.add).then_inc(ms_ready, 1)

                def latents_normed():
                    for t in range(T):
                        dve.wait_ge(rms_ready, T * l + t + 1)
                        dve.tensor_scalar(proj[:, t, C_Q:C_KV], proj[:, t, C_Q:C_KV], rms[:, t, 2:3], None, ALU.mult)
                        dve.tensor_scalar(proj[:, t, C_KV:C_KR], proj[:, t, C_KV:C_KR], rms[:, t, 3:4], None, ALU.mult).then_inc(lat_norm, 1)
                    for t in range(T):
                        rope(heads_of(proj[:, t, C_KR:C_DQ], 1), t, 1, ROPE, rope32)

                def ropes_dsa(t):
                    dve.wait_ge(proj_ev, T * (NCH * l + chunks_to(C_DV)))
                    rope(heads_of(proj[:, t, C_DQ:C_DK], HEADS), t, HEADS, DH, rope64)
                    rope(heads_of(proj[:, t, C_DK:C_DV], HEADS), t, HEADS, DH, rope64, (dsa_roped, T * l + t + 1))

                def ropes_indexer():
                    dve.wait_ge(proj_ev, T * (NCH * l + 1))
                    for t in range(T):
                        rope(heads_of(proj[:, t, C_IQ:C_IK], IDX_HEADS), t, IDX_HEADS, IDX_DIM, rope32)
                        rope(heads_of(proj[:, t, C_IK:C_IW], 1), t, 1, IDX_DIM, rope32)
                        ik4 = score[:, t, 0:P].rearrange("p (r d) -> p r d", r=4)
                        dve.tensor_copy(ik4, proj[:, t:t + 1, C_IK:C_IW].to_broadcast([P, 4, IDX_DIM])).then_inc(idx_roped, 1)

                def scores(heads):
                    dve.wait_ge(idx_tr, T * (l + 1))
                    for h in heads:
                        dve.wait_ge(relu_ev, IDX_HEADS * l + h + 1)
                        for t in range(T):
                            keys = (t + 1) * P
                            part = relu[:, h % 4, t * P:t * P + keys]
                            prev = causal[:, t, 0:keys] if h == 0 else score[:, t, 0:keys]
                            ins = dve.scalar_tensor_tensor(out=score[:, t, 0:keys], in0=part, scalar=proj[:, t, C_IW + h:C_IW + h + 1],
                                                           in1=prev, op0=ALU.mult, op1=ALU.add)
                        ins.then_inc(scored, 1)
                        dve.wait_ge(scored, IDX_HEADS * l + h + 1)

                def best_keys(rounds):
                    for r in rounds:
                        for t in range(T):
                            ins = dve.max(top8[:, t, :], score[:, t, 0:(t + 1) * P])
                        step(ins)
                        for t in range(T):
                            keys = (t + 1) * P
                            ins = dve.match_replace(out=score[:, t, 0:keys], in_to_replace=top8[:, t, :],
                                                    in_values=score[:, t, 0:keys], imm_value=TAKEN)
                        step(ins)

                def selection():
                    for t in range(T):
                        keys = (t + 1) * P
                        step(dve.tensor_scalar(select[:, t, 0:keys], score[:, t, 0:keys], TAKEN * 0.5, MASKED, ALU.is_gt, ALU.mult))
                        step(dve.tensor_tensor(select[:, t, 0:keys], select[:, t, 0:keys], causal[:, t, 0:keys], ALU.add))

                def latents_rest():
                    for t in range(T):
                        dve.wait_ge(c_ev, T * l + t + 1)
                        for k in range(5):
                            at = slice(t * P, (t + 1) * P)
                            ins = dve.scalar_tensor_tensor(out=cT[:, REST, k, at], in0=bank[4 + 2 * t + k // 4][:, (k % 4) * P:(k % 4 + 1) * P],
                                                           scalar=gcol[:, l, k:k + 1], in1=cT[:, HEAD, k, at].bitcast(F32),
                                                           op0=ALU.mult, op1=ALU.subtract)
                        ins.then_inc(c_rest, 1)

                R = N_SEL // 8
                for m in range(2 * NCH):
                    rest(m + SPLIT)
                    if m == 1:
                        if l == 0:
                            rope_tables()
                        ropes_indexer()
                    if m == 5:
                        scores(range(0, 4))
                        latents()
                    if m == 6:
                        scores(range(4, 8))
                    if m == 7:
                        latents_normed()
                    if m in (9, 10):
                        ropes_dsa(m - 9)
                    if m == 11:
                        latents_rest()
                    if 8 <= m < 16:
                        best_keys(range(R * (m - 8) // 8, R * (m - 7) // 8))
                    if m == 16:
                        selection()
                rest(18 + SPLIT)
                for t in range(T):
                    for h in range(2):
                        dve.wait_ge(ukv_mm, 4 * l + 2 * t + h + 1)
                        src = bank[2 * t + h][:, :].rearrange("p (h d) -> p h d", h=4)
                        dve.tensor_copy(heads_of(km[:, t, :], HEADS)[:, 4 * h:4 * h + 4, 0:NOPE], src[:, :, 0:NOPE])
                        dve.tensor_copy(heads_of(vm[:, t, :], HEADS)[:, 4 * h:4 * h + 4, :], src[:, :, NOPE:P]).then_inc(ukv_ev, 1)
                    dve.tensor_copy(heads_of(km[:, t, :], HEADS)[:, :, NOPE:QK],
                                    proj[:, t:t + 1, C_KR:C_DQ].to_broadcast([P, HEADS, ROPE])).then_inc(kr_put, 1)
                dve.wait_ge(uq_ev, 4 * (l + 1))
                for t in range(T):
                    rope(heads_of(qm[:, t, :], HEADS)[:, :, NOPE:QK], t, HEADS, ROPE, rope32, (qm_roped, T * l + t + 1))
                for t in range(T):
                    for h in range(2):
                        dve.wait_ge(mk_tr, 4 * l + 2 * t + h + 1)
                        dve.tensor_copy(kTm[:, 4 * h:4 * h + 4, t * P:(t + 1) * P],
                                        bank[2 * t + h][0:QK, :].rearrange("p (k s) -> p k s", k=4)).then_inc(mk_ev, 1)

                def maxima(u):
                    k = 16 * l + u
                    mask = causal if u < 8 else select
                    scale = float(QK if u < 8 else DH) ** -0.5
                    dve.wait_ge(qk_mm, k + 1)
                    if u >= NSM:
                        dve.wait_ge(p_tr, k - NSM + 1)
                    for t in range(T):
                        lo_, keys = t * P, (t + 1) * P
                        ins = dve.tensor_tensor_reduce(sm[:, u % NSM, lo_:lo_ + keys], bank[u % 2][:, lo_:lo_ + keys],
                                                       mask[:, t, 0:keys], 1.0, FLOOR, ALU.add, ALU.max, mx[:, u, t:t + 1])
                    step(ins)
                    dve.tensor_scalar(mx[:, u, :], mx[:, u, :], -scale, None, ALU.mult).then_inc(row_max, 1)

                def norm_heads(m):
                    dve.wait_ge(pv_mm, 16 * l + 8 * (m + 1))
                    for t in range(T):
                        step(dve.reciprocal(rden[:, t, :], den[:, 8 * m:8 * m + 8, t]))
                        dve.tensor_tensor(heads_of(o_tok[m][t], HEADS), heads_of(bank[4 + 2 * m + t][:, :], HEADS),
                                          rden[:, t, :].unsqueeze(2).to_broadcast([P, HEADS, VDIM]), ALU.mult).then_inc(o_ev, 1)

                for u in range(16):
                    maxima(u)
                    if u == 4:
                        rest(19 + SPLIT)
                    if u == 8:
                        rest(20 + SPLIT)
                    if u == 12:
                        norm_heads(0)
                norm_heads(1)
                for m in range(2):
                    for t in range(T):
                        dve.wait_ge(oT_ev, 4 * l + 2 * m + t + 1)
                        rest_of(dve, [oT[:, i, m, :, t * P:(t + 1) * P] for i in (HEAD, REST)], blocks(bank[2 * m + t], 4), o_rest)

                def merge(h):
                    for t in range(T):
                        ga, gb = proj[:, t, C_GA + h * W:C_GA + (h + 1) * W], proj[:, t, C_GB + h * W:C_GB + (h + 1) * W]
                        dve.wait_ge(y_mm, 4 * l + 2 * h + t + 1)
                        dve.tensor_tensor(ga, ga, bank[4 * (1 - h) + t][:, :], ALU.mult)
                        step(dve.tensor_tensor(gb, gb, bank[4 * (1 - h) + 2 + t][:, :], ALU.mult))
                        dve.tensor_tensor(ga, ga, gb, ALU.add).then_inc(merged, 1)

                def merged_rest(h):
                    for t in range(T):
                        dve.wait_ge(m_ev, 4 * l + 2 * h + t + 1)
                        rest_of(dve, [xT[:, i, 4 * h:4 * h + 4, t * P:(t + 1) * P] for i in (HEAD, REST)], blocks(bank[4 * (1 - h) + t], 4), m_rest)

                def out_half(t, h):
                    dve.wait_ge(out_mm, 4 * l + 2 * h + t + 1)
                    add_residual(t, h, 4 + 2 * (1 - h) + t)

                for m in range(21, 28):
                    if m == 22:
                        merge(0)
                    if m == 24:
                        merge(1)
                    if (l, m) == (1, 26):
                        dve.wait_ge(wr_ready, 1)
                        dve.tensor_tensor(wrs[:, REST, :], wr[:, :], wrs[:, HEAD, :].bitcast(F32), ALU.subtract).then_inc(wr_ready, 1)
                    if m == 27:
                        first_half_stats(lambda t: out_half(t, 0))
                    rest(m + SPLIT)
                    if m == 23:
                        merged_rest(0)
                    if m == 25:
                        merged_rest(1)
                if l == 0:
                    layer_norm(0, x, lambda t: out_half(t, 1), 1)
                    rest(28 + SPLIT)
                    dve_dense(dve, step, layer_norm, first_half_stats, add_residual)
                    make_rest(dve, LAYER + SPLIT - 2)
                    make_rest(dve, LAYER + SPLIT - 1)
                else:
                    layer_norm(2, x, lambda t: out_half(t, 1), 3)
                    dve_experts(dve, step)
                    first_half_stats(lambda t: None, y)
                    layer_norm(3, y, lambda t: None)

        def product(pe, out_, act_, w, first, last):
            pe.matmul(out_, act_[REST], w[HEAD], start=first, stop=False)
            pe.matmul(out_, act_[HEAD], w[HEAD], start=False, stop=False)
            return pe.matmul(out_, act_[HEAD], w[REST], start=False, stop=last)

        def split_ready(pe, n):
            pe.wait_ge(rests_made, n + 1)

        def x_at(k, t):
            return [xT[:, i, k, t * P:(t + 1) * P] for i in (HEAD, REST)]

        def cols(w, k, c0=0, n=None):
            return [v[:, k, c0:(c0 + n if n else None)] for v in w]

        def pe_mixer(pe, l, tp, turn_x, x_split):
            base = T * NCH * l

            def unit(*u):
                n = number(u)
                split_ready(pe, n)
                return halves(n, *source(u)[1:])

            def chunk(c, half, t):
                n = CHUNKS[c][1]
                w = unit("in", l, c, half)
                k = T * c + t
                if k >= 4 and half == 0:
                    pe.wait_ge(proj_ev, base + k - 3)
                for i in range(4):
                    ins = product(pe, bank[k % 4][:, 0:n], x_at(4 * half + i, t), cols(w, i),
                                  half == 0 and i == 0, half == 1 and i == 3)
                if half:
                    ins.then_inc(proj_mm, 1)
                elif t == T - 1:
                    ins.then_inc(half_mm, 1)

            def dots(heads):
                for h in heads:
                    r = IDX_DIM * (h % 4)
                    rows = slice(r, r + IDX_DIM)
                    if h >= 4:
                        pe.wait_ge(relu_ev, IDX_HEADS * l + h - 3)
                    for t in range(T):
                        keys = (t + 1) * P
                        ins = pe.matmul(bank[4 + h % 4][:, t * P:t * P + keys], iT[rows, h // 4, t * P:(t + 1) * P],
                                        iT[rows, 2, 0:keys], start=True, stop=True)
                    ins.then_inc(dots_mm, 1)

            def indexer_turn():
                for t in range(T):
                    pe.wait_ge(idx_roped, T * l + t + 1)
                    for i in range(2):
                        tp(bank[4 + t][:, i * P:(i + 1) * P], proj[:, t, C_IQ + i * P:C_IQ + (i + 1) * P])
                    tp(bank[4 + t][:, 2 * P:3 * P], score[:, t, 0:P]).then_inc(idx_tr, 1)

            def latents_turn():
                pe.wait_ge(relu_ev, IDX_HEADS * (l + 1))
                for t in range(T):
                    pe.wait_ge(lat_norm, T * l + t + 1)
                    for k in range(5):
                        ins = tp(bank[4 + 2 * t + k // 4][:, (k % 4) * P:(k % 4 + 1) * P], proj[:, t, k * P:(k + 1) * P])
                    ins.then_inc(c_tr, 1)

            for m in range(2 * NCH):
                for t in range(T):
                    if m == 0:
                        for ready in (t,) if l else range(t * T, T):
                            turn_x(2 * l, ready)
                        x_split(2 * l, t)
                    chunk(m // 2, m % 2, t)
                if m == 3:
                    indexer_turn()
                if m == 5:
                    pe.wait_ge(idx_ev, T * (l + 1))
                    dots(range(0, 4))
                if m == 6:
                    dots(range(4, 8))
                if m == 11:
                    latents_turn()
            pe.wait_ge(c_rest, T * (l + 1))

            def c_at(k, t):
                return [cT[:, i, k, t * P:(t + 1) * P] for i in (HEAD, REST)]

            for h in range(2):
                w = unit("uq", l, h)
                for t in range(T):
                    for i in range(3):
                        ins = product(pe, bank[4 + 2 * t + h][:, 0:384], c_at(i, t), cols(w, i), i == 0, i == 2)
                    ins.then_inc(uq_mm, 1)
            pe.wait_ge(proj_ev, base + T * NCH)
            w = unit("ukv", l)
            for t in range(T):
                for h in range(2):
                    for i in range(2):
                        ins = product(pe, bank[2 * t + h][:, :], c_at(3 + i, t), cols(w, i, h * W, W), i == 0, i == 1)
                    ins.then_inc(ukv_mm, 1)
            pe.wait_ge(dsa_roped, T * (l + 1))
            pe.wait_ge(ukv_ev, 4 * (l + 1))
            for i, c0 in enumerate((C_DQ, C_DK)):
                for t in range(T):
                    for k in range(4):
                        ins = tp(bank[2 * i + t][:, k * P:(k + 1) * P], proj[:, t, c0 + k * P:c0 + (k + 1) * P])
                    ins.then_inc(dsa_tr, 1)
            for t in range(T):
                pe.wait_ge(qm_roped, T * l + t + 1)
                for h in range(2):
                    for k in range(4):
                        ins = tp(bank[4 + 2 * t + h][0:QK, k * P:(k + 1) * P], qm[:, t, (4 * h + k) * QK:(4 * h + k + 1) * QK])
                    ins.then_inc(mq_tr, 1)
            pe.wait_ge(dsa_ev, 4 * (l + 1))
            for t in range(T):
                pe.wait_ge(kr_put, T * l + t + 1)
                for h in range(2):
                    for k in range(4):
                        ins = tp(bank[2 * t + h][0:QK, k * P:(k + 1) * P], km[:, t, (4 * h + k) * QK:(4 * h + k + 1) * QK])
                    ins.then_inc(mk_tr, 1)
            pe.wait_ge(mq_ev, 4 * (l + 1))
            pe.wait_ge(mk_ev, 4 * (l + 1))

            def qk(u):
                h = u % 8
                if u >= 2:
                    pe.wait_ge(row_max, 16 * l + u - 1)
                for t in range(T):
                    keys = (t + 1) * P
                    if u < 8:
                        q, kk = qTm[:, h, t * P:(t + 1) * P], kTm[:, h, 0:keys]
                    else:
                        rows = slice(DH * (h % 2), DH * (h % 2) + DH)
                        q, kk = qTd[rows, h // 2, t * P:(t + 1) * P], kTd[rows, h // 2, 0:keys]
                    ins = pe.matmul(bank[u % 2][:, t * P:t * P + keys], q, kk, start=True, stop=True)
                ins.then_inc(qk_mm, 1)

            def turn_probs(u):
                pe.wait_ge(probs, 16 * l + u + 1)
                if u >= 2:
                    pe.wait_ge(p_ev, 16 * l + u - 1)
                for i in range(3):
                    ins = tp(bank[2 + u % 2][:, i * P:(i + 1) * P], sm[:, u % NSM, i * P:(i + 1) * P])
                ins.then_inc(p_tr, 1)

            def pv(u):
                h, m = u % 8, u // 8
                pe.wait_ge(p_ev, 16 * l + u + 1)

                def v(t):
                    if m == 0:
                        return vm[:, t, h * VDIM:(h + 1) * VDIM]
                    return proj[:, t, C_DV + h * DH:C_DV + (h + 1) * DH]

                at = slice(h * VDIM, (h + 1) * VDIM)
                pe.matmul(bank[4 + 2 * m][:, at], pT[:, u % NPT, 0:P], v(0), start=True, stop=True)
                pe.matmul(bank[5 + 2 * m][:, at], pT[:, u % NPT, P:2 * P], v(0), start=True, stop=False)
                pe.matmul(bank[5 + 2 * m][:, at], pT[:, u % NPT, 2 * P:3 * P], v(1), start=False, stop=True).then_inc(pv_mm, 1)

            for i in range(16 + 3):
                if i < 16:
                    qk(i)
                if 2 <= i < 18:
                    turn_probs(i - 2)
                if i >= 3:
                    pv(i - 3)
            pe.wait_ge(row_max, 16 * (l + 1))
            for m in range(2):
                for t in range(T):
                    pe.wait_ge(o_ev, 4 * l + 2 * m + t + 1)
                    for k in range(4):
                        ins = tp(bank[2 * m + t][:, k * P:(k + 1) * P], o_tok[m][t][:, k * P:(k + 1) * P])
                    ins.then_inc(o_tr, 1)
            pe.wait_ge(o_rest, 4 * (l + 1))

            def branch(name, m, h):
                w = unit(name, l, h)
                for t in range(T):
                    for i in range(4):
                        ins = product(pe, bank[4 * (1 - h) + 2 * m + t][:, :], [oT[:, s_, m, i, t * P:(t + 1) * P] for s_ in (HEAD, REST)],
                                      cols(w, i), i == 0, i == 3)
                    if m:
                        ins.then_inc(y_mm, 1)
                if m == 0:
                    ins.then_inc(ya_mm, 1)

            def turn_merged(h):
                for t in range(T):
                    pe.wait_ge(merged, 4 * l + 2 * h + t + 1)
                    for i in range(4):
                        ins = tp(bank[4 * (1 - h) + t][:, i * P:(i + 1) * P], proj[:, t, C_GA + h * W + i * P:C_GA + h * W + (i + 1) * P])
                    ins.then_inc(m_tr, 1)

            def out_projection(h, half):
                w = unit("out", l, h, half)
                for t in range(T):
                    for i in range(4):
                        ins = product(pe, bank[4 + 2 * (1 - h) + t][:, :], x_at(4 * half + i, t), cols(w, i),
                                      half == 0 and i == 0, half == 1 and i == 3)
                    if half:
                        ins.then_inc(out_mm, 1)
                if not half:
                    ins.then_inc(half_mm, 1)

            branch("oa", 0, 0)
            branch("ob", 1, 0)
            branch("oa", 0, 1)
            turn_merged(0)
            branch("ob", 1, 1)
            pe.wait_ge(m_rest, 4 * l + 2)
            out_projection(0, 0)
            turn_merged(1)
            out_projection(1, 0)
            pe.wait_ge(m_rest, 4 * l + 4)
            out_projection(0, 1)
            out_projection(1, 1)

        def pe_dense(pe, tp, turn_x, x_split):
            def turn(g):
                for t in range(T):
                    pe.wait_ge(hid_ev, T * g + t + 1)
                    for i in range(DENSE[g][1] // P):
                        ins = tp(bank[2 * t][:, i * P:(i + 1) * P], hid[:, t, i * P:(i + 1) * P])
                    ins.then_inc(h_tr, 1)

            units = ffn_units(DG)
            for m, t in [(m, t) for m in range(PER_DENSE) for t in range(T)]:
                if m == 0:
                    turn_x(1, t)
                    x_split(1, t)
                kind, g, half = units[m]
                n = MIXER + m
                split_ready(pe, n)
                w = halves(n, *source(STREAM[n])[1:])
                n_hid = DENSE[g][1]
                if kind == "w2":
                    pe.wait_ge(h_rest, T * (g + 1))
                    for i in range(n_hid // P):
                        ins = product(pe, bank[4 + 2 * t + half][:, :], [hT_of(g)[:, s_, i, t * P:(t + 1) * P] for s_ in (HEAD, REST)],
                                      cols(w, i), g == 0 and i == 0, g == DG - 1 and i == n_hid // P - 1)
                    ins.then_inc(w2_mm if t else w2_tile, 1)
                    if t == T - 1 and half == 0 and g + 1 < DG:
                        turn(g + 1)
                else:
                    full, first_half, b = (w1_mm, w1_half, 0) if kind == "w1" else (w3_mm, w3_half, 1)
                    if g and kind == "w1" and half == 0:
                        pe.wait_ge(h_rest, T * (g - 1) + t + 1)
                    for i in range(4):
                        ins = product(pe, bank[2 * t + b][:, 0:n_hid], x_at(4 * half + i, t), cols(w, i),
                                      half == 0 and i == 0, half == 1 and i == 3)
                    if half:
                        ins.then_inc(full, 1)
                    elif t == T - 1:
                        ins.then_inc(first_half, 1)
                    if (kind, g, half, t) == ("w3", 0, 1, T - 1):
                        turn(0)

        def pe_experts(pe, tp, turn_x, x_split):
            w = [wrs[:, i, :].rearrange("p (k e) -> p k e", k=KD) for i in (HEAD, REST)]
            for t in range(T):
                turn_x(3, t)
                x_split(3, t)
                if t == 0:
                    pe.wait_ge(wr_ready, 2)
                for i in range(KD):
                    x_i, out_ = x_at(i, t), bank[6][0:EXPERTS, t * P:(t + 1) * P]
                    pe.matmul(out_, w[HEAD][:, i, :], x_i[REST], start=(i == 0), stop=False)
                    pe.matmul(out_, w[REST][:, i, :], x_i[HEAD], start=False, stop=False)
                    ins = pe.matmul(out_, w[HEAD][:, i, :], x_i[HEAD], start=False, stop=(i == KD - 1))
            ins.then_inc(route_mm, 1)
            pe.wait_ge(logits_ev, 1)
            for t in range(T):
                ins = pe.transpose(bank[7][:, t * EXPERTS:(t + 1) * EXPERTS], logitsT[:, t * P:(t + 1) * P], ident[0:EXPERTS, 0:EXPERTS])
            ins.then_inc(logits_tr, 1)
            pe.wait_ge(chosen, 1)
            b = bank[6]
            E = EXPERTS
            pe.matmul(b[:, 0:E], before[:, :], r_sel[:, 0, :], start=True, stop=True)
            pe.matmul(b[:, E:2 * E], ones[:, :], r_sel[:, 0, :], start=True, stop=False)
            pe.matmul(b[:, E:2 * E], before[:, :], r_sel[:, 1, :], start=False, stop=True)
            pe.matmul(b[:, 2 * E:3 * E], ones[:, :], r_sel[:, 0, :], start=True, stop=False)
            pe.matmul(b[:, 2 * E:3 * E], ones[:, :], r_sel[:, 1, :], start=False, stop=True).then_inc(pos_mm, 1)

            def scatter(j):
                pe.wait_ge(comb_ev, j + (1 + CREDIT))
                for h in range(2):
                    pe.wait_ge(oe_ev, 2 * j + (h + 1 + CREDIT))
                    for t in range(T):
                        pe.matmul(bank[SCATTER[h][t]][:, :], combT[:, t * P:(t + 1) * P], oe[:, h * W:(h + 1) * W],
                                  start=True, stop=True).then_inc(sc_mm, 1)

            def job(j, is_first):
                g0 = T * DG
                pe.wait_ge(pick_put, j + 1)
                pe.wait_ge(h_rest, NG * j + g0)
                pe.wait_ge(comb_ev, j + CREDIT)
                for h in range(2):
                    for i in range(4):
                        for t in range(T):
                            ins = pe.matmul(bank[6 + h][:, i * P:(i + 1) * P], x[:, t, (4 * h + i) * P:(4 * h + i + 1) * P],
                                            pick[:, t, :], start=(t == 0), stop=(t == T - 1))
                    ins.then_inc(gat_mm, 1)
                if not is_first:
                    scatter(j - 1)
                pe.wait_ge(gat_rest, 2 * j + 2)

                def turn(g):
                    pe.wait_ge(hid_ev, NG * j + (g0 + g + 1))
                    pe.wait_ge(h_rest, NG * j + (g0 + g))
                    for i in range(4):
                        ins = tp(bank[6][:, i * P:(i + 1) * P], hid[:, g % 2, i * P:(i + 1) * P])
                    ins.then_inc(h_tr, 1)

                for m, (kind, g, half) in enumerate(JOB):
                    n = FIRST + m
                    w = halves(n, 4, W)
                    if kind == "w2":
                        if half == 0:
                            pe.wait_ge(h_rest, NG * j + (g0 + g + 1))
                    elif half == 0:
                        if (kind, g) == ("w3", 0):
                            pe.wait_ge(y_add, 4 * j + CREDIT)
                        elif g >= 2:
                            pe.wait_ge(hid_ev, NG * j + (g0 + g - 1))
                    pe.wait_ge(rests_made, PER_JOB * j + (n + 1))
                    if kind == "w2":
                        for i in range(4):
                            ins = product(pe, bank[4 + half][:, :], [hT[:, s_, i, slots_of(g)] for s_ in (HEAD, REST)], cols(w, i),
                                          g == 0 and i == 0, g == NG - 1 and i == 3)
                        ins.then_inc(w2_mm, 1)
                    else:
                        full, first_half, b1 = (w1_mm, w1_half, 0) if kind == "w1" else (w3_mm, w3_half, 1)
                        for i in range(4):
                            ins = product(pe, bank[2 * (g % 2) + b1][:, :], [xeT[:, s_, 4 * half + i, :] for s_ in (HEAD, REST)],
                                          cols(w, i), half == 0 and i == 0, half == 1 and i == 3)
                        ins.then_inc(full if half else first_half, 1)
                    if (kind, half) == ("w1", 1) and g:
                        turn(g - 1)
                    if (kind, g, half) == ("w2", 1, 1):
                        pe.wait_ge(comb_put, j + (1 + CREDIT))
                        for t in range(T):
                            ins = tp(bank[7][:, t * P:(t + 1) * P], comb_at[:, t, :])
                        ins.then_inc(comb_tr, 1)
                    if (kind, g, half) == ("w2", NG - 2, 0):
                        turn(NG - 1)

            for ready in (gat_mm, comb_tr, sc_mm):
                pe.sem_inc(ready, CREDIT)
            extra = all_jobs(pe, job)
            scatter(extra + (EXPERTS - 1))

        @block.tensor
        def _(pe):
            def tp(dst, src):
                return pe.transpose(dst, src, ident[:, :])

            def turn_x(k, t):
                if k:
                    pe.wait_ge(ln_done, T * (k - 1) + t + 1)
                for h in range(2):
                    for i in range(4):
                        ins = tp(bank[2 * t + h][:, i * P:(i + 1) * P], x[:, t, (4 * h + i) * P:(4 * h + i + 1) * P])
                    ins.then_inc(x_tr, 1)

            def x_split(k, t):
                pe.wait_ge(x_rest, 4 * k + 2 * (t + 1))

            pe.wait_ge(consts, 1)
            pe.wait_ge(x_in, 16)
            for l in range(DEPTH):
                pe_mixer(pe, l, tp, turn_x, x_split)
                if l == 0:
                    pe_dense(pe, tp, turn_x, x_split)
                else:
                    pe_experts(pe, tp, turn_x, x_split)


_INS = ["x", "positions", "w_in", "mla_q_norm", "w_uq", "mla_kv_norm", "w_ukv", "w_o_mla", "w_o_dsa", "w_out",
        "ln1_g", "ln1_b", "ln2_g", "ln2_b", "dense_w1", "dense_w3", "dense_w2", "moe_router", "moe_w1", "moe_w3", "moe_w2"]


def kernel(**inputs):
    import numpy as np
    import concourse.bacc as bacc
    from concourse.bass_utils import run_bass_kernel_spmd

    nc = bacc.Bacc("TRN2", target_bir_lowering=False, num_devices=1, dynamic_dma_scratch_size=1024)
    arrays, a = {}, {}
    freq = [np.power(np.float32(THETA), -np.arange(0, d, 2, dtype=np.float32) / np.float32(d)) for d in (ROPE, DH)]
    given = {name: np.ascontiguousarray(inputs[name]) for name in _INS}
    given["inv_freq"] = np.concatenate(freq).astype(np.float32)[None, :]
    for name, v in given.items():
        arrays[name + "_dram"] = v
        a[name] = nc.dram_tensor(name + "_dram", v.shape, mybir.dt.from_np(v.dtype), kind="ExternalInput").ap()
    out = nc.dram_tensor("out_dram", (1, SEQ, D), F32, kind="ExternalOutput").ap()
    build(nc, a, out)
    r = run_bass_kernel_spmd(nc, [arrays], core_ids=[0])
    return r.results[0]["out_dram"]
```
